# Optimizing a Trainium2 kernel written in Bass

```python
import math
import jax
import jax.numpy as jnp
from jax import lax
import numpy as np

D_MODEL = 1024
BATCH = 1
SEQ = 128
DEPTH = 1
DEC_BATCH = 1
DEC_SEQ = 256
PAST_LEN = 128

GRID_W = 64
HY_WIDTH = D_MODEL // 4
RG_WIDTH = D_MODEL // 4
HG_WIDTH = D_MODEL // 4
RET_WIDTH = D_MODEL - HY_WIDTH - RG_WIDTH - HG_WIDTH
HY_ORDER = 2
HY_SHORT = 3
HY_EMB = 33
HY_BANDS = (HY_EMB - 1) // 2
HY_FFN = 64
HY_DECAY_TARGET = 1e-2
HY_DECAY_SHORT = 0.3
HY_DECAY_LONG = 1.5
RG_HEADS = 8
RG_HEAD_DIM = RG_WIDTH // RG_HEADS
RG_CONV = 4
RG_C = 8.0
HG_HEADS = 4
HG_DK = HG_WIDTH // HG_HEADS
HG_DV = HG_WIDTH // HG_HEADS
HG_CHUNK = 32
RET_HEADS = 4
RET_DH = RET_WIDTH // RET_HEADS
RET_CHUNK = 64
ROPE_BASE = 10000.0
N_EXPERTS = 16
N_GROUPS = 4
E_PER_GROUP = N_EXPERTS // N_GROUPS
TOP_K = 2
D_EXPERT = 512
N_MOD = 6
EPS = 1e-6
PROJ_SPLITS = ((HY_ORDER + 1) * HY_WIDTH, RG_WIDTH, RG_WIDTH,
               HG_WIDTH, HG_WIDTH, HG_WIDTH, HG_WIDTH, HG_WIDTH,
               RET_WIDTH, RET_WIDTH, RET_WIDTH, RET_WIDTH)
PROJ_WIDTH = sum(PROJ_SPLITS)

kernel_name = "hybrid_flow_backbone_step"

def rmsnorm(x, gain=None):
    xf = x.astype(jnp.float32)
    y = xf * lax.rsqrt(jnp.mean(jnp.square(xf), axis=-1, keepdims=True) + EPS)
    if gain is not None:
        y = y * gain.astype(jnp.float32)
    return y.astype(x.dtype)

def short_conv(u, w, b, pad_left):
    K = w.shape[0]
    L = u.shape[1]
    up = jnp.pad(u, ((0, 0), (pad_left, K - 1 - pad_left), (0, 0)))
    out = b
    for k in range(K):
        out = out + w[k] * up[:, k:k + L]
    return out

def hyena_filters(L, w1, b1, w2, b2, w3):
    f32 = jnp.float32
    t = jnp.arange(L, dtype=f32)
    t_norm = t / max(L - 1, 1)
    bands = jnp.linspace(1e-4, HY_BANDS - 1, HY_BANDS, dtype=f32)
    ang = (2.0 * math.pi / L) * t[:, None] * bands[None, :]
    z = jnp.concatenate([t_norm[:, None], jnp.cos(ang), jnp.sin(ang)], axis=-1)
    h = jnp.sin(z @ w1.astype(f32) + b1.astype(f32))
    h = jnp.sin(h @ w2.astype(f32) + b2.astype(f32))
    h = (h @ w3.astype(f32)).reshape(L, HY_ORDER, 2, HY_WIDTH)
    deltas = jnp.abs(jnp.linspace(math.log(HY_DECAY_TARGET) / HY_DECAY_LONG,
                                  math.log(HY_DECAY_TARGET) / HY_DECAY_SHORT, HY_WIDTH, dtype=f32))
    window = jnp.exp(-t_norm[:, None] * deltas[None, :])
    h = h * window[:, None, None, :]
    h = h * lax.rsqrt(jnp.sum(jnp.square(h), axis=(0, 2), keepdims=True) + EPS)
    h_fwd, h_bwd = h[:, :, 0], h[:, :, 1]
    h_circ = jnp.concatenate([h_fwd, jnp.zeros((1, HY_ORDER, HY_WIDTH), f32), h_bwd[1:][::-1]], axis=0)
    return jnp.fft.rfft(h_circ, axis=0)

def fft_long_conv(z, h_freq):
    L = z.shape[1]
    zf = jnp.fft.rfft(z.astype(jnp.float32), n=2 * L, axis=1)
    y = jnp.fft.irfft(zf * h_freq[None], n=2 * L, axis=1)[:, :L]
    return y.astype(z.dtype)

def hyena_mixer(u, conv_w, conv_b, w1, b1, w2, b2, w3, d_bias):
    L = u.shape[1]
    u = short_conv(u, conv_w, conv_b, (HY_SHORT - 1) // 2)
    v, x1, x2 = jnp.split(u, HY_ORDER + 1, axis=-1)
    hf = hyena_filters(L, w1, b1, w2, b2, w3)
    z = x1 * (fft_long_conv(v, hf[:, 0]) + d_bias[0] * v)
    z = x2 * (fft_long_conv(z, hf[:, 1]) + d_bias[1] * z)
    return z

def linear_scan(a, b, h0):
    def combine(left, right):
        al, bl = left
        ar, br = right
        return al * ar, ar * bl + br
    a_cum, b_cum = lax.associative_scan(combine, (a, b), axis=1)
    return b_cum + a_cum * h0[:, None]

def rglru_mixer(xr, gate, conv_w, conv_b, wa, ba, wx, bx, lam, h0):
    B, L, W = xr.shape
    xc = short_conv(xr, conv_w, conv_b, RG_CONV // 2)
    xh = xc.reshape(B, L, RG_HEADS, RG_HEAD_DIM)
    r = jax.nn.sigmoid(jnp.einsum("blhi,dhij->dblhj", xh, wa).reshape(2, B, L, W) + ba[:, None, None])
    i = jax.nn.sigmoid(jnp.einsum("blhi,dhij->dblhj", xh, wx).reshape(2, B, L, W) + bx[:, None, None])
    log_a = -RG_C * r * jax.nn.softplus(-lam)[:, None, None]
    a = jnp.exp(log_a)
    b = jnp.sqrt(-jnp.expm1(2.0 * log_a)) * (i * xc[None])
    h_f = linear_scan(a[0], b[0], h0[:, 0])
    h_b = jnp.flip(linear_scan(jnp.flip(a[1], 1), jnp.flip(b[1], 1), h0[:, 1]), 1)
    y = (h_f + h_b) * jax.nn.gelu(gate)
    state = jnp.stack([h_f[:, -1], h_b[:, 0]], axis=1)
    return y, state

def chunk_state_scan(decay, U, s0):
    def step(s, xs):
        dec, u = xs
        return (dec * s + u).astype(s.dtype), s
    xs = (jnp.moveaxis(decay.astype(U.dtype), 1, 0), jnp.moveaxis(U, 1, 0))
    s_final, s_prev = lax.scan(step, s0.astype(U.dtype), xs)
    return jnp.moveaxis(s_prev, 0, 1), s_final

def chunk_gla(q, k, v, log_f, s0, chunk, reverse):
    if reverse:
        q, k, v, log_f = (jnp.flip(t, 1) for t in (q, k, v, log_f))
    B, L, H, K = q.shape
    V = v.shape[-1]
    N = L // chunk
    q, k, log_f = (t.reshape(B, N, chunk, H, K) for t in (q, k, log_f))
    v = v.reshape(B, N, chunk, H, V)
    G = jnp.cumsum(log_f, axis=2)
    causal = jnp.tril(jnp.ones((chunk, chunk), dtype=bool))[None, None, :, :, None, None]
    diff = G[:, :, :, None] - G[:, :, None, :]
    decay = jnp.exp(jnp.where(causal, diff, -jnp.inf))
    scores = jnp.einsum("bnthk,bntshk,bnshk->bnhts", q, decay, k)
    o_intra = jnp.einsum("bnhts,bnshv->bnthv", scores, v)
    G_last = G[:, :, -1]
    U = jnp.einsum("bnchk,bnchv->bnhkv", k * jnp.exp(G_last[:, :, None] - G), v)
    s_prev, s_final = chunk_state_scan(jnp.exp(G_last)[..., None], U, s0)
    o_inter = jnp.einsum("bnthk,bnhkv->bnthv", q * jnp.exp(G), s_prev)
    o = (o_intra + o_inter).reshape(B, L, H, V)
    if reverse:
        o = jnp.flip(o, 1)
    return o, s_final

def chunk_retention(q, k, v, log_gamma, s0, chunk, reverse):
    if reverse:
        q, k, v = (jnp.flip(t, 1) for t in (q, k, v))
    B, L, H, K = q.shape
    V = v.shape[-1]
    N = L // chunk
    q, k = (t.reshape(B, N, chunk, H, K) for t in (q, k))
    v = v.reshape(B, N, chunk, H, V)
    pos = jnp.arange(chunk)
    rel = pos[:, None] - pos[None, :]
    lg = log_gamma
    dmat = jnp.exp(jnp.where(rel[None] >= 0, rel[None].astype(lg.dtype) * lg[:, None, None], -jnp.inf))
    scores = jnp.einsum("bnthk,bnshk->bnhts", q, k) * dmat
    o_intra = jnp.einsum("bnhts,bnshv->bnthv", scores, v)
    inner = jnp.exp((pos + 1).astype(lg.dtype)[:, None] * lg[None])
    tail = jnp.exp((chunk - 1 - pos).astype(lg.dtype)[:, None] * lg[None])
    U = jnp.einsum("bnchk,ch,bnchv->bnhkv", k, tail, v)
    dec = jnp.broadcast_to(jnp.exp(chunk * lg)[:, None, None], (B, N, H, 1, 1))
    s_prev, s_final = chunk_state_scan(dec, U, s0)
    o_inter = jnp.einsum("bnthk,th,bnhkv->bnthv", q, inner, s_prev)
    o = (o_intra + o_inter).reshape(B, L, H, V)
    if reverse:
        o = jnp.flip(o, 1)
    return o, s_final

def hgrn2_mixer(q, f_fwd, f_bwd, inp, g, lb, norm_gain, s0):
    B, L, _ = q.shape
    qh = jax.nn.silu(q).reshape(B, L, HG_HEADS, HG_DK)
    vh = inp.reshape(B, L, HG_HEADS, HG_DV)
    outs, states = [], []
    for d, f_pre in enumerate((f_fwd, f_bwd)):
        lbd = lb[d]
        log_f = jnp.logaddexp(jnp.log(lbd), jnp.log1p(-lbd) + jax.nn.log_sigmoid(f_pre))
        k = (1 - lbd) * jax.nn.sigmoid(-f_pre)
        o, s = chunk_gla(qh, k.reshape(B, L, HG_HEADS, HG_DK), vh,
                         log_f.reshape(B, L, HG_HEADS, HG_DK), s0[:, d], HG_CHUNK, d == 1)
        outs.append(o)
        states.append(s)
    o = rmsnorm(outs[0] + outs[1], norm_gain.reshape(HG_HEADS, HG_DV)).reshape(B, L, HG_WIDTH)
    return o * jax.nn.silu(g), jnp.stack(states, axis=1)

def grid_rope(L, dtype):
    rows = L // GRID_W
    row = jnp.repeat(jnp.arange(rows), GRID_W).astype(jnp.float32)
    col = (jnp.arange(L) % GRID_W).astype(jnp.float32)
    n_freq = RET_DH // 4
    inv_freq = ROPE_BASE ** (-jnp.arange(n_freq, dtype=jnp.float32) / n_freq)
    ang = jnp.concatenate([row[:, None] * inv_freq, col[:, None] * inv_freq], axis=-1)
    return jnp.cos(ang).astype(dtype), jnp.sin(ang).astype(dtype)

def apply_rope(x, cos, sin):
    x1, x2 = x[..., 0::2], x[..., 1::2]
    c, s = cos[None, :, None], sin[None, :, None]
    return jnp.stack([x1 * c - x2 * s, x1 * s + x2 * c], axis=-1).reshape(x.shape)

def retention_mixer(q, k, v, g, decay_logit, s0, rope):
    B, L, _ = q.shape
    qh = q.reshape(B, L, RET_HEADS, RET_DH)
    kh = k.reshape(B, L, RET_HEADS, RET_DH) * (RET_DH ** -0.5)
    vh = v.reshape(B, L, RET_HEADS, RET_DH)
    if rope is not None:
        qh = apply_rope(qh, rope[0], rope[1])
        kh = apply_rope(kh, rope[0], rope[1])
    log_gamma = jax.nn.log_sigmoid(decay_logit)
    outs, states = [], []
    for d in range(2):
        o, s = chunk_retention(qh, kh, vh, log_gamma[d], s0[:, d], RET_CHUNK, d == 1)
        outs.append(o)
        states.append(s)
    o = rmsnorm(outs[0] + outs[1]).reshape(B, L, RET_WIDTH)
    return jax.nn.silu(g) * o, jnp.stack(states, axis=1)

def moe_ffn(x, w_router, router_bias, w_gate, w_up, w_down):
    B, L, D = x.shape
    t = x.reshape(-1, D)
    probs = jax.nn.softmax(jnp.dot(t, w_router).astype(jnp.float32), axis=-1)
    sel = probs + router_bias.astype(jnp.float32)
    grp_score = lax.top_k(sel.reshape(-1, N_GROUPS, E_PER_GROUP), TOP_K)[0].sum(-1)
    best = jnp.argmax(grp_score, axis=-1)
    in_group = (jnp.arange(N_EXPERTS) // E_PER_GROUP)[None] == best[:, None]
    _, idx = lax.top_k(jnp.where(in_group, sel, -jnp.inf), TOP_K)
    w = jnp.take_along_axis(probs, idx, axis=-1)
    w = w / jnp.sum(w, axis=-1, keepdims=True)
    gates = jnp.sum(jax.nn.one_hot(idx, N_EXPERTS, dtype=jnp.float32) * w[..., None], axis=1)
    h = jax.nn.silu(jnp.einsum("td,edf->tef", t, w_gate)) * jnp.einsum("td,edf->tef", t, w_up)
    h = h * gates.astype(h.dtype)[..., None]
    return jnp.einsum("tef,efd->td", h, w_down).reshape(B, L, D)

def trunk_layer(P, l, x, cond, rg_h0, hg_s0, ret_s0, lb, rope):
    mod = jnp.dot(jax.nn.silu(cond), P["w_ada"][l]) + P["b_ada"][l]
    sh1, sc1, g1, sh2, sc2, g2 = jnp.split(mod[:, None, :], N_MOD, axis=-1)
    h = rmsnorm(x, P["norm1"][l]) * (1 + sc1) + sh1
    proj = jnp.einsum("bld,dp->blp", h, P["w_in"][l])
    points = [int(s) for s in np.cumsum(PROJ_SPLITS)[:-1]]
    (hy_u, rg_x, rg_g, hg_q, hg_ff, hg_fb, hg_i, hg_g,
     ret_q, ret_k, ret_v, ret_g) = jnp.split(proj, points, axis=-1)
    y_hy = hyena_mixer(hy_u, P["hy_conv_w"][l], P["hy_conv_b"][l], P["hy_w1"][l], P["hy_b1"][l],
                       P["hy_w2"][l], P["hy_b2"][l], P["hy_w3"][l], P["hy_d"][l])
    y_rg, st_rg = rglru_mixer(rg_x, rg_g, P["rg_conv_w"][l], P["rg_conv_b"][l], P["rg_wa"][l],
                              P["rg_ba"][l], P["rg_wx"][l], P["rg_bx"][l], P["rg_lambda"][l], rg_h0)
    y_hg, st_hg = hgrn2_mixer(hg_q, hg_ff, hg_fb, hg_i, hg_g, lb, P["hg_norm"][l], hg_s0)
    y_ret, st_ret = retention_mixer(ret_q, ret_k, ret_v, ret_g, P["ret_decay"][l], ret_s0, rope)
    mixed = jnp.concatenate([y_hy, y_rg, y_hg, y_ret], axis=-1)
    x = x + g1 * jnp.einsum("blm,md->bld", mixed, P["w_out"][l])
    h = rmsnorm(x, P["norm2"][l]) * (1 + sc2) + sh2
    x = x + g2 * moe_ffn(h, P["w_router"], P["router_bias"], P["w_gate"][l], P["w_up"][l], P["w_down"][l])
    return x, st_rg, st_hg, st_ret

def setup_inputs(seed: int = 0) -> dict:
    key = jax.random.key(seed)
    ks = iter(jax.random.split(key, 48))
    f32 = jnp.float32

    def nrm(shape, scale):
        return scale * jax.random.normal(next(ks), shape, f32)

    u = jax.random.uniform(next(ks), (DEPTH, 2, RG_WIDTH), f32, minval=0.9, maxval=0.999)
    a0 = u ** (1.0 / RG_C)
    rg_lambda = jnp.log(a0) - jnp.log1p(-a0)
    gam = 1.0 - 2.0 ** (-5.0 - jnp.arange(RET_HEADS, dtype=f32))
    ret_decay = (jnp.log(gam) - jnp.log1p(-gam))[None, None] + nrm((DEPTH, 2, RET_HEADS), 0.1)
    return {
        "x_prompt": nrm((BATCH, SEQ, D_MODEL), 1.0),
        "x_sample": nrm((DEC_BATCH, DEC_SEQ, D_MODEL), 1.0),
        "state_rglru": nrm((DEC_BATCH, DEPTH, 2, RG_WIDTH), 0.5),
        "state_hgrn": nrm((DEC_BATCH, DEPTH, 2, HG_HEADS, HG_DK, HG_DV), 0.5),
        "state_ret": nrm((DEC_BATCH, DEPTH, 2, RET_HEADS, RET_DH, RET_DH), 0.5),
        "c": nrm((DEC_BATCH, D_MODEL), 1.0),
        "c_ctx": nrm((D_MODEL,), 1.0),
        "norm1": 1.0 + nrm((DEPTH, D_MODEL), 0.02),
        "norm2": 1.0 + nrm((DEPTH, D_MODEL), 0.02),
        "norm_final": 1.0 + nrm((D_MODEL,), 0.02),
        "w_ada": nrm((DEPTH, D_MODEL, N_MOD * D_MODEL), 0.5 * D_MODEL ** -0.5),
        "b_ada": nrm((DEPTH, N_MOD * D_MODEL), 0.02),
        "w_in": nrm((DEPTH, D_MODEL, PROJ_WIDTH), D_MODEL ** -0.5),
        "w_out": nrm((DEPTH, D_MODEL, D_MODEL), D_MODEL ** -0.5),
        "hy_conv_w": nrm((DEPTH, HY_SHORT, (HY_ORDER + 1) * HY_WIDTH), HY_SHORT ** -0.5),
        "hy_conv_b": nrm((DEPTH, (HY_ORDER + 1) * HY_WIDTH), 0.02),
        "hy_w1": nrm((DEPTH, HY_EMB, HY_FFN), 1.0),
        "hy_b1": nrm((DEPTH, HY_FFN), 0.1),
        "hy_w2": nrm((DEPTH, HY_FFN, HY_FFN), HY_FFN ** -0.5),
        "hy_b2": nrm((DEPTH, HY_FFN), 0.1),
        "hy_w3": nrm((DEPTH, HY_FFN, HY_ORDER * 2 * HY_WIDTH), HY_FFN ** -0.5),
        "hy_d": nrm((DEPTH, HY_ORDER, HY_WIDTH), 0.5),
        "rg_conv_w": nrm((DEPTH, RG_CONV, RG_WIDTH), RG_CONV ** -0.5),
        "rg_conv_b": nrm((DEPTH, RG_WIDTH), 0.02),
        "rg_wa": nrm((DEPTH, 2, RG_HEADS, RG_HEAD_DIM, RG_HEAD_DIM), RG_HEAD_DIM ** -0.5),
        "rg_ba": nrm((DEPTH, 2, RG_WIDTH), 0.1),
        "rg_wx": nrm((DEPTH, 2, RG_HEADS, RG_HEAD_DIM, RG_HEAD_DIM), RG_HEAD_DIM ** -0.5),
        "rg_bx": nrm((DEPTH, 2, RG_WIDTH), 0.1),
        "rg_lambda": rg_lambda,
        "hg_lb": nrm((DEPTH, 2, HG_WIDTH), 1.0),
        "hg_norm": 1.0 + nrm((DEPTH, HG_WIDTH), 0.02),
        "ret_decay": ret_decay,
        "w_router": nrm((D_MODEL, N_EXPERTS), D_MODEL ** -0.5),
        "router_bias": nrm((N_EXPERTS,), 0.01),
        "w_gate": nrm((DEPTH, N_EXPERTS, D_MODEL, D_EXPERT), D_MODEL ** -0.5),
        "w_up": nrm((DEPTH, N_EXPERTS, D_MODEL, D_EXPERT), D_MODEL ** -0.5),
        "w_down": nrm((DEPTH, N_EXPERTS, D_EXPERT, D_MODEL), D_EXPERT ** -0.5),
    }

def reference(x_prompt, x_sample, state_rglru, state_hgrn, state_ret, c, c_ctx,
              norm1, norm2, norm_final, w_ada, b_ada, w_in, w_out,
              hy_conv_w, hy_conv_b, hy_w1, hy_b1, hy_w2, hy_b2, hy_w3, hy_d,
              rg_conv_w, rg_conv_b, rg_wa, rg_ba, rg_wx, rg_bx, rg_lambda,
              hg_lb, hg_norm, ret_decay, w_router, router_bias, w_gate, w_up, w_down):
    P = {"norm1": norm1, "norm2": norm2, "w_ada": w_ada, "b_ada": b_ada, "w_in": w_in, "w_out": w_out,
         "hy_conv_w": hy_conv_w, "hy_conv_b": hy_conv_b, "hy_w1": hy_w1, "hy_b1": hy_b1,
         "hy_w2": hy_w2, "hy_b2": hy_b2, "hy_w3": hy_w3, "hy_d": hy_d,
         "rg_conv_w": rg_conv_w, "rg_conv_b": rg_conv_b, "rg_wa": rg_wa, "rg_ba": rg_ba,
         "rg_wx": rg_wx, "rg_bx": rg_bx, "rg_lambda": rg_lambda, "hg_norm": hg_norm,
         "ret_decay": ret_decay, "w_router": w_router, "router_bias": router_bias,
         "w_gate": w_gate, "w_up": w_up, "w_down": w_down}
    lb_cum = jnp.cumsum(jax.nn.softmax(hg_lb.astype(jnp.float32), axis=0), axis=0)
    lb_all = (lb_cum - lb_cum[0:1]).astype(hg_lb.dtype)

    B = x_prompt.shape[0]
    dt = x_prompt.dtype
    z_rg = jnp.zeros((B, 2, RG_WIDTH), dt)
    z_hg = jnp.zeros((B, 2, HG_HEADS, HG_DK, HG_DV), dt)
    z_ret = jnp.zeros((B, 2, RET_HEADS, RET_DH, RET_DH), dt)
    xc = x_prompt
    st_rg, st_hg, st_ret = [], [], []
    for l in range(DEPTH):
        xc, s1, s2, s3 = trunk_layer(P, l, xc, c_ctx[None], z_rg, z_hg, z_ret, lb_all[l], None)
        st_rg.append(s1)
        st_hg.append(s2)
        st_ret.append(s3)
    y_prompt = rmsnorm(xc, norm_final)
    new_state_rglru = jnp.stack(st_rg, axis=1)
    new_state_hgrn = jnp.stack(st_hg, axis=1)
    new_state_ret = jnp.stack(st_ret, axis=1)

    rope = grid_rope(x_sample.shape[1], x_sample.dtype)
    xs = x_sample
    for l in range(DEPTH):
        xs, _, _, _ = trunk_layer(P, l, xs, c, state_rglru[:, l], state_hgrn[:, l], state_ret[:, l],
                                  lb_all[l], rope)
    y_sample = rmsnorm(xs, norm_final)
    return (y_prompt, y_sample, new_state_rglru, new_state_hgrn, new_state_ret)


_drawn_inputs = setup_inputs


def setup_inputs(seed=0):
    import zlib

    import numpy as np

    out = dict(_drawn_inputs(seed))
    spreads = {}
    factors = {'state_hgrn': 8.0,
     'norm2': 2.958,
     'norm_final': 2.822,
     'hy_conv_b': 2.912,
     'rg_ba': 4.135,
     'hg_norm': 4.584}
    for name, (base, spread) in spreads.items():
        noise = np.random.default_rng([zlib.crc32(name.encode()), seed]).standard_normal(out[name].shape)
        drawn = base * np.exp(spread * noise) if base else spread * noise
        out[name] = jnp.asarray(drawn.astype(out[name].dtype))
    for name, factor in factors.items():
        out[name] = (out[name] * factor).astype(out[name].dtype)
    return out
```

```python
import math
from contextlib import ExitStack

import numpy as np

import concourse.bass as bass
from concourse import mybir

ALU = mybir.AluOpType
ACT = mybir.ActivationFunctionType
AX = mybir.AxisListType
F32 = mybir.dt.float32
I32 = mybir.dt.int32
U8 = mybir.dt.uint8
F16 = mybir.dt.float16

P = 128
D = 1024
KT = D // P
CTX, LAT = 128, 256
TOK = CTX + LAT
NT = TOK // P
NMOD = 6
CW = 512
ADA_CHUNKS = NMOD * D // CW
E, FE, NG = 16, 512, 4
ROWS = P
OVER = 2 * TOK // P - 1
EPS = 1e-6
GRID_W, DH = 64, 64
HY_EMB, HY_FFN = 33, 64
HYC = 256
SEG_C, SEG_L = 2, 133
PADW = 390
RUN = PADW - 3
LATO = SEG_L - SEG_C
MAGIC = 12582912.0
LEVELS = (64, 32, 16, 8, 4, 2, 1)
NLEV = len(LEVELS) + 1

VROWS = {}
_n = 0
for _name, _rows in (("c", 16), ("norm1", 8), ("norm2", 8), ("hcw", 18), ("hcb", 6), ("rcw", 8), ("rcb", 2),
                     ("rba", 4), ("rbx", 4), ("lam", 4), ("hyd", 4), ("rst", 4)):
    VROWS[_name] = _n
    _n += _rows
NV = _n


def shape_constants():
    cols, parts = {}, []
    at = 0

    def put(name, a):
        nonlocal at
        full = np.zeros((P, a.shape[1]), np.float64)
        full[:a.shape[0]] = a
        cols[name] = (at, a.shape[1])
        parts.append(full)
        at += a.shape[1]

    p = np.arange(P)
    put("ident", np.eye(P))
    put("sel12", np.repeat(np.eye(ADA_CHUNKS), 2, axis=1))
    pick = np.zeros((P, 2))
    pick[0::32, 0] = pick[1::32, 1] = 1.0
    put("pick", pick)
    swap = np.zeros((P, P))
    for i in range(0, P, 2):
        swap[i + 1, i] = -1.0
        swap[i, i + 1] = 1.0
    put("swap", swap)
    put("triu", (p[:, None] < p[None]).astype(float))
    put("ones", np.ones((P, P)))

    def dft(L):
        t, f = np.arange(L)[:, None], np.arange(L)[None]
        re = np.cos(np.pi * f * t / L)
        im = -np.sin(np.pi * f * t / L)
        im[:, 0] = np.cos(np.pi * t[:, 0])
        w = np.full((1, L), 1.0 / L)
        w[0, 0] = 0.5 / L
        return re, im, (re * w).T, (im * w).T
    re, im, ire, iim = dft(CTX)
    put("dft_ctx", np.concatenate([re, im], 1))
    put("idft_ctx", np.concatenate([ire, iim], 1))
    re, im, ire, iim = dft(LAT)
    put("dft_lat", np.concatenate([np.concatenate([re[tt * P:tt * P + P, u * P:u * P + P],
                                                   im[tt * P:tt * P + P, u * P:u * P + P]], 1)
                                   for tt in range(2) for u in range(2)], 1))
    put("idft_lat", np.concatenate([np.concatenate([ire[u * P:u * P + P], iim[u * P:u * P + P]], 1)
                                    for u in range(2)], 1))
    put("alt", np.cos(np.pi * p)[:, None])
    t = np.arange(LAT)
    nf = DH // 4
    inv = 10000.0 ** (-np.arange(nf) / nf)
    ang = np.concatenate([(t // GRID_W)[:, None] * inv, (t % GRID_W)[:, None] * inv], 1)
    half = (p % DH) // 2
    put("cos", np.cos(ang[:, half]).T)
    put("sin", np.sin(ang[:, half]).T)
    s, q = p[:, None], p[None]
    put("dist_f", np.maximum(q - s, 0))
    put("dist_b", np.maximum(s - q, 0))
    put("dist_up", P + q - s)
    put("dist_lo", P + s - q)
    put("mask_f", (q >= s).astype(float))
    put("mask_b", (s >= q).astype(float))
    put("count", np.tile(np.arange(257)[None], (P, 1)))
    put("tokid", np.stack([p + P * j for j in range(NT)], 1))
    put("w4", np.tile(np.array([[4, 3, 2, 1.0]]), (P, 1)))
    put("w16", np.tile(np.arange(16, 0, -1)[None], (P, 1)))
    put("erow", np.tile((np.arange(16) * ROWS)[None], (P, 1)))
    put("selc", np.repeat(pick, P, axis=1))
    reset = np.ones((P, TOK))
    reset[:, ::P] = 0.0
    put("reset", reset)
    big = np.concatenate(parts, 1).astype(np.float32)

    zs, wins = [], []
    deltas = np.abs(np.linspace(np.log(1e-2) / 1.5, np.log(1e-2) / 0.3, HYC))
    for L in (CTX, LAT):
        tl = np.arange(L, dtype=np.float64)
        tn = tl / (L - 1)
        a = (2 * np.pi / L) * tl[:, None] * np.linspace(1e-4, (HY_EMB - 1) // 2 - 1, (HY_EMB - 1) // 2)[None]
        zs.append(np.concatenate([tn[:, None], np.cos(a), np.sin(a)], 1))
        wins.append(np.exp(-tn[:, None] * deltas[None]))
    z = np.concatenate(zs, 0).T
    win = np.concatenate(wins, 0).reshape(NT, P, HYC).transpose(1, 0, 2).reshape(P, NT * HYC)
    masks = np.zeros((P, NLEV, 2, P), np.float32)
    for n, h in enumerate(LEVELS):
        same = (s // (2 * h)) == (q // (2 * h))
        masks[:, n, 0] = same & (s % (2 * h) < h) & (q % (2 * h) >= h)
        masks[:, n, 1] = same & (s % (2 * h) >= h) & (q % (2 * h) < h)
    masks[:, NLEV - 1, :] = np.eye(P)[:, None]
    return big, cols, z.astype(np.float32), win.astype(np.float32), masks.reshape(P, -1)


def backbone_step(nc, cols, A, O):
    PRE = ([("ada", n) for n in range(4)] + [("in", n) for n in (2, 3, 4, 0, 1)] +
           [("ada", n) for n in range(4, 10)] + [("in", 5), ("in", 6), ("out", 0), ("out", 1)] +
           [("ada", 10), ("ada", 11)])
    NS = 3
    assert len(PRE) % NS == 0
    PRE_USES = len(PRE) // NS
    order = {key: i for i, key in enumerate(PRE)}

    ctx = ExitStack()
    with ctx:
        def sem(name):
            return ctx.enter_context(nc.semaphore(name))

        def alloc(stack, name, shape, dt=F32):
            return stack.enter_context(nc.sbuf_tensor(name, shape, dt))

        def sb(name, shape, dt=F32):
            return alloc(ctx, name, shape, dt)

        slot = [sb(f"slot{i}", [P, KT, CW]) for i in range(NS)]
        hT = sb("hT", [P, KT, TOK])
        XS = sb("XS", [P, 8 * PADW])
        NCONST = sum(w for _, w in cols.values())
        FIRST = cols["pick"][0] + cols["pick"][1]
        const = sb("const", [P, NCONST])
        mask = sb("mask", [P, NLEV, 2, P], U8)
        G1 = sb("G1", [P, 2, D])
        VR = sb("VR", [P, P])
        VC = sb("VC", [P, NV])
        SC16 = sb("SC16", [P, 16])
        sptmp = sb("sptmp", [P, 6, 16])
        modrow = sb("modrow", [P, 2, CW])
        bada = sb("bada", [ADA_CHUNKS, CW])
        MC = sb("MC", [P, 4, KT, 2])
        AB = sb("AB", [P, 2, KT, 2])
        siluc = sb("siluc", [P, KT, 32])
        sige = sb("sige", [P, 16])
        stat = sb("stat", [P, 4, 16])
        mhalf = sb("mhalf", [P, 16])
        wr = sb("wr", [P, KT, E])
        rbias = sb("rbias", [P, E])
        hgn = sb("hgn", [P, HYC])
        halfb = sb("halfb", [P, 8])
        tokid16 = sb("tokid16", [P, NT], F16)
        lamc = sb("lamc", [P, 4])

        def C(name):
            a, w = cols[name]
            return const[:, a:a + w]
        ident = C("ident")

        def col(name, i=0):
            r = VROWS[name] + i
            return VC[:, r:r + 1]

        x_in = XS[:, 0:NT * D].rearrange("p (j d) -> p j d", j=NT)
        CU = XS[:, :].rearrange("p (i w) -> p i w", i=8)
        BD = XS[:, 0:1024].rearrange("p (d k t n) -> p d k t n", d=2, k=2, t=2)
        SC = XS[:, 0:3072].rearrange("p (d r b t q) -> p d r b t q", d=2, r=2, b=NT, t=2)

        mix = ExitStack()

        def mb(name, shape, dt=F32):
            return alloc(mix, name, shape, dt)
        U = mb("U", [P, 6, PADW])
        XC = mb("XC", [P, 2, PADW])
        RGG = mb("RGG", [P, 2, TOK])
        HQ = mb("HQ", [P, 2 * TOK])
        HX = mb("HX", [P, 2, 2 * TOK])
        HK = mb("HK", [P, 2, 2 * TOK])
        HTOT = mb("HTOT", [P, 2, 6])
        TMH = mb("TMH", [P, NT, 2 * HYC])
        HF = mb("HF", [P, 3, 2, 2, HYC])
        HNY = mb("HNY", [1, 2, 2, HYC])
        HGS = mb("HGS", [P, 2, 2, 2, P])
        STO = mb("STO", [P, 4, 2, 64])
        RGO = mb("RGO", [P, 4])
        PR = HX[:, :, :].rearrange("p d (t n) -> p (d t) n", t=2)
        TMR = HK[:, :, :].rearrange("p d n -> p (d n)").rearrange("p (j n) -> p j n", j=NT)
        T = mb("T", [P, 7040])

        def t_at(a, n):
            return T[:, a:a + n]
        w1 = U[:, 0, 0:64]
        w2 = U[:, 0, 64:128]
        b12 = U[:, 0, 128:130]
        z_t = U[:, 1, 0:TOK]
        fu = [U[:, 2 + i, 0:TOK] for i in range(3)]
        w3 = TMH[:, :, :].rearrange("p j n -> p (j n)")[:, 0:1024]
        win = HQ[:, :].rearrange("p (j n) -> p j n", j=NT)
        FSQ = [v[:, :, :].rearrange("p d n -> p (d n)").rearrange("p (j n) -> p j n", j=NT) for v in (HX, HK)]
        FH = t_at(0, 3072).rearrange("p (j o d c) -> p j o d c", j=NT, o=2, d=2)
        FS = t_at(3072, 1536).rearrange("p (j n) -> p j n", j=NT)
        FD = t_at(4608, 1536).rearrange("p (j n) -> p j n", j=NT)
        FRS = G1[:, 0, :].rearrange("p (g n) -> p g n", g=2)
        LF = t_at(0, 1536).rearrange("p (d n) -> p d n", d=2)
        W = t_at(1536, 1536).rearrange("p (d n) -> p d n", d=2)
        QL = t_at(3072, 1536).rearrange("p (d n) -> p d n", d=2)
        KL = t_at(4608, 1536).rearrange("p (d n) -> p d n", d=2)
        KTOK = t_at(1536, 1024).rearrange("p (d i t n) -> p d i t n", d=2, i=2, t=2)
        HO = t_at(0, 768).rearrange("p (j n) -> p j n", j=NT)
        HO2 = t_at(768, 768).rearrange("p (j n) -> p j n", j=NT)
        HGATE = t_at(4608, 768).rearrange("p (j n) -> p j n", j=NT)
        RI = t_at(0, 8 * RUN).rearrange("p (d k t n) -> p d k t n", d=2, k=2, t=2)
        RA = t_at(8 * RUN, 4 * RUN).rearrange("p (d t n) -> p d t n", d=2, t=2)
        RB = t_at(12 * RUN, 4 * RUN).rearrange("p (d t n) -> p d t n", d=2, t=2)
        VT = t_at(6192, 768).rearrange("p (j c) -> p j c", j=NT)
        Y = t_at(0, 1536).rearrange("p (u r c) -> p u r c", u=3, r=2)
        M1 = t_at(1536, 1024).rearrange("p (i n) -> p i n", i=2)
        M2 = t_at(2560, 1024).rearrange("p (i n) -> p i n", i=2)
        ZT = t_at(3584, 768).rearrange("p (t n) -> p t n", t=2)
        DEC = t_at(0, 2048).rearrange("p (h k q) -> p h k q", h=4, k=4)
        WL = t_at(2048, 2048).rearrange("p (h n) -> p h n", h=4)
        WC = t_at(4096, 512).rearrange("p (r h n) -> p r h n", r=2, h=2)
        TAIL = t_at(4608, 512).rearrange("p (d t n) -> p d t n", d=2, t=2)
        RKT = t_at(5120, 512).rearrange("p (d t n) -> p d t n", d=2, t=2)
        RS = t_at(5632, 512).rearrange("p (d t n) -> p d t n", d=2, t=2)
        DTMP = t_at(6144, 512).rearrange("p (h q) -> p h q", h=4)
        hf = HF[:, :, :, :, :].rearrange("p u r o c -> p (u r o c)")
        mask_in = hf[:, 0:NLEV * 2 * P]
        EI = hf[:, 0:1024].rearrange("p (d t n) -> p d t n", d=2, t=2)
        QD = hf[:, 1024:2048].rearrange("p (d t n) -> p d t n", d=2, t=2)
        PX = hf[:, 2048:3072].rearrange("p (i n) -> p i n", i=4)
        uf = U[:, :, :].rearrange("p i n -> p (i n)")
        RO = uf[:, 0:768].rearrange("p (j n) -> p j n", j=NT)
        RO2 = uf[:, 768:1536].rearrange("p (j n) -> p j n", j=NT)
        RGATE = uf[:, 1536:2304].rearrange("p (j n) -> p j n", j=NT)
        mix.close()

        moe = ExitStack()

        def eb(name, shape, dt=F32):
            return alloc(moe, name, shape, dt)
        slot += [eb(f"slot{i}", [P, KT, CW]) for i in range(NS, 2 * NS)]
        xe = [eb(f"xe{i}", [P, D]) for i in range(2)]
        xeTa = eb("xeTa", [P, 2, KT, P])
        xeT = [xeTa[:, i] for i in range(2)]
        he = eb("he", [P, 2, FE])
        heT = eb("heT", [P, FE // P, P])
        ye = [eb(f"ye{i}", [P, D]) for i in range(2)]
        G2 = eb("G2", [P, 2, D])
        gw = eb("gw", [P, NT, 2])
        lst = eb("lst", [P, NT * E], I32)
        rows = eb("rows", [P, NT, 2], I32)
        further_passes = eb("further_passes", [1, 1 + OVER], I32)
        OV = eb("OV", [P, 8, E])
        lsto = eb("lsto", [P, OVER], I32)
        RT = eb("RT", [P, 12, NT, E])
        GR = eb("GR", [P, 3, NT * NG])
        PS = eb("PS", [P, NT * NG, 6])
        SEL = eb("SEL", [P, E, P], F16)
        h2tok = [xe[0], xe[1], ye[0]]
        YG = [slot[3 + k][:, :, :].rearrange("p k n -> p (k n)")[:, 0:NT * D].rearrange("p (j n) -> p j n", j=NT)
              for k in range(2)]
        SO = xeTa[:, 0].rearrange("p k n -> p (k n)")[:, 0:2 * NT * P].rearrange("p (i n) -> p i n", i=2 * NT)
        NF = he[:, :, :].rearrange("p a n -> p (a n)")
        moe.close()
        XR = x_in

        psum = ctx.enter_context(nc.psum_tensor("psum", [P, 8, 512], F32))
        filled = [sem(f"filled{b}") for b in range(8)]
        emptied = [sem(f"emptied{b}") for b in range(8)]
        loaded = [sem(f"loaded{i}") for i in range(2 * NS)]
        s = {name: sem(name) for name in (
            "y_zero", "route2", "o_xe", "o_out", "o_lst", "o_sel", "o_selm", "o_step", "o_xt", "o_xtr", "o_w", "o_up", "o_h", "o_ht",
            "o_htr", "o_down", "o_exp", "o_y", "o_h1", "o_h2", "o_h3",
            "act_step", "bd_ready", "first_in", "const_in", "mask_in", "mask_ready", "dec", "down_done", "dve_step", "ei", "filt_in", "fin_in",
            "fin_out", "fin_ready", "fin_rstd", "fin_sq", "fin_var", "frs_sqrt", "fs_ready", "fsq_ready",
            "fu_arg", "fu_sin", "g_exp", "gate_done", "gelu_arg", "gelu_t", "h1", "h2", "h2_out", "h3",
            "h_ready", "hg_abs", "hg_exp", "hg_qk", "hg_texp", "hg_tx", "ho_gexp", "ho_ready", "ho_rstd",
            "ho_var", "hq_exp", "ht_filled", "ht_ready", "hy_done", "late_in", "lev_arg", "lev_exp",
            "lev_ready", "logits_exp", "mod1", "n2_ready", "n2_rstd", "n2_sq", "n2_var", "nf_in", "pads",
            "pool_step", "qd", "res_in", "rg_a", "rg_b", "rg_b2", "rg_r", "rgo", "ro_gexp", "ro_ready",
            "ro_rstd", "ro_var", "rope", "route", "rs_ready", "rtail", "sc_zero", "sel", "sel_used", "siluc",
            "siluc_exp", "sp_abs", "sp_in", "sp_ready", "state_out", "states0", "u_ready", "up_done",
            "vec_in", "x1", "x2", "x_in", "x_rstd", "x_sq", "x_var", "xc_ready", "xe0", "xe1", "xn_ready",
            "xt_filled", "xt_ready", "y_out0", "y_out1", "ya", "yb", "z1")}
        block = ctx.enter_context(nc.Block())

        uses = {}

        def claim(eng, key):
            n = len(uses)
            uses[key] = n
            if n >= 8:
                eng.wait_ge(emptied[n % 8], n // 8)
            return psum[:, n % 8, :]

        def fill(ins, key):
            ins.then_inc(filled[uses[key] % 8], 1)

        def take(eng, key):
            n = uses[key]
            eng.wait_ge(filled[n % 8], n // 8 + 1)
            return psum[:, n % 8, :]

        def give(ins, key):
            ins.then_inc(emptied[uses[key] % 8], 1)

        def taken(eng, key):
            n = uses[key]
            eng.wait_ge(emptied[n % 8], n // 8 + 1)

        def chunk(eng, key):
            i = order[key]
            eng.wait_ge(loaded[i % NS], 16 * (i // NS + 1))
            return slot[i % NS]

        def further(eng):
            eng.wait_ge(s["route2"], 1)
            return eng.value_load(further_passes[0:1, 0:1], min_val=0, max_val=OVER)

        def tile(j):
            return slice(j * P, j * P + P)

        def seg(v, j0):
            return v[..., 0:CTX] if j0 == 0 else v[..., CTX:TOK]

        @block.tensor
        def _(pe):
            mm = nc.tensor.matmul
            tr = nc.tensor.transpose
            pe.wait_ge(s["first_in"], 16)
            pe.wait_ge(s["vec_in"], 16 * N_VEC)
            o = claim(pe, "vcols")
            fill(tr(o[:, 0:NV], VR[0:NV, :], ident[0:NV, 0:NV]), "vcols")

            def ada(n):
                w = chunk(pe, ("ada", n))
                if n == 0:
                    pe.wait_ge(s["siluc"], 1)
                o = claim(pe, ("ada", n))
                for kt in range(KT):
                    g = kt % 4
                    last = mm(o[32 * g:32 * g + 32, :], siluc[:, kt, :], w[:, kt, :], start=(kt < 4), stop=(kt >= 4),
                              tile_position=(0, 32 * g))
                fill(last, ("ada", n))

            ada_seen = []

            def ada_post(n):
                ada_seen.append(n)
                taken(pe, ("ada", n))
                if n // 2 in (2, 5):
                    for c in range(2):
                        o = claim(pe, ("adag", n, c))
                        mm(o[:, :], C("selc")[:, tile(c)], modrow[:, n % 2, :], start=True, stop=False)
                        fill(mm(o[:, :], C("sel12")[0:ADA_CHUNKS, 2 * n:2 * n + 1].to_broadcast([ADA_CHUNKS, P]),
                                bada[:, :], start=False, stop=True), ("adag", n, c))
                else:
                    o = claim(pe, ("adac", n))
                    for q in range(4):
                        mm(o[:, 2 * q:2 * q + 2], modrow[:, n % 2, tile(q)], C("pick"), start=True, stop=False)
                        last = mm(o[:, 2 * q:2 * q + 2], bada[:, tile(q)], C("sel12")[0:ADA_CHUNKS, 2 * n:2 * n + 2],
                                  start=False, stop=True)
                    fill(last, ("adac", n))

            ada(0)
            pe.wait_ge(s["filt_in"], 16 * N_FILT)
            o = claim(pe, ("fu", 0))
            fill(mm(o[0:HY_FFN, 0:TOK], w1[0:HY_EMB, :], z_t[0:HY_EMB, :], start=True, stop=True), ("fu", 0))
            ada(1)
            ada_post(0)
            pe.wait_ge(s["fu_sin"], 1)
            o = claim(pe, ("fu", 1))
            fill(mm(o[0:HY_FFN, 0:TOK], w2[0:HY_FFN, :], fu[1][0:HY_FFN, :], start=True, stop=True), ("fu", 1))
            ada(2)
            ada_post(1)
            pe.wait_ge(s["fu_sin"], 2)
            for j in range(NT):
                for q in range(2):
                    o = claim(pe, ("fh", j, q))
                    fill(mm(o[:, :], fu[1][0:HY_FFN, tile(j)], w3[0:HY_FFN, q * 512:q * 512 + 512],
                            start=True, stop=True), ("fh", j, q))
            ada(3)
            ada_post(2)
            pe.wait_ge(s["const_in"], 16)
            pe.wait_ge(s["fsq_ready"], 1)
            for g, js in enumerate(((0,), (1, 2))):
                o = claim(pe, ("fss", g))
                for q in range(2):
                    for j in js:
                        for d in range(2):
                            last = mm(o[:, q * HYC:q * HYC + HYC], C("ones"), FSQ[q][:, j, d * HYC:d * HYC + HYC],
                                      start=(j == js[0] and d == 0), stop=(j == js[-1] and d == 1))
                fill(last, ("fss", g))
            ada_post(3)
            pe.wait_ge(s["xn_ready"], 1)
            for kt in range(KT):
                o = claim(pe, ("xT", kt))
                for j in range(NT):
                    last = tr(o[:, tile(j)], x_in[:, j, tile(kt)], ident)
                fill(last, ("xT", kt))
            pe.wait_ge(s["fs_ready"], 1)

            def dft(o, u, part, rhs):
                if u == 0:
                    return mm(o, C("dft_ctx")[:, part * P:part * P + P], rhs(0), start=True, stop=True)
                for tt in range(2):
                    a = (tt * 2 + u - 1) * 2 * P + part * P
                    last = mm(o, C("dft_lat")[:, a:a + P], rhs(1 + tt), start=(tt == 0), stop=(tt == 1))
                return last

            for u in range(3):
                for r in range(2):
                    o = claim(pe, ("fd", u, r))
                    fill(dft(o[:, :], u, r, lambda j: (FS, FD)[r][:, j, :]), ("fd", u, r))
            for g, js in enumerate(((0,), (1, 2))):
                o = claim(pe, ("fn", g))
                for j in js:
                    last = mm(o[0:1, :], C("alt"), FS[:, j, :], start=(j == js[0]), stop=(j == js[-1]))
                fill(last, ("fn", g))

            def proj_T(n, tiles=range(4)):
                w = chunk(pe, ("in", n))
                for i in tiles:
                    o = claim(pe, ("in", n, i))
                    for kt in range(KT):
                        last = mm(o[:, 0:TOK], w[:, kt, tile(i)], hT[:, kt, :], start=(kt == 0), stop=(kt == KT - 1))
                    fill(last, ("in", n, i))

            def proj_rows(n):
                w = chunk(pe, ("in", n))
                for j in range(NT):
                    o = claim(pe, ("in", n, j))
                    for kt in range(KT):
                        last = mm(o[:, :], hT[:, kt, tile(j)], w[:, kt, :], start=(kt == 0), stop=(kt == KT - 1))
                    fill(last, ("in", n, j))

            for kt in range(KT):
                taken(pe, ("xT", kt))
            for n in (2, 3):
                proj_T(n)
            proj_rows(4)
            for n in (0, 1):
                proj_T(n)

            for lev in range(NLEV):
                for d in range(2):
                    if lev < NLEV - 1:
                        pe.wait_ge(s["lev_ready"], 2 * lev + d + 1)
                        ka, qa = KL[:, d, :], QL[:, d, :]
                    else:
                        ka, qa = HK[:, d, :], HQ[:, :]
                    for par in range(2):
                        for g, blks in enumerate(((0, 1), (2,))):
                            o = claim(pe, ("lev", lev, d, par, g))
                            for i, b in enumerate(blks):
                                for t in range(2):
                                    a = t * TOK + b * P
                                    c = (i * 2 + t) * P
                                    last = mm(o[:, c:c + P], ka[par * 64:par * 64 + 64, a:a + P],
                                              qa[par * 64:par * 64 + 64, a:a + P], start=True, stop=True)
                            fill(last, ("lev", lev, d, par, g))
                if lev < 6:
                    ada(4 + lev)
                if lev >= 1 and lev <= 6:
                    ada_post(3 + lev)
            pe.wait_ge(s["hg_qk"], 2)
            for d in range(2):
                o = claim(pe, ("kt", d))
                for i in range(2):
                    b = 0 if i == 0 else (1 if d == 0 else 2)
                    for t in range(2):
                        c = (i * 2 + t) * P
                        last = tr(o[:, c:c + P], KL[:, d, t * TOK + b * P:t * TOK + b * P + P], ident)
                fill(last, ("kt", d))
            for d in range(2):
                taken(pe, ("kt", d))
                o = claim(pe, ("hU", d))
                for i in range(2):
                    b = 0 if i == 0 else (1 if d == 0 else 2)
                    for t in range(2):
                        c = (i * 2 + t) * P
                        last = mm(o[:, c:c + P], KTOK[:, d, i, t, :], TMH[:, b, t * P:t * P + P], start=True, stop=True)
                fill(last, ("hU", d))
            for d in range(2):
                for par in range(2):
                    for g in range(2):
                        taken(pe, ("lev", NLEV - 1, d, par, g))
            for j in range(NT):
                o = claim(pe, ("ho", j))
                first = True
                if j == 1:
                    for d in range(2):
                        taken(pe, ("hU", d))
                if j > 0:
                    for d in range(2):
                        w = (j - 1) if d == 0 else (2 - j)
                        for t in range(2):
                            mm(o[:, t * P:t * P + P], QL[:, d, t * TOK + j * P:t * TOK + j * P + P], HGS[:, w, d, t, :],
                               start=first, stop=False, skip_group_check=True)
                            first = False
                for t in range(2):
                    for par in range(2):
                        h = 2 * t + par
                        for d in range(2):
                            last = mm(o[:, h * 64:h * 64 + 64], SC[:, d, par, j, t, :], TMH[:, j, h * 64:h * 64 + 64],
                                      start=first, stop=(d == 1), skip_group_check=True)
                            first = False
                fill(last, ("ho", j))
            proj_T(5)
            proj_rows(6)

            def turn(name, src, ready, count):
                pe.wait_ge(s[ready], count)
                for t in range(2):
                    o = claim(pe, (name, t))
                    for j in range(NT):
                        last = tr(o[:, tile(j)], src[:, j, tile(t)], ident)
                    fill(last, (name, t))

            turn("hm", HO, "ho_ready", 1)
            pe.wait_ge(s["bd_ready"], 16 * 16)
            pe.wait_ge(s["xc_ready"], 1)
            for d in range(2):
                for k in range(2):
                    for t in range(2):
                        o = claim(pe, ("rg", d, k, t))
                        fill(mm(o[:, 0:RUN], BD[:, d, k, t, :], XC[:, t, SEG_C:SEG_C + RUN], start=True, stop=True),
                             ("rg", d, k, t))

            def spectra(n):
                for u in range(3):
                    o = claim(pe, ("V", n, u))
                    for r in range(2):
                        last = dft(o[:, r * HYC:r * HYC + HYC], u, r, lambda j: VT[:, j, :])
                    fill(last, ("V", n, u))
                for u in range(3):
                    taken(pe, ("V", n, u))
                for t in range(2):
                    o = claim(pe, ("y", n, t))
                    for r in range(2):
                        mm(o[:, 0:CTX], Y[:, 0, r, tile(t)], C("idft_ctx")[:, r * CTX:r * CTX + CTX],
                           start=(r == 0), stop=(r == 1))
                    for u in range(2):
                        for r in range(2):
                            a = (u * 2 + r) * LAT
                            last = mm(o[:, CTX:TOK], Y[:, 1 + u, r, tile(t)], C("idft_lat")[:, a:a + LAT],
                                      start=(u == 0 and r == 0), stop=(u == 1 and r == 1))
                    fill(last, ("y", n, t))

            def turn_tokens(n, src):
                for j in range(NT):
                    o = claim(pe, ("vt", n, j))
                    for t in range(2):
                        last = tr(o[:, tile(t)], src(t, j), ident)
                    fill(last, ("vt", n, j))

            pe.wait_ge(s["u_ready"], 1)
            turn_tokens(0, lambda t, j: U[:, t, SEG_C:SEG_C + P] if j == 0 else
                        U[:, t, SEG_L + (j - 1) * P:SEG_L + j * P])
            for j in range(NT):
                taken(pe, ("vt", 0, j))
            spectra(0)
            pe.wait_ge(s["z1"], 1)
            turn_tokens(1, lambda t, j: ZT[:, t, tile(j)])
            for j in range(NT):
                taken(pe, ("vt", 1, j))
            spectra(1)

            for i in range(4):
                taken(pe, ("in", 5, i))
            for i in range(4):
                o = claim(pe, ("rope", i))
                fill(mm(o[:, 0:LAT], C("swap"), PR[:, i, CTX:TOK], start=True, stop=True), ("rope", i))
            pe.wait_ge(s["rope"], 1)
            for par in range(2):
                o = claim(pe, ("rsc", par))
                rp = slice(par * 64, par * 64 + 64)
                for t in range(2):
                    last = mm(o[:, tile(t)], PR[rp, 2 + t, 0:CTX], PR[rp, t, 0:CTX], start=True, stop=True)
                fill(last, ("rsc", par))
            for h in range(4):
                rp = slice((h % 2) * 64, (h % 2) * 64 + 64)
                o = claim(pe, ("rsl", h))
                for st in range(2):
                    last = mm(o[:, st * LAT:st * LAT + LAT], PR[rp, 2 + h // 2, CTX + st * P:CTX + st * P + P],
                              PR[rp, h // 2, CTX:TOK], start=True, stop=True)
                fill(last, ("rsl", h))
            pe.wait_ge(s["rtail"], 1)
            o = claim(pe, "rkt")
            for d in range(2):
                for t in range(2):
                    last = tr(o[:, tile(2 * d + t)], TAIL[:, d, t, :], ident)
            fill(last, "rkt")
            taken(pe, "rkt")
            o = claim(pe, "rU")
            for d in range(2):
                for t in range(2):
                    last = mm(o[:, tile(2 * d + t)], RKT[:, d, t, :], TMR[:, 0, tile(t)], start=True, stop=True)
            fill(last, "rU")
            for par in range(2):
                taken(pe, ("rsc", par))
            for j in range(NT):
                o = claim(pe, ("ro", j))
                first = True
                if j == 1:
                    for h in range(4):
                        taken(pe, ("rsl", h))
                    pe.wait_ge(s["qd"], 1)
                    pe.wait_ge(s["rs_ready"], 16 * 4)
                if j > 0:
                    for d in range(2):
                        for t in range(2):
                            mm(o[:, tile(t)], QD[:, d, t, (j - 1) * P:j * P], RS[:, d, t, :],
                               start=first, stop=False, skip_group_check=True)
                            first = False
                for h in range(4):
                    c = slice(h * 64, h * 64 + 64)
                    if j == 0:
                        last = mm(o[:, c], WC[:, h % 2, h // 2, :], TMR[:, 0, c], start=first, stop=True,
                                  skip_group_check=True)
                        first = False
                    else:
                        for st in range(2):
                            a = st * LAT + (j - 1) * P
                            last = mm(o[:, c], WL[:, h, a:a + P], TMR[:, 1 + st, c], start=False, stop=(st == 1),
                                      skip_group_check=True)
                fill(last, ("ro", j))
            turn("rm", RO, "ro_ready", 1)

            pe.wait_ge(s["rgo"], 1)
            pe.wait_ge(s["hy_done"], 1)
            for name in ("hm", "rm"):
                for t in range(2):
                    taken(pe, (name, t))
            for n in range(2):
                w = chunk(pe, ("out", n))
                for j in range(NT):
                    o = claim(pe, ("out", n, j))
                    for kt in range(KT):
                        last = mm(o[:, :], hT[:, kt, tile(j)], w[:, kt, :], start=(kt == 0), stop=(kt == KT - 1))
                    fill(last, ("out", n, j))
            ada(10)
            ada(11)
            ada_post(10)
            ada_post(11)
            pe.wait_ge(s["n2_ready"], 1)
            for kt in range(KT):
                o = claim(pe, ("x2T", kt))
                for j in range(NT):
                    last = tr(o[:, tile(j)], h2tok[j][:, tile(kt)], ident)
                fill(last, ("x2T", kt))
            for kt in range(KT):
                taken(pe, ("x2T", kt))
            o = claim(pe, "logits")
            for j in range(NT):
                for kt in range(KT):
                    last = mm(o[:, j * E:j * E + E], hT[:, kt, tile(j)], wr[:, kt, :], start=(kt == 0),
                              stop=(kt == KT - 1))
            fill(last, "logits")
            for j in range(NT):
                for half in range(2):
                    o = claim(pe, ("h2", j, half))
                    for q in range(4):
                        last = tr(o[:, tile(q)], hT[:, half * 4 + q, tile(j)], ident)
                    fill(last, ("h2", j, half))
            pe.wait_ge(s["route"], 1)
            o = claim(pe, "places")
            for j in range(NT):
                for i in range(j + 1):
                    mm(o[:, j * E:j * E + E], C("triu") if i == j else C("ones"), RT[:, 6, i, :],
                       start=(i == 0), stop=(i == j))
            for i in range(NT):
                last = mm(o[:, NT * E:NT * E + E], C("ones"), RT[:, 6, i, :], start=(i == 0), stop=(i == NT - 1))
            fill(last, "places")
            o = claim(pe, "lst")
            for j in range(NT):
                pe.wait_ge(s["sel"], j + 1)
                for e in range(E):
                    last = mm(o[:, e:e + 1], SEL[:, e, :], tokid16[:, j:j + 1], start=(j == 0 and e == 0),
                              stop=(j == NT - 1), skip_group_check=True)
                if j < NT - 1:
                    last.then_inc(s["sel_used"], 1)
            fill(last, "lst")
            n = len(uses)
            for b in range(8):
                pe.wait_ge(emptied[b], (n - b + 7) // 8)

            def load_x(n, p, it, lead):
                pe.wait_ge(s[f"xe{p}"], 16 * it + 16)
                if not lead:
                    pe.wait_ge(s["xt_ready"], n)
                for kt in range(KT):
                    last = tr(psum[:, kt // 4, tile(kt % 4)], xe[p][:, tile(kt)], ident)
                last.then_inc(s["xt_filled"], 1)

            def experts(it, first, last_pair):
                for p in range(2):
                    n = 2 * it + p
                    base = 0 if p else PRE_USES
                    pe.wait_ge(s["xt_ready"], n + 1)
                    if not (first and p == 0):
                        pe.wait_ge(s["h_ready"], n)
                    for k, (what, bank) in enumerate((("gate_done", 2), ("up_done", 3))):
                        w = slot[NS * p + k]
                        pe.wait_ge(loaded[NS * p + k], 16 * (it + base) + 16)
                        for kt in range(KT):
                            ins = mm(psum[:, bank, :], xeT[p][:, kt, :], w[:, kt, :], start=(kt == 0), stop=(kt == KT - 1))
                        ins.then_inc(s[what], 1)
                    if not (last_pair and p == 1):
                        load_x(n + 1, 1 - p, it + p, False)
                    pe.wait_ge(s["h_ready"], n + 1)
                    if not (first and p == 0):
                        pe.wait_ge(s["ht_ready"], n)
                    for q in range(FE // P):
                        ins = tr(psum[:, 4, tile(q)], he[:, p, tile(q)], ident)
                    ins.then_inc(s["ht_filled"], 1)
                    w = slot[NS * p + 2][:, :, :].rearrange("p k n -> p (k n)").rearrange("p (k d) -> p k d", d=D)
                    pe.wait_ge(loaded[NS * p + 2], 16 * (it + base) + 16)
                    pe.wait_ge(s["ht_ready"], n + 1)
                    if not (first and p == 0):
                        pe.wait_ge(s["ya"], n)
                        pe.wait_ge(s["yb"], n)
                    for half in range(2):
                        for q in range(FE // P):
                            ins = mm(psum[:, 5 + half, :], heT[:, q, :], w[:, q, half * 512:half * 512 + 512],
                                     start=(q == 0), stop=(q == FE // P - 1))
                    ins.then_inc(s["down_done"], 1)

            load_x(0, 0, 0, True)
            experts(0, True, False)
            with pe.Fori(1, E // 2 - 1) as it:
                experts(it, False, False)
            experts(E // 2 - 1, False, True)

            with pe.If(further(pe) > 0):
                for o in range(OVER):
                    pe.wait_ge(s["o_sel"], o + 1)
                    if o > 0:
                        pe.wait_ge(s["o_lst"], o)
                    for i in range(2 * NT):
                        last = mm(psum[:, 7, 0:1], SO[:, i, :], C("tokid")[:, i % NT:i % NT + 1],
                                  start=(i == 0), stop=(i == 2 * NT - 1))
                    last.then_inc(s["o_selm"], 1)
                with pe.Fori(0, OVER) as o:
                    pe.wait_ge(s["o_xe"], 16 * o + 16)
                    for kt in range(KT):
                        last = tr(psum[:, kt // 4, tile(kt % 4)], xe[0][:, tile(kt)], ident)
                    last.then_inc(s["o_xt"], 1)
                    pe.wait_ge(s["o_xtr"], o + 1)
                    pe.wait_ge(s["o_w"], 48 * o + 48)
                    for k in range(2):
                        for kt in range(KT):
                            last = mm(psum[:, 2 + k, :], xeT[0][:, kt, :], slot[k][:, kt, :], start=(kt == 0),
                                      stop=(kt == KT - 1))
                    last.then_inc(s["o_up"], 1)
                    pe.wait_ge(s["o_h"], o + 1)
                    for q in range(FE // P):
                        last = tr(psum[:, 4, tile(q)], he[:, 0, tile(q)], ident)
                    last.then_inc(s["o_ht"], 1)
                    pe.wait_ge(s["o_htr"], o + 1)
                    w = slot[2][:, :, :].rearrange("p k n -> p (k n)").rearrange("p (k d) -> p k d", d=D)
                    for half in range(2):
                        for q in range(FE // P):
                            last = mm(psum[:, 5 + half, :], heT[:, q, :], w[:, q, half * 512:half * 512 + 512],
                                      start=(q == 0), stop=(q == FE // P - 1))
                    last.then_inc(s["o_down"], 1)

        def steps(eng, name):
            count = [0]

            def link(ins):
                count[0] += 1
                ins.then_inc(s[name], 1)
                eng.wait_ge(s[name], count[0])
            return link

        @block.sync
        def _(sp):
            last_of = {"ada": lambda n: ("ada", n), "in": lambda n: ("in", n, 2 if n in (4, 6) else 3),
                       "out": lambda n: ("out", n, NT - 1)}
            src_of = {"ada": A["w_ada"][0], "in": A["w_in"][0], "out": A["w_out"][0]}
            for i, (kind, n) in enumerate(PRE):
                if i >= NS:
                    take(sp, last_of[PRE[i - NS][0]](PRE[i - NS][1]))
                sp.dma_start(slot[i % NS][:, :, :],
                             src_of[kind][:, n * CW:n * CW + CW].rearrange("(k p) n -> p k n", p=P)
                             ).then_inc(loaded[i % NS], 16)
                if i == 0:
                    sp.dma_start(x_in[:, 0, :], A["x_prompt"][0]).then_inc(s["x_in"], 16)
                    sp.dma_start(x_in[:, 1:3, :], A["x_sample"][0].rearrange("(j p) d -> p j d", p=P)
                                 ).then_inc(s["x_in"], 16)

            def load_expert(e, p, k, it, signal=None):
                w = (A["w_gate"], A["w_up"], A["w_down"])[k]
                dst = slot[NS * p + k]
                src = w[0, e] if isinstance(e, int) else w[0, bass.ds(e, 1)].rearrange("o a b -> (o a) b")
                if k == 2:
                    dst = dst[:, :, :].rearrange("p k n -> p (k n)").rearrange("p (k d) -> p k d", d=D)
                    src = src.rearrange("(k p) d -> p k d", p=P)
                else:
                    dst = dst[:, :, :]
                    src = src.rearrange("(k p) f -> p k f", p=P)
                sp.dma_start(dst, src).then_inc(loaded[NS * p + k] if signal is None else signal, 16)

            for k in range(3):
                key = PRE[len(PRE) - NS + k]
                take(sp, last_of[key[0]](key[1]))
                load_expert(0, 0, k, 0)
            take(sp, ("rm", 1))
            sp.wait_ge(s["state_out"], 16 * 3)
            for k in range(3):
                load_expert(1, 1, k, 0)
            with sp.Fori(1, E // 2) as it:
                for p in range(2):
                    for k, what in enumerate(("gate_done", "up_done", "down_done")):
                        sp.wait_ge(s[what], 2 * it + p - 1)
                        load_expert(2 * it + p, p, k, it)
            with sp.If(further(sp) > 0):
                sp.wait_ge(s["down_done"], E)
                for k in range(3):
                    load_expert(sp.value_load(further_passes[0:1, 1:2], min_val=0, max_val=E - 1), 0, k, 0, s["o_w"])
                with sp.Fori(1, OVER) as o:
                    sp.wait_ge(s["o_down"], o)
                    e = sp.value_load(further_passes[0:1, bass.ds(o + 1, 1)], min_val=0, max_val=E - 1)
                    for k in range(3):
                        load_expert(e, 0, k, 0, s["o_w"])

        @block.gpsimd
        def _(pool):
            link = steps(pool, "pool_step")
            g = nc.gpsimd
            link(g.memset(mhalf[:, :], -0.5))
            g.memset(HGS[:, :, :, :, :], 0.0).then_inc(s["pads"], 1)

            def rstd(kind, dst, src):
                pool.wait_ge(s[kind + "_var"], 1)
                n = src.shape[-1]
                g.tensor_tensor(dst, src, mhalf[:, 0:n], ALU.pow).then_inc(s[kind + "_rstd"], 1)

            pool.wait_ge(s["mask_in"], 16)
            g.tensor_copy(mask[:, :, :, :].rearrange("p l d q -> p (l d q)"), mask_in).then_inc(s["mask_ready"], 1)
            rstd("x", stat[:, 1, 0:NT], stat[:, 0, 0:NT])
            pool.wait_ge(s["pads"], 1)
            zeros = HGS[:, :, :, :, :].rearrange("p w d t n -> p (w d t n)")
            for o in range(OVER):
                pool.dma_start(A["y_rows"][(E + o) * P:(E + o + 1) * P, :], zeros).then_inc(s["y_zero"], 16)
            pool.wait_ge(s["y_zero"], 16 * OVER)
            for half in range(2):
                r = slice(half * 64, half * 64 + 64)
                for d in range(2):
                    pool.dma_start(HGS[r, 0, d, :, half * 64:half * 64 + 64],
                                   A["state_hgrn"][0, 0, d].rearrange("(t h) k v -> h k t v", h=2)[half]
                                   ).then_inc(s["states0"], 16)
            take(pool, ("xT", KT - 1))
            for a, w in ((0, 2), (130, 3), (389, 1)):
                last = g.memset(CU[:, :, a:a + w], 0.0)
            last.then_inc(s["pads"], 1)
            pool.wait_ge(s["u_ready"], 1)
            pool.wait_ge(s["xc_ready"], 1)
            g.memset(XS[:, 0:3072], 0.0).then_inc(s["sc_zero"], 1)
            rstd("ho", stat[:, 3, 0:12], stat[:, 2, 0:12])
            take(pool, ("ho", NT - 1))
            link(g.memset(XS[:, 0:1024], 0.0))
            for k, name in enumerate(("rg_wa", "rg_wx")):
                for q in range(4):
                    r = slice(q * 32, q * 32 + 32)
                    for d in range(2):
                        pool.dma_start(BD[r, d, k, :, q * 32:q * 32 + 32],
                                       A[name][0, d].rearrange("(t q) i j -> q i t j", q=4)[q]).then_inc(s["bd_ready"], 16)
            take(pool, ("rg", 1, 1, 1))
            pool.dma_start(XR[:, 0, :], A["x_prompt"][0]).then_inc(s["res_in"], 16)
            pool.dma_start(XR[:, 1:3, :], A["x_sample"][0].rearrange("(j p) d -> p j d", p=P)).then_inc(s["res_in"], 16)
            pool.wait_ge(s["hy_done"], 1)
            link(g.memset(RS[:, :, :, :], 0.0))
            for half in range(2):
                r = slice(half * 64, half * 64 + 64)
                for d in range(2):
                    pool.dma_start(RS[r, d, :, half * 64:half * 64 + 64],
                                   A["state_ret"][0, 0, d].rearrange("(t h) k v -> h k t v", h=2)[half]
                                   ).then_inc(s["rs_ready"], 16)
            rstd("ro", stat[:, 3, 0:12], stat[:, 2, 0:12])
            rstd("n2", stat[:, 1, 0:NT], stat[:, 0, 0:NT])
            for j in range(NT):
                for half in range(2):
                    taken(pool, ("h2", j, half))
            for j in range(NT):
                pool.dma_start(A["h2_rows"][tile(j), :], h2tok[j][:, :]).then_inc(s["h2_out"], 16)
            taken(pool, "lst")

            pool.wait_ge(s["h2_out"], 16 * NT)
            for n in range(E):
                if n >= 2:
                    pool.wait_ge(s["xt_filled"], n - 1)
                g.indirect_dma_start(out=xe[n % 2][:, :], out_offset=None, in_=A["h2_rows"],
                                     in_offset=bass.IndirectOffsetOnAxis(ap=lst[:, n:n + 1], axis=0)
                                     ).then_inc(s[f"xe{n % 2}"], 16)
            with pool.If(further(pool) > 0):
                for o in range(OVER):
                    pool.wait_ge(s["o_lst"], o + 1)
                    pool.wait_ge(s["xt_filled"], E) if o == 0 else pool.wait_ge(s["o_xt"], o)
                    g.indirect_dma_start(out=xe[0][:, :], out_offset=None, in_=A["h2_rows"],
                                         in_offset=bass.IndirectOffsetOnAxis(ap=lsto[:, o:o + 1], axis=0)
                                         ).then_inc(s["o_xe"], 16)
                pool.wait_ge(s["o_out"], 16 * OVER)
            for p in range(2):
                pool.wait_ge(s[f"y_out{p}"], 16 * E // 2)
            for j in range(NT):
                for k in range(2):
                    g.indirect_dma_start(out=YG[k][:, j, :], out_offset=None, in_=A["y_rows"],
                                         in_offset=bass.IndirectOffsetOnAxis(ap=rows[:, j, k:k + 1], axis=0)).then_inc(s["fin_in"], 16)
            rstd("fin", stat[:, 1, 0:NT], stat[:, 0, 0:NT])

        @block.scalar
        def _(act):
            link = steps(act, "act_step")
            a = nc.scalar.activation
            act.dma_start(const[:, 0:FIRST], A["const"][:, 0:FIRST]).then_inc(s["first_in"], 16)
            vec = {"c": [A["c_ctx"].rearrange("(r n) -> r n", n=P), A["c"].rearrange("b (r n) -> (b r) n", n=P)],
                   "norm1": [A["norm1"].rearrange("b (r n) -> (b r) n", n=P)],
                   "norm2": [A["norm2"].rearrange("b (r n) -> (b r) n", n=P)],
                   "hcw": [A["hy_conv_w"].rearrange("b k (r n) -> (b k r) n", n=P)],
                   "hcb": [A["hy_conv_b"].rearrange("b (r n) -> (b r) n", n=P)],
                   "rcw": [A["rg_conv_w"].rearrange("b k (r n) -> (b k r) n", n=P)],
                   "rcb": [A["rg_conv_b"].rearrange("b (r n) -> (b r) n", n=P)],
                   "rba": [A["rg_ba"].rearrange("b d (r n) -> (b d r) n", n=P)],
                   "rbx": [A["rg_bx"].rearrange("b d (r n) -> (b d r) n", n=P)],
                   "lam": [A["rg_lambda"].rearrange("b d (r n) -> (b d r) n", n=P)],
                   "hyd": [A["hy_d"].rearrange("b d (r n) -> (b d r) n", n=P)],
                   "rst": [A["state_rglru"].rearrange("b l d (r n) -> (b l d r) n", n=P)]}
            n_vec = 0
            for name, parts in vec.items():
                r = VROWS[name]
                for part in parts:
                    act.dma_start(VR[r:r + part.shape[0], :], part).then_inc(s["vec_in"], 16)
                    r += part.shape[0]
                    n_vec += 1
            act.dma_start(bada[:, :], A["b_ada"].rearrange("b (r n) -> (b r) n", n=CW)).then_inc(s["vec_in"], 16)
            act.dma_start(SC16[:, 4:12], A["ret_decay"].rearrange("b d h -> b (d h)").to_broadcast([P, 8])
                          ).then_inc(s["vec_in"], 16)
            for half in range(2):
                act.dma_start(SC16[half * 64:half * 64 + 64, 12:16].rearrange("p (d t) -> p d t", d=2),
                              A["ret_decay"].rearrange("b d (t h) -> h b d t", h=2)[half].to_broadcast([64, 2, 2]),
                              allow_slow_non_contiguous=True).then_inc(s["vec_in"], 16)
            assert n_vec + 4 == N_VEC
            act.dma_start(w1[0:HY_EMB, :], A["hy_w1"][0]).then_inc(s["filt_in"], 16)
            act.dma_start(w2[0:HY_FFN, :], A["hy_w2"][0]).then_inc(s["filt_in"], 16)
            act.dma_start(w3[0:HY_FFN, :], A["hy_w3"][0]).then_inc(s["filt_in"], 16)
            act.dma_start(b12[0:HY_FFN, 0:1], A["hy_b1"].rearrange("b n -> n b"),
                          allow_slow_non_contiguous=True).then_inc(s["filt_in"], 16)
            act.dma_start(b12[0:HY_FFN, 1:2], A["hy_b2"].rearrange("b n -> n b"),
                          allow_slow_non_contiguous=True).then_inc(s["filt_in"], 16)
            act.dma_start(z_t[0:HY_EMB, :], A["z_table"]).then_inc(s["filt_in"], 16)
            act.dma_start(win, A["window"].rearrange("p (j n) -> p j n", j=NT)).then_inc(s["filt_in"], 16)
            act.dma_start(const[:, FIRST:], A["const"][:, FIRST:]).then_inc(s["const_in"], 16)
            act.dma_start(mask_in, A["masks"]).then_inc(s["mask_in"], 16)
            act.dma_start(wr[:, :, :], A["w_router"].rearrange("(k p) e -> p k e", p=P)).then_inc(s["late_in"], 16)
            act.dma_start(rbias[:, :], A["router_bias"].rearrange("(o e) -> o e", o=1).to_broadcast([P, E])
                          ).then_inc(s["late_in"], 16)
            act.dma_start(hgn[:, :], A["hg_norm"].to_broadcast([P, HYC])).then_inc(s["late_in"], 16)

            taken(act, "vcols")
            a(sige[:, :], VC[:, 0:16], ACT.Exp, scale=-1.0).then_inc(s["siluc_exp"], 1)
            act.wait_ge(s["sp_in"], 1)
            link(a(sptmp[:, 0, :], SC16[:, :], ACT.Abs))
            a(sptmp[:, 1, :], sptmp[:, 0, :], ACT.Exp, scale=-1.0).then_inc(s["sp_abs"], 1)
            act.wait_ge(s["x_in"], 32)
            for j in range(NT):
                last = a(T[:, 3072 + j * D:3072 + j * D + D], x_in[:, j, :], ACT.Square, accum_out=stat[:, 2, j:j + 1])
            last.then_inc(s["x_sq"], 1)

            def modrow_out(n):
                o = take(act, ("ada", n))
                if n >= 2:
                    take(act, ("adag", n - 2, 1) if (n - 2) // 2 in (2, 5) else ("adac", n - 2))
                give(a(modrow[:, n % 2, :], o[:, :], ACT.Copy), ("ada", n))

            def gate_out(n, dst):
                for c in range(2):
                    o = take(act, ("adag", n, c))
                    give(a(dst[:, c, (n % 2) * CW:(n % 2) * CW + CW], o[:, :], ACT.Copy), ("adag", n, c))

            modrow_out(0)
            act.wait_ge(s["fu_arg"], 1)
            a(fu[1][0:HY_FFN, :], fu[0][0:HY_FFN, :], ACT.Sin).then_inc(s["fu_sin"], 1)
            modrow_out(1)
            act.wait_ge(s["fu_arg"], 2)
            a(fu[1][0:HY_FFN, :], fu[0][0:HY_FFN, :], ACT.Sin).then_inc(s["fu_sin"], 1)
            modrow_out(2)
            modrow_out(3)
            for j in range(NT):
                for q in range(2):
                    taken(act, ("fh", j, q))
            for q in range(2):
                v = FH[:, :, q, :, :].rearrange("p j d c -> p j (d c)")
                last = a(FSQ[q], v, ACT.Square)
            last.then_inc(s["fsq_ready"], 1)
            for g in range(2):
                taken(act, ("fss", g))
            a(FRS, FRS, ACT.Sqrt).then_inc(s["frs_sqrt"], 1)
            act.wait_ge(s["mod1"], 1)
            for kt in range(1, KT, 2):
                o = take(act, ("xT", kt))
                for c, r in ((0, slice(0, CTX)), (1, slice(CTX, TOK))):
                    last = a(hT[:, kt, r], o[:, r], ACT.Identity, scale=AB[:, 0, kt, c:c + 1], bias=MC[:, 0, kt, c:c + 1])
                give(last, ("xT", kt))
            for i in range(4):
                o = take(act, ("in", 2, i))
                dst = RGG[:, i, :] if i < 2 else HQ[:, (i - 2) * TOK:(i - 1) * TOK]
                give(a(dst, o[:, 0:TOK], ACT.Copy), ("in", 2, i))
            act.wait_ge(s["fs_ready"], 1)
            for i in range(4):
                o = take(act, ("in", 3, i))
                give(a(LF[:, i // 2, (i % 2) * TOK:(i % 2 + 1) * TOK], o[:, 0:TOK], ACT.Copy), ("in", 3, i))
            for i in range(4):
                taken(act, ("in", 3, i))
            link(a(W, LF, ACT.Abs))
            link(a(W, W, ACT.Exp, scale=-1.0))
            a(W, W, ACT.Ln, bias=1.0).then_inc(s["hg_abs"], 1)
            a(HK[:, :, :], LF, ACT.Exp).then_inc(s["hg_exp"], 1)
            for g in range(2):
                taken(act, ("fn", g))
            for i in (2, 3):
                taken(act, ("in", 2, i))
            a(QL[:, 0, :], HQ[:, :], ACT.Exp, scale=-1.0).then_inc(s["hq_exp"], 1)
            for j in range(NT):
                o = take(act, ("in", 4, j))
                give(a(TMH[:, j, :], o[:, :], ACT.Copy), ("in", 4, j))
            for n in (0, 1):
                for i in range(4):
                    o = take(act, ("in", n, i))
                    a(CU[:, 4 * n + i, SEG_C:SEG_C + CTX], o[:, 0:CTX], ACT.Copy)
                    give(a(CU[:, 4 * n + i, SEG_L:SEG_L + LAT], o[:, CTX:TOK], ACT.Copy), ("in", n, i))
            for lev in range(NLEV):
                if lev < NLEV - 1:
                    for d in range(2):
                        act.wait_ge(s["lev_arg"], 2 * lev + d + 1)
                        a(W[:, d, :], W[:, d, :], ACT.Exp).then_inc(s["lev_exp"], 1)
                if 1 <= lev <= 6:
                    modrow_out(3 + lev)
                if lev in (2, 3):
                    gate_out(2 + lev, G1)
            act.wait_ge(s["hg_tx"], 1)
            a(W, HX[:, :, :], ACT.Exp)
            a(LF, LF, ACT.Exp)
            a(HTOT[:, :, :], HTOT[:, :, :], ACT.Exp).then_inc(s["hg_texp"], 1)
            take(act, ("kt", 1))
            act.wait_ge(s["hg_qk"], 2)
            a(HGATE, TMH[:, :, HYC:2 * HYC], ACT.Exp, scale=-1.0).then_inc(s["ho_gexp"], 1)
            for j in range(NT):
                o = take(act, ("ho", j))
                give(a(HO[:, j, :], o[:, 0:HYC], ACT.Copy), ("ho", j))
            for i in range(4):
                o = take(act, ("in", 5, i))
                give(a(PR[:, i, :], o[:, 0:TOK], ACT.Copy, scale=1.0 if i < 2 else DH ** -0.5), ("in", 5, i))
            for j in range(NT):
                o = take(act, ("in", 6, j))
                give(a(TMR[:, j, :], o[:, :], ACT.Copy), ("in", 6, j))
            for t in range(2):
                o = take(act, ("hm", t))
                give(a(hT[:, 4 + t, :], o[:, 0:TOK], ACT.Copy), ("hm", t))
            act.wait_ge(s["gelu_arg"], 1)
            for d in range(2):
                for k in range(2):
                    for t in range(2):
                        o = take(act, ("rg", d, k, t))
                        c = 4 * k + 2 * d + t
                        give(a(RI[:, d, k, t, :], o[:, 0:RUN], ACT.Tanh, scale=0.5, bias=halfb[:, c:c + 1]),
                             ("rg", d, k, t))
            for d in range(2):
                for t in range(2):
                    taken(act, ("rg", d, 0, t))
            for d in range(2):
                for t in range(2):
                    c = lamc[:, 2 * d + t:2 * d + t + 1]
                    a(RA[:, d, t, :], RI[:, d, 0, t, :], ACT.Exp, scale=c, bias=c)
                    last = a(RB[:, d, t, :], RI[:, d, 0, t, :], ACT.Tanh, scale=c, bias=c)
            last.then_inc(s["rg_a"], 1)
            a(HQ[:, :], HQ[:, :], ACT.Tanh, scale=math.sqrt(2.0 / math.pi)).then_inc(s["gelu_t"], 1)
            act.wait_ge(s["rg_b2"], 1)
            a(RB, RB, ACT.Sqrt, scale=-1.0).then_inc(s["rg_b"], 1)
            for n in range(2):
                for j in range(NT):
                    o = take(act, ("vt", n, j))
                    give(a(VT[:, j, :], o[:, 0:HYC], ACT.Copy), ("vt", n, j))
            act.wait_ge(s["hy_done"], 1)
            cnt = C("count")
            for t in range(2):
                for d in range(2):
                    c = SC16[:, 12 + 2 * d + t:13 + 2 * d + t]
                    a(TAIL[:, d, t, :], cnt[:, 0:P] if d else cnt[:, P - 1::-1], ACT.Exp, scale=c)
                    last = a(EI[:, d, t, :], cnt[:, LAT:0:-1] if d else cnt[:, 1:LAT + 1], ACT.Exp, scale=c)
            last.then_inc(s["ei"], 1)
            for h in range(4):
                f, b = SC16[:, 4 + h:5 + h], SC16[:, 8 + h:9 + h]
                a(DEC[:, h, 0, :], C("dist_f"), ACT.Exp, scale=f)
                a(DTMP[:, h, :], C("dist_b"), ACT.Exp, scale=b)
                a(DEC[:, h, 1, :], C("dist_up"), ACT.Exp, scale=f)
                last = a(DEC[:, h, 2, :], C("dist_lo"), ACT.Exp, scale=b)
            last.then_inc(s["dec"], 1)
            act.wait_ge(s["rtail"], 1)
            a(RGATE, TMR[:, :, HYC:2 * HYC], ACT.Exp, scale=-1.0).then_inc(s["ro_gexp"], 1)
            o = take(act, "rkt")
            give(a(RKT.rearrange("p d t n -> p (d t n)"), o[:, :], ACT.Copy), "rkt")
            taken(act, "rU")
            act.wait_ge(s["rgo"], 1)
            for i, name in enumerate(("new_state_hgrn", "new_state_ret")):
                act.dma_start(O[name][0, 0].rearrange("d (t h) k v -> (h k) d t v", h=2), STO[:, 2 * i:2 * i + 2, :, :]
                              ).then_inc(s["state_out"], 16)
            act.dma_start(O["new_state_rglru"][0, 0].rearrange("d (t p) -> p d t", p=P),
                          RGO[:, :].rearrange("p (d t) -> p d t", d=2), allow_slow_non_contiguous=True).then_inc(s["state_out"], 16)
            for j in range(NT):
                o = take(act, ("ro", j))
                give(a(RO[:, j, :], o[:, 0:HYC], ACT.Copy), ("ro", j))
            for t in range(2):
                o = take(act, ("rm", t))
                give(a(hT[:, 6 + t, :], o[:, 0:TOK], ACT.Copy), ("rm", t))
            act.wait_ge(s["state_out"], 48)
            modrow_out(10)
            modrow_out(11)
            gate_out(10, G2)
            gate_out(11, G2)
            act.wait_ge(s["x1"], 1)
            for j in range(NT):
                last = a(h2tok[j][:, :], XR[:, j, :], ACT.Square, accum_out=stat[:, 2, j:j + 1])
            last.then_inc(s["n2_sq"], 1)
            for kt in range(1, KT, 2):
                o = take(act, ("x2T", kt))
                for c, r in ((0, slice(0, CTX)), (1, slice(CTX, TOK))):
                    last = a(hT[:, kt, r], o[:, r], ACT.Identity, scale=AB[:, 1, kt, c:c + 1], bias=MC[:, 2, kt, c:c + 1])
                give(last, ("x2T", kt))
            for j in range(NT):
                for half in range(2):
                    o = take(act, ("h2", j, half))
                    give(a(h2tok[j][:, half * 512:half * 512 + 512], o[:, :], ACT.Copy), ("h2", j, half))
                if j == 0:
                    taken(act, "logits")
                    a(RT[:, 0], RT[:, 0], ACT.Exp).then_inc(s["logits_exp"], 1)

            def xt_out(n, p, it, lead):
                act.wait_ge(s["xt_filled"], n + 1)
                if not lead:
                    act.wait_ge(s["up_done"], n - 1)
                a(xeTa[:, p].rearrange("p k n -> p (k n)"), psum[:, 0:2, :].rearrange("p b n -> p (b n)"), ACT.Copy
                  ).then_inc(s["xt_ready"], 1)

            def experts(it, first, last_pair):
                for p in range(2):
                    n = 2 * it + p
                    act.wait_ge(s["gate_done"], n + 1)
                    if not first:
                        act.wait_ge(s["ht_filled"], n - 1)
                    a(he[:, p, :], psum[:, 2, :], ACT.Exp, scale=-1.0).then_inc(s["g_exp"], 1)
                    if not (last_pair and p == 1):
                        xt_out(n + 1, 1 - p, it + p, first and p == 0)
                    act.wait_ge(s["down_done"], n + 1)
                    if not first:
                        act.wait_ge(s[f"y_out{p}"], 16 * it)
                    a(ye[p][:, 0:512], psum[:, 5, :], ACT.Copy).then_inc(s["ya"], 1)
                    act.wait_ge(s["ya"], n + 1)
                    act.wait_ge(s["yb"], n + 1)
                    dst = A["y_rows"][n * ROWS:n * ROWS + P, :] if isinstance(n, int) else \
                        A["y_rows"][bass.ds(n * ROWS, P), :]
                    act.dma_start(dst, ye[p][:, :]).then_inc(s[f"y_out{p}"], 16)

            xt_out(0, 0, 0, True)
            experts(0, True, False)
            with act.Fori(1, E // 2 - 1) as it:
                experts(it, False, False)
            experts(E // 2 - 1, False, True)
            with act.If(further(act) > 0):
                with act.Fori(0, OVER) as o:
                    act.wait_ge(s["o_xt"], o + 1)
                    a(xeTa[:, 0].rearrange("p k n -> p (k n)"), psum[:, 0:2, :].rearrange("p b n -> p (b n)"), ACT.Copy
                      ).then_inc(s["o_xtr"], 1)
                    act.wait_ge(s["o_up"], o + 1)
                    a(he[:, 0, :], psum[:, 2, :], ACT.Exp, scale=-1.0).then_inc(s["o_exp"], 1)
                    act.wait_ge(s["o_y"], o + 1)
                    act.dma_start(A["y_rows"][bass.ds((E + o) * P, P), :], ye[0][:, :]).then_inc(s["o_out"], 16)
                    act.wait_ge(s["o_out"], 16 * o + 16)
            act.dma_start(NF, A["norm_final"].rearrange("(o n) -> o n", o=1).to_broadcast([P, D])
                          ).then_inc(s["nf_in"], 16)
            act.wait_ge(s["x2"], 1)
            for j in range(NT):
                last = a(YG[1][:, j, :], XR[:, j, :], ACT.Square, accum_out=stat[:, 2, j:j + 1])
            last.then_inc(s["fin_sq"], 1)
            act.wait_ge(s["fin_ready"], 1)
            act.dma_start(O["y_prompt"][0], XR[:, 0, :]).then_inc(s["fin_out"], 16)
            act.dma_start(O["y_sample"][0].rearrange("(j p) d -> p j d", p=P), XR[:, 1:3, :]).then_inc(s["fin_out"], 16)
            act.wait_ge(s["fin_out"], 32)

        @block.vector
        def _(dve):
            link = steps(dve, "dve_step")
            v = nc.vector

            o = take(dve, "vcols")
            give(v.tensor_copy(VC[:, :], o[:, 0:NV]), "vcols")
            taken(dve, "vcols")
            dve.wait_ge(s["vec_in"], 16 * N_VEC)
            v.tensor_copy(SC16[:, 0:4], VC[:, VROWS["lam"]:VROWS["lam"] + 4]).then_inc(s["sp_in"], 1)
            v.tensor_scalar(halfb[:, :], VC[:, VROWS["rba"]:VROWS["rba"] + 8], 0.5, None, ALU.mult)
            dve.wait_ge(s["siluc_exp"], 1)
            link(v.memset(siluc[:, :, :], 0.0))
            link(v.tensor_scalar(sige[:, :], sige[:, :], 1.0, None, ALU.add))
            link(v.reciprocal(sige[:, :], sige[:, :]))
            v.tensor_tensor(siluc[:, :, 0:2].rearrange("p k c -> p c k"),
                            sige[:, :].rearrange("p (c k) -> p c k", c=2),
                            VC[:, 0:16].rearrange("p (c k) -> p c k", c=2), ALU.mult).then_inc(s["siluc"], 1)
            dve.wait_ge(s["x_sq"], 1)
            v.tensor_scalar(stat[:, 0, 0:NT], stat[:, 2, 0:NT], 1.0 / D, EPS, ALU.mult, ALU.add).then_inc(s["x_var"], 1)
            dve.wait_ge(s["sp_abs"], 1)
            w = sptmp[:, 1, :]
            link(v.tensor_scalar(sptmp[:, 2, :], w, 2.0, None, ALU.add))
            link(v.reciprocal(sptmp[:, 2, :], sptmp[:, 2, :]))
            link(v.tensor_tensor(sptmp[:, 2, :], sptmp[:, 2, :], w, ALU.mult))
            link(v.tensor_tensor(sptmp[:, 3, :], sptmp[:, 2, :], sptmp[:, 2, :], ALU.mult))
            link(v.tensor_scalar(sptmp[:, 4, :], sptmp[:, 3, :], 1.0 / 17, 1.0 / 15, ALU.mult, ALU.add))
            for k in range(6, -1, -1):
                link(v.tensor_tensor(sptmp[:, 4, :], sptmp[:, 4, :], sptmp[:, 3, :], ALU.mult))
                link(v.tensor_scalar(sptmp[:, 4, :], sptmp[:, 4, :], 1.0 / (2 * k + 1), None, ALU.add))
            link(v.scalar_tensor_tensor(sptmp[:, 4, :], sptmp[:, 4, :], -2.0, sptmp[:, 2, :], ALU.mult, ALU.mult))
            link(v.scalar_tensor_tensor(SC16[:, :], SC16[:, :], 0.0, sptmp[:, 4, :], ALU.min, ALU.add))
            v.tensor_scalar(lamc[:, :], SC16[:, 0:4], 4.0, None, ALU.mult).then_inc(s["sp_ready"], 1)
            dve.wait_ge(s["x_rstd"], 1)
            for j in range(NT):
                last = v.tensor_scalar(x_in[:, j, :], x_in[:, j, :], stat[:, 1, j:j + 1], None, ALU.mult)
            last.then_inc(s["xn_ready"], 1)

            def sine_arg(n):
                o = take(dve, ("fu", n))
                r, k = fu[0][0:HY_FFN, :], fu[2][0:HY_FFN, :]
                give(v.tensor_scalar(r, o[0:HY_FFN, 0:TOK], b12[0:HY_FFN, n:n + 1], None, ALU.add), ("fu", n))
                taken(dve, ("fu", n))
                link(v.tensor_scalar(k, r, 1.0 / (2 * math.pi), MAGIC, ALU.mult, ALU.add))
                link(v.tensor_scalar(k, k, MAGIC, None, ALU.subtract))
                link(v.scalar_tensor_tensor(r, k, -TURN_HI, r, ALU.mult, ALU.add))
                link(v.scalar_tensor_tensor(r, k, -TURN_LO, r, ALU.mult, ALU.add))
                v.tensor_scalar(r, r, PI_DOWN, -PI_DOWN, ALU.min, ALU.max).then_inc(s["fu_arg"], 1)

            def modcol_out(n):
                o = take(dve, ("adac", n))
                kind = {0: 0, 1: 1, 3: 2, 4: 3}[n // 2]
                give(v.tensor_copy(MC[:, kind, (n % 2) * 4:(n % 2) * 4 + 4, :],
                                   o[:, 0:8].rearrange("p (k c) -> p k c", c=2)), ("adac", n))

            dve.wait_ge(s["filt_in"], 16 * N_FILT)
            sine_arg(0)
            modcol_out(0)
            sine_arg(1)
            modcol_out(1)
            for j in range(NT):
                for q in range(2):
                    o = take(dve, ("fh", j, q))
                    ins = v.tensor_tensor(FH[:, j, q, :, :], o[:, :].rearrange("p (d c) -> p d c", d=2),
                                          win[:, j, :].unsqueeze(1).to_broadcast([P, 2, HYC]), ALU.mult)
                    give(ins, ("fh", j, q))
            modcol_out(2)
            for g in range(2):
                o = take(dve, ("fss", g))
                give(v.tensor_scalar(FRS[:, g, :], o[:, :], EPS, None, ALU.add), ("fss", g))
            modcol_out(3)
            taken(dve, ("adac", 2))
            taken(dve, ("adac", 3))
            v.scalar_tensor_tensor(AB[:, 0], MC[:, 1], 1.0,
                                   VC[:, VROWS["norm1"]:VROWS["norm1"] + KT].unsqueeze(2).to_broadcast([P, KT, 2]),
                                   ALU.add, ALU.mult).then_inc(s["mod1"], 1)
            dve.wait_ge(s["mod1"], 1)

            def modulate(name, which, kts):
                for kt in kts:
                    o = take(dve, (name, kt))
                    for c, r in ((0, slice(0, CTX)), (1, slice(CTX, TOK))):
                        last = v.tensor_scalar(hT[:, kt, r], o[:, r], AB[:, which, kt, c:c + 1],
                                               MC[:, 2 * which, kt, c:c + 1], ALU.mult, ALU.add)
                    give(last, (name, kt))

            dve.wait_ge(s["fsq_ready"], 1)
            for j in (0, 1):
                link(v.memset(FH[0:1, j, :, 1, :], 0.0))
            v.tensor_tensor(FS.rearrange("p j (o c) -> p (j o) c", o=2),
                            FH[:, :, :, 0, :].rearrange("p j o c -> p (j o) c"),
                            FH[:, :, :, 1, :].rearrange("p j o c -> p (j o) c"), ALU.add)
            v.tensor_tensor(FD.rearrange("p j (o c) -> p (j o) c", o=2),
                            FH[:, :, :, 0, :].rearrange("p j o c -> p (j o) c"),
                            FH[:, :, :, 1, :].rearrange("p j o c -> p (j o) c"), ALU.subtract).then_inc(s["fs_ready"], 1)
            modulate("xT", 0, range(0, KT, 2))
            dve.wait_ge(s["frs_sqrt"], 1)
            link(v.reciprocal(FRS, FRS))
            dve.wait_ge(s["mask_ready"], 1)
            for u in range(3):
                for r in range(2):
                    o = take(dve, ("fd", u, r))
                    give(v.tensor_tensor(HF[:, u, r].rearrange("p o c -> p (o c)"), o[:, :], FRS[:, min(u, 1), :],
                                         ALU.mult), ("fd", u, r))
            for g in range(2):
                o = take(dve, ("fn", g))
                give(v.tensor_tensor(HNY[0:1, g].rearrange("p o c -> p (o c)"), o[0:1, :], FRS[0:1, g, :], ALU.mult),
                     ("fn", g))

            dve.wait_ge(s["hg_abs"], 1)
            dve.wait_ge(s["hg_exp"], 1)
            link(v.scalar_tensor_tensor(LF, LF, 0.0, W, ALU.min, ALU.subtract))
            for d in range(2):
                dst = HX[:, 0, :] if d == 0 else W[:, 1, :]
                for t in range(2):
                    r = slice(t * TOK, t * TOK + TOK)
                    last = v.tensor_tensor_scan(dst[:, r], C("reset"), LF[:, d, r], 0.0, ALU.mult, ALU.add)
            link(last)
            wb = W[:, 1, :].rearrange("p (g n) -> p g n", n=P)
            xb = HX[:, 1, :].rearrange("p (g n) -> p g n", n=P)
            v.tensor_copy(HTOT[:, 0, :], HX[:, 0, :].rearrange("p (g n) -> p g n", n=P)[:, :, P - 1])
            v.tensor_copy(HTOT[:, 1, :], wb[:, :, P - 1])
            v.tensor_copy(xb[:, :, 1:P], wb[:, :, 0:P - 1])
            v.memset(xb[:, :, 0:1], 0.0)
            link(v.tensor_scalar(HK[:, :, :], HK[:, :, :], 1.0, None, ALU.add))
            v.reciprocal(HK[:, :, :], HK[:, :, :])
            dve.wait_ge(s["hq_exp"], 1)
            link(v.tensor_scalar(QL[:, 0, :], QL[:, 0, :], 1.0, None, ALU.add))
            link(v.reciprocal(QL[:, 0, :], QL[:, 0, :]))
            link(v.tensor_tensor(HQ[:, :], HQ[:, :], QL[:, 0, :], ALU.mult))
            v.memset(QL, 0.0)
            link(v.memset(KL, 0.0))

            def conv(dst, src, taps, first, w, b, groups):
                n = PADW - (taps - 1)
                for k in range(taps):
                    for t in range(groups):
                        i_, o_ = src(t)[:, k:k + n], dst(t)[:, first:first + n]
                        if k == 0:
                            last = v.tensor_scalar(o_, i_, w(k, t), b(t), ALU.mult, ALU.add)
                        else:
                            last = v.scalar_tensor_tensor(o_, i_, w(k, t), o_, ALU.mult, ALU.add)
                    if k < taps - 1:
                        link(last)
                return last

            dve.wait_ge(s["pads"], 2)
            for n in (0, 1):
                for i in range(4):
                    taken(dve, ("in", n, i))
            conv(lambda t: U[:, t, :], lambda t: CU[:, t, :], 3, 1, lambda k, t: col("hcw", 6 * k + t),
                 lambda t: col("hcb", t), 6).then_inc(s["u_ready"], 1)
            conv(lambda t: XC[:, t, :], lambda t: CU[:, 6 + t, :], 4, 2, lambda k, t: col("rcw", 2 * k + t),
                 lambda t: col("rcb", t), 2).then_inc(s["xc_ready"], 1)

            scf = XS[:, 0:3072].rearrange("p (e g q) -> p e g q", e=4, g=6)

            def place_scores(lev):
                for d in range(2):
                    for par in range(2):
                        for g, (a0, b0) in enumerate(((0, 4), (4, 6))):
                            o = take(dve, ("lev", lev, d, par, g))
                            give(v.copy_predicated(
                                scf[:, 2 * d + par, a0:b0, :],
                                mask[:, lev, d, :].unsqueeze(1).to_broadcast([P, b0 - a0, P]),
                                o[:, 0:(b0 - a0) * P].rearrange("p (g q) -> p g q", q=P)), ("lev", lev, d, par, g))

            for lev, h in enumerate(LEVELS):
                def halves(a):
                    b = a.rearrange("p (g n) -> p g n", n=2 * h)
                    return b[:, :, 0:h], b[:, :, h:2 * h], b
                if lev > 0:
                    dve.wait_ge(s["lev_ready"], 2 * lev)
                for d in range(2):
                    x0, x1, x = halves(HX[:, d, :])
                    e0, e1, _ = halves(W[:, d, :])
                    ref = x[:, :, h - 1 + d:h + d].to_broadcast([P, 2 * TOK // (2 * h), h])
                    if d == 0:
                        v.tensor_tensor(e0, ref, x0, ALU.subtract)
                        v.tensor_tensor(e1, x1, ref, ALU.subtract).then_inc(s["lev_arg"], 1)
                    else:
                        v.tensor_tensor(e0, ref, x0, ALU.subtract)
                        v.tensor_tensor(e1, x1, ref, ALU.subtract).then_inc(s["lev_arg"], 1)
                for d in range(2):
                    e0, e1, _ = halves(W[:, d, :])
                    q0, q1, _ = halves(HQ[:, :])
                    k0, k1, _ = halves(HK[:, d, :])
                    ql0, ql1, _ = halves(QL[:, d, :])
                    kl0, kl1, _ = halves(KL[:, d, :])
                    dve.wait_ge(s["lev_exp"], 2 * lev + d + 1)
                    if lev > 0:
                        take(dve, ("lev", lev - 1, d, 1, 1))
                    if d == 0:
                        v.tensor_tensor(ql1, q1, e1, ALU.mult)
                        v.tensor_tensor(kl0, k0, e0, ALU.mult).then_inc(s["lev_ready"], 1)
                    else:
                        v.tensor_tensor(ql0, q0, e0, ALU.mult)
                        v.tensor_tensor(kl1, k1, e1, ALU.mult).then_inc(s["lev_ready"], 1)
                if lev == 0:
                    dve.wait_ge(s["sc_zero"], 1)
                else:
                    place_scores(lev - 1)
                if 2 + lev in (6, 7, 8):
                    modcol_out(2 + lev)
            dve.wait_ge(s["lev_ready"], 2 * NLEV - 2)
            last = v.scalar_tensor_tensor(
                LF.rearrange("p d (g n) -> p (d g) n", n=P), HX[:, :, :].rearrange("p d (g n) -> p (d g) n", n=P), -1.0,
                HTOT[:, :, :].rearrange("p d g -> p (d g)").unsqueeze(2).to_broadcast([P, 12, P]), ALU.mult, ALU.add)
            last.then_inc(s["hg_tx"], 1)
            place_scores(NLEV - 2)
            modcol_out(9)
            place_scores(NLEV - 1)
            dve.wait_ge(s["hg_texp"], 1)
            v.tensor_tensor(QL[:, 0, :], HQ[:, :], W[:, 0, :], ALU.mult)
            v.tensor_tensor(KL[:, 0, :], HK[:, 0, :], LF[:, 0, :], ALU.mult).then_inc(s["hg_qk"], 1)
            v.tensor_tensor(QL[:, 1, :], HQ[:, :], LF[:, 1, :], ALU.mult)
            v.tensor_tensor(KL[:, 1, :], HK[:, 1, :], W[:, 1, :], ALU.mult).then_inc(s["hg_qk"], 1)
            for d in range(2):
                o = take(dve, ("kt", d))
                give(v.tensor_copy(KTOK[:, d].rearrange("p i t n -> p (i t n)"), o[:, :]), ("kt", d))
            dve.wait_ge(s["states0"], 16 * 4)

            def diagonals(o, dst):
                for half in range(2):
                    r = slice(half * 64, half * 64 + 64)
                    yield r, o[r, :, half * 64:half * 64 + 64], dst[r]

            for d in range(2):
                o = take(dve, ("hU", d))
                oo = o[:, :].rearrange("p (i t n) -> p i t n", i=2, t=2)
                for r, src, dst in diagonals(oo[:, 0], STO[:, d]):
                    v.tensor_copy(dst, src)
                b = 1 if d == 0 else 2
                for t in range(2):
                    for half in range(2):
                        r, c = slice(half * 64, half * 64 + 64), slice(half * 64, half * 64 + 64)
                        last = v.scalar_tensor_tensor(HGS[r, 1, d, t, c], HGS[r, 0, d, t, c],
                                                      HTOT[r, d, 3 * t + b:3 * t + b + 1], oo[r, 1, t, c],
                                                      ALU.mult, ALU.add)
                give(last, ("hU", d))

            def head_norm(name, x, x2, gate, g_src, gain):
                n = x.shape[1] * 4
                for j in range(NT):
                    taken(dve, (name, j))
                link(v.tensor_tensor(x2, x, x, ALU.mult))
                link(v.tensor_reduce(stat[:, 0, 0:n], x2.rearrange("p j (h c) -> p (j h) c", c=64), AX.X, ALU.add))
                v.tensor_scalar(stat[:, 2, 0:n], stat[:, 0, 0:n], 1.0 / 64, EPS, ALU.mult, ALU.add
                                ).then_inc(s[name + "_var"], 1)
                dve.wait_ge(s[name + "_gexp"], 1)
                link(v.tensor_scalar(gate, gate, 1.0, None, ALU.add))
                link(v.reciprocal(gate, gate))
                link(v.tensor_tensor(gate, gate, g_src, ALU.mult))
                if gain is not None:
                    link(v.tensor_tensor(gate, gate, gain, ALU.mult))
                dve.wait_ge(s[name + "_rstd"], 1)
                xv = x.rearrange("p j (h c) -> p (j h) c", c=64)
                link(v.tensor_tensor(xv, xv, stat[:, 3, 0:n].unsqueeze(2).to_broadcast([P, n, 64]), ALU.mult))
                v.tensor_tensor(x, x, gate, ALU.mult).then_inc(s[name + "_ready"], 1)

            dve.wait_ge(s["late_in"], 48)
            head_norm("ho", HO, HO2, HGATE, TMH[:, :, HYC:2 * HYC], hgn[:, :].unsqueeze(1).to_broadcast([P, NT, HYC]))

            gx = RGG[:, :, :].rearrange("p t n -> p (t n)")
            link(v.tensor_tensor(HQ[:, :], gx, gx, ALU.mult))
            link(v.tensor_scalar(HQ[:, :], HQ[:, :], 0.044715, 1.0, ALU.mult, ALU.add))
            v.tensor_tensor(HQ[:, :], HQ[:, :], gx, ALU.mult).then_inc(s["gelu_arg"], 1)
            for d in range(2):
                for k in range(2):
                    for t in range(2):
                        taken(dve, ("rg", d, k, t))
            for d in range(2):
                v.scalar_tensor_tensor(RI[:, d, 1], RI[:, d, 1], 1.0, XC[:, :, SEG_C:SEG_C + RUN], ALU.add, ALU.mult)
            dve.wait_ge(s["rg_a"], 1)
            for d in range(2):
                last = v.tensor_tensor(RI[:, d, 0], RA[:, d], RA[:, d], ALU.mult)
            link(last)
            for d in range(2):
                last = v.scalar_tensor_tensor(RB[:, d], RI[:, d, 0], 1.0, RB[:, d], ALU.add, ALU.mult)
            last.then_inc(s["rg_b2"], 1)
            dve.wait_ge(s["gelu_t"], 1)
            link(v.scalar_tensor_tensor(gx, HQ[:, :], 1.0, gx, ALU.add, ALU.mult))
            dve.wait_ge(s["rg_b"], 1)
            for d in range(2):
                last = v.scalar_tensor_tensor(RB[:, d], RI[:, d, 1], 0.5, RB[:, d], ALU.mult, ALU.mult)
            link(last)
            for t in range(2):
                for d in range(2):
                    out = RI[:, d, 0, t, :]
                    st = col("rst", 2 * d + t)
                    fw = slice(None, None, 1 if d == 0 else -1)
                    v.tensor_tensor_scan(out[:, 0:CTX][:, fw], RA[:, d, t, 0:CTX][:, fw], RB[:, d, t, 0:CTX][:, fw],
                                         0.0, ALU.mult, ALU.add)
                    last = v.tensor_tensor_scan(out[:, LATO:RUN][:, fw], RA[:, d, t, LATO:RUN][:, fw],
                                                RB[:, d, t, LATO:RUN][:, fw], st, ALU.mult, ALU.add)
            link(last)
            v.tensor_copy(RGO[:, 0:2], RI[:, 0, 0, :, CTX - 1])
            link(v.tensor_copy(RGO[:, 2:4], RI[:, 1, 0, :, 0]))
            link(v.tensor_tensor(RI[:, 0, 0], RI[:, 0, 0], RI[:, 1, 0], ALU.add))
            take(dve, ("in", 6, NT - 1))
            for a0, a1, b0 in ((0, CTX, 0), (CTX, TOK, LATO)):
                last = v.scalar_tensor_tensor(hT[:, 2:4, a0:a1], RI[:, 0, 0, :, b0:b0 + a1 - a0], 0.5,
                                              RGG[:, :, a0:a1], ALU.mult, ALU.mult)
            last.then_inc(s["rgo"], 1)

            for n in range(2):
                for u in range(3):
                    o = take(dve, ("V", n, u))
                    m1, m2 = M1[:, u % 2], M2[:, u % 2]
                    if n == 1 and u == 0:
                        dve.wait_ge(filled[uses[("y", 0, 1)] % 8], uses[("y", 0, 1)] // 8 + 1)
                    re, im = HF[:, u, 0, n, :], HF[:, u, 1, n, :]
                    v.tensor_tensor(m1.rearrange("p (r c) -> p r c", r=2), o[:, :].rearrange("p (r c) -> p r c", r=2),
                                    re.unsqueeze(1).to_broadcast([P, 2, HYC]), ALU.mult)
                    last = v.tensor_tensor(m2.rearrange("p (r c) -> p r c", r=2),
                                           o[:, :].rearrange("p (r c) -> p r c", r=2),
                                           im.unsqueeze(1).to_broadcast([P, 2, HYC]), ALU.mult)
                    link(last)
                    if u < 2:
                        ny = HNY[0:1, u, n, :]
                        v.tensor_tensor(m1[0:1, HYC:], o[0:1, HYC:], ny, ALU.mult)
                        link(v.memset(m2[0:1, :], 0.0))
                    v.tensor_tensor(Y[:, u, 0, :], m1[:, 0:HYC], m2[:, HYC:], ALU.subtract)
                    give(v.tensor_tensor(Y[:, u, 1, :], m1[:, HYC:], m2[:, 0:HYC], ALU.add), ("V", n, u))
                for t in range(2):
                    o = take(dve, ("y", n, t))
                    for a0, a1, b0 in ((0, CTX, SEG_C), (CTX, TOK, SEG_L)):
                        z0 = U[:, t, b0:b0 + a1 - a0] if n == 0 else ZT[:, t, a0:a1]
                        last = v.scalar_tensor_tensor(M1.rearrange("p i n -> p (i n)")[:, t * TOK + a0:t * TOK + a1], z0,
                                                      col("hyd", 2 * n + t), o[:, a0:a1], ALU.mult, ALU.add)
                    give(last, ("y", n, t))
                    taken(dve, ("y", n, t))
                dst = ZT if n == 0 else hT[:, 0:2, :]
                for a0, a1, b0 in ((0, CTX, SEG_C), (CTX, TOK, SEG_L)):
                    last = v.tensor_tensor(dst[:, :, a0:a1], M1.rearrange("p i n -> p (i n)")[:, 0:2 * TOK].rearrange(
                        "p (t n) -> p t n", t=2)[:, :, a0:a1], U[:, 2 + 2 * n:4 + 2 * n, b0:b0 + a1 - a0], ALU.mult)
                last.then_inc(s["z1" if n == 0 else "hy_done"], 1)

            dve.wait_ge(s["hy_done"], 1)
            for i in range(4):
                o = take(dve, ("rope", i))
                give(v.tensor_tensor(PX[:, i, :], o[:, 0:LAT], C("sin"), ALU.mult), ("rope", i))
            for i in range(4):
                taken(dve, ("rope", i))
            lat = PR[:, :, CTX:TOK]
            link(v.tensor_tensor(lat, lat, C("cos").unsqueeze(1).to_broadcast([P, 4, LAT]), ALU.mult))
            v.tensor_tensor(lat, lat, PX, ALU.add).then_inc(s["rope"], 1)
            dve.wait_ge(s["rope"], 1)
            dve.wait_ge(s["ei"], 1)
            for d in range(2):
                last = v.tensor_tensor(TAIL[:, d], TAIL[:, d], PR[:, 2:4, 0:CTX], ALU.mult)
            last.then_inc(s["rtail"], 1)
            for d in range(2):
                last = v.tensor_tensor(QD[:, d], EI[:, d], PR[:, 0:2, CTX:TOK], ALU.mult)
            last.then_inc(s["qd"], 1)
            dve.wait_ge(s["dec"], 1)
            last = v.tensor_tensor(DEC[:, :, 0, :], DEC[:, :, 0, :], C("mask_f").unsqueeze(1).to_broadcast([P, 4, P]),
                                   ALU.mult)
            link(v.tensor_tensor(DTMP, DTMP, C("mask_b").unsqueeze(1).to_broadcast([P, 4, P]), ALU.mult))
            link(v.tensor_tensor(DEC[:, :, 0, :], DEC[:, :, 0, :], DTMP, ALU.add))
            link(v.tensor_copy(DEC[:, :, 3, :], DEC[:, :, 0, :]))
            for par in range(2):
                o = take(dve, ("rsc", par))
                give(v.tensor_tensor(WC[:, par], o[:, 0:2 * P].rearrange("p (h q) -> p h q", h=2),
                                     DEC[:, par:4:2, 0, :], ALU.mult), ("rsc", par))
            for h in range(4):
                o = take(dve, ("rsl", h))
                give(v.tensor_tensor(WL[:, h, :], o[:, :], DEC[:, h].rearrange("p k q -> p (k q)"), ALU.mult),
                     ("rsl", h))
            o = take(dve, "rU")
            oo = o[:, :].rearrange("p (d t n) -> p d t n", d=2, t=2)
            for d in range(2):
                for r, src, dst in diagonals(oo[:, d], STO[:, 2 + d]):
                    last = v.tensor_copy(dst, src)
            give(last, "rU")
            head_norm("ro", RO, RO2, RGATE, TMR[:, :, HYC:2 * HYC], None)

            dve.wait_ge(s["res_in"], 32)
            dve.wait_ge(s["state_out"], 48)
            for n in range(2):
                for j in range(NT):
                    o = take(dve, ("out", n, j))
                    c = slice(n * CW, n * CW + CW)
                    g1 = G1[:, min(j, 1), c]
                    give(v.tensor_tensor(h2tok[j][:, c], o[:, :], g1, ALU.mult), ("out", n, j))
                    taken(dve, ("out", n, j))
                    last = v.tensor_tensor(XR[:, j, c], XR[:, j, c], h2tok[j][:, c], ALU.add)
            last.then_inc(s["x1"], 1)

            def norm(name, outs, gain):
                dve.wait_ge(s[name + "_sq"], 1)
                v.tensor_scalar(stat[:, 0, 0:NT], stat[:, 2, 0:NT], 1.0 / D, EPS, ALU.mult, ALU.add
                                ).then_inc(s[name + "_var"], 1)
                dve.wait_ge(s[name + "_rstd"], 1)
                for j in range(NT):
                    if gain is None:
                        last = v.tensor_scalar(outs[j], XR[:, j, :], stat[:, 1, j:j + 1], None, ALU.mult)
                    else:
                        last = v.scalar_tensor_tensor(outs[j], XR[:, j, :], stat[:, 1, j:j + 1], gain, ALU.mult, ALU.mult)
                last.then_inc(s[name + "_ready"], 1)

            link(v.scalar_tensor_tensor(AB[:, 1], MC[:, 3], 1.0,
                                        VC[:, VROWS["norm2"]:VROWS["norm2"] + KT].unsqueeze(2).to_broadcast([P, KT, 2]),
                                        ALU.add, ALU.mult))
            norm("n2", [h2tok[j][:, :] for j in range(NT)], None)
            modulate("x2T", 1, range(0, KT, 2))

            R = [RT[:, i] for i in range(12)]
            o = take(dve, "logits")
            mx = stat[:, 0, 0:NT]
            lg = o[:, 0:NT * E].rearrange("p (j e) -> p j e", j=NT)

            def over(a, n):
                return a.unsqueeze(2).to_broadcast([P, a.shape[1], n])
            link(v.tensor_reduce(mx, lg, AX.X, ALU.max))
            give(v.tensor_tensor(R[0], lg, over(mx, E), ALU.subtract), "logits")
            dve.wait_ge(s["logits_exp"], 1)
            link(v.tensor_reduce(mx, R[0], AX.X, ALU.add))
            link(v.reciprocal(mx, mx))
            link(v.tensor_tensor(R[0], R[0], over(mx, E), ALU.mult))
            link(v.tensor_tensor(R[1], R[0], rbias[:, :].unsqueeze(1).to_broadcast([P, NT, E]), ALU.add))
            sg = R[1].rearrange("p j (g i) -> p (j g) i", g=NG)
            for a0, b0, c0, w_ in ((0, 1, 0, 3), (0, 2, 3, 2), (0, 3, 5, 1)):
                last = v.tensor_tensor(PS[:, :, c0:c0 + w_], sg[:, :, a0:a0 + w_], sg[:, :, b0:b0 + w_], ALU.add)
            link(last)
            gs, gk, gm = GR[:, 0, :], GR[:, 1, :], stat[:, 1, 0:NT]
            link(v.tensor_reduce(gs, PS[:, :, :], AX.X, ALU.max))
            g3 = gs.rearrange("p (j g) -> p j g", j=NT)
            k3 = gk.rearrange("p (j g) -> p j g", j=NT)

            def first_highest(out, key, x, m, order_row, n):
                link(v.tensor_reduce(m, x, AX.X, ALU.max))
                link(v.tensor_tensor(key, x, over(m, n), ALU.is_equal))
                link(v.tensor_tensor(key, key, order_row.unsqueeze(1).to_broadcast([P, NT, n]), ALU.mult))
                link(v.tensor_reduce(m, key, AX.X, ALU.max))
                link(v.tensor_tensor(out, key, over(m, n), ALU.is_equal))

            first_highest(GR[:, 2, :].rearrange("p (j g) -> p j g", j=NT), k3, g3, gm, C("w4"), NG)
            oh = GR[:, 2, :]
            link(v.tensor_scalar(gs, oh, 1e30, -1e30, ALU.mult, ALU.add))
            m16 = R[2].rearrange("p j (g i) -> p (j g) i", g=NG)
            link(v.tensor_tensor(m16, sg, over(oh, 4), ALU.mult))
            link(v.tensor_tensor(m16, m16, over(gs, 4), ALU.add))
            first_highest(R[3], R[5], R[2], gm, C("w16"), E)
            link(v.scalar_tensor_tensor(R[2], R[3], -3e30, R[2], ALU.mult, ALU.add))
            first_highest(R[4], R[5], R[2], gm, C("w16"), E)
            v.tensor_tensor(R[6], R[3], R[4], ALU.add).then_inc(s["route"], 1)
            v.tensor_tensor(R[8], R[0], R[3], ALU.mult)
            link(v.tensor_tensor(R[9], R[0], R[4], ALU.mult))
            v.tensor_reduce(gw[:, :, 0], R[8], AX.X, ALU.add)
            link(v.tensor_reduce(gw[:, :, 1], R[9], AX.X, ALU.add))
            link(v.tensor_reduce(gm, gw[:, :, :], AX.X, ALU.add))
            link(v.reciprocal(gm, gm))
            link(v.tensor_tensor(gw[:, :, :], gw[:, :, :], over(gm, 2), ALU.mult))
            o = take(dve, "places")
            link(v.tensor_copy(R[7], o[:, 0:NT * E].rearrange("p (j e) -> p j e", j=NT)))
            cnt, more, upto, base, shift = (OV[:, i, :] for i in range(5))
            give(v.tensor_copy(cnt, o[:, NT * E:NT * E + E]), "places")
            taken(dve, "places")
            link(v.scalar_tensor_tensor(R[10], R[7], 1.0, R[6], ALU.add, ALU.mult))
            link(v.tensor_scalar(R[10], R[10], -1.0, None, ALU.add))
            v.tensor_copy(tokid16[:, :], C("tokid"))
            dve.wait_ge(s["n2_sq"], 1)
            for j in range(NT):
                if j > 0:
                    dve.wait_ge(s["sel_used"], j)
                v.tensor_tensor(SEL[:, :, :], C("count")[:, 0:P].unsqueeze(1).to_broadcast([P, E, P]),
                                R[10][:, j, :].unsqueeze(2).to_broadcast([P, E, P]), ALU.is_equal).then_inc(s["sel"], 1)
            v.tensor_scalar(more, cnt, float(P), None, ALU.is_gt)
            link(v.tensor_scalar(base, cnt, 2.0 * P, None, ALU.is_gt))
            link(v.tensor_tensor(more, more, base, ALU.add))
            link(v.tensor_tensor_scan(upto, C("ones")[:, 0:E], more, 0.0, ALU.mult, ALU.add))
            link(v.tensor_tensor(base, upto, more, ALU.subtract))
            link(v.tensor_scalar(shift, base, float(P), (E - 1.0) * P, ALU.mult, ALU.add))
            link(v.tensor_tensor(shift, shift, C("erow"), ALU.subtract))
            link(v.tensor_scalar(R[8], R[7], float(P), None, ALU.is_ge))
            link(v.tensor_tensor(R[8], R[8], shift.unsqueeze(1).to_broadcast([P, NT, E]), ALU.mult))
            link(v.tensor_tensor(R[8], R[8], R[7], ALU.add))
            link(v.tensor_tensor(R[8], R[8], C("erow").unsqueeze(1).to_broadcast([P, NT, E]), ALU.add))
            for k in range(2):
                link(v.tensor_tensor(R[9], R[8], R[3 + k], ALU.mult))
                link(v.tensor_reduce(GR[:, 0, k * NT:k * NT + NT], R[9], AX.X, ALU.add))
                link(v.tensor_copy(rows[:, :, k], GR[:, 0, k * NT:k * NT + NT]))
            for o in range(OVER):
                link(v.tensor_scalar(OV[:, 5, :], upto, float(o), None, ALU.is_gt))
                link(v.tensor_scalar(OV[:, 6, :], base, float(o), None, ALU.is_le))
                link(v.tensor_tensor(OV[:, 5, :], OV[:, 5, :], OV[:, 6, :], ALU.mult))
                link(v.tensor_tensor(OV[:, 5, :], OV[:, 5, :], C("count")[:, 0:E], ALU.mult))
                link(v.tensor_reduce(OV[:, 7, o:o + 1], OV[:, 5, :], AX.X, ALU.add))
            v.tensor_copy(further_passes[0:1, 1:1 + OVER], OV[0:1, 7, 0:OVER])
            v.tensor_copy(further_passes[0:1, 0:1], upto[0:1, E - 1:E]).then_inc(s["route2"], 1)
            o = take(dve, "lst")
            give(v.tensor_copy(lst[:, 0:E], o[:, 0:E]), "lst")

            def experts(it, first):
                for p in range(2):
                    n = 2 * it + p
                    dve.wait_ge(s["g_exp"], n + 1)
                    v.tensor_scalar(he[:, p, :], he[:, p, :], 1.0, None, ALU.add).then_inc(s["h1"], 1)
                    dve.wait_ge(s["h1"], n + 1)
                    v.reciprocal(he[:, p, :], he[:, p, :]).then_inc(s["h2"], 1)
                    dve.wait_ge(s["h2"], n + 1)
                    v.tensor_tensor(he[:, p, :], he[:, p, :], psum[:, 2, :], ALU.mult).then_inc(s["h3"], 1)
                    dve.wait_ge(s["h3"], n + 1)
                    dve.wait_ge(s["up_done"], n + 1)
                    v.tensor_tensor(he[:, p, :], he[:, p, :], psum[:, 3, :], ALU.mult).then_inc(s["h_ready"], 1)
                    dve.wait_ge(s["ht_filled"], n + 1)
                    if not (first and p == 0):
                        dve.wait_ge(s["down_done"], n)
                    v.tensor_copy(heT[:, :, :].rearrange("p q n -> p (q n)"), psum[:, 4, :]).then_inc(s["ht_ready"], 1)
                    dve.wait_ge(s["down_done"], n + 1)
                    if not first:
                        dve.wait_ge(s[f"y_out{p}"], 16 * it)
                    v.tensor_copy(ye[p][:, 512:1024], psum[:, 6, :]).then_inc(s["yb"], 1)

            experts(0, True)
            with dve.Fori(1, E // 2) as it:
                experts(it, False)
            with dve.If(further(dve) > 0):
                link_further = steps(dve, "o_step")
                dve.wait_ge(s["up_done"], E)
                for o in range(OVER):
                    if o > 0:
                        dve.wait_ge(s["o_selm"], o)
                    for i in range(2 * NT):
                        link_further(v.tensor_scalar(OV[:, 7, i:i + 1], GR[:, 0, i:i + 1], -1.0 * (E + o) * P, None, ALU.add))
                        last = v.tensor_scalar(SO[:, i, :], C("count")[:, 0:P], OV[:, 7, i:i + 1], None, ALU.is_equal)
                    last.then_inc(s["o_sel"], 1)
                    dve.wait_ge(s["o_selm"], o + 1)
                    v.tensor_copy(lsto[:, o:o + 1], psum[:, 7, 0:1]).then_inc(s["o_lst"], 1)
                dve.wait_ge(s["y_out0"], 16 * E // 2)
                with dve.Fori(0, OVER) as o:
                    dve.wait_ge(s["o_exp"], o + 1)
                    v.tensor_scalar(he[:, 0, :], he[:, 0, :], 1.0, None, ALU.add).then_inc(s["o_h1"], 1)
                    dve.wait_ge(s["o_h1"], o + 1)
                    v.reciprocal(he[:, 0, :], he[:, 0, :]).then_inc(s["o_h2"], 1)
                    dve.wait_ge(s["o_h2"], o + 1)
                    v.tensor_tensor(he[:, 0, :], he[:, 0, :], psum[:, 2, :], ALU.mult).then_inc(s["o_h3"], 1)
                    dve.wait_ge(s["o_h3"], o + 1)
                    v.tensor_tensor(he[:, 0, :], he[:, 0, :], psum[:, 3, :], ALU.mult).then_inc(s["o_h"], 1)
                    dve.wait_ge(s["o_ht"], o + 1)
                    v.tensor_copy(heT[:, :, :].rearrange("p q n -> p (q n)"), psum[:, 4, :]).then_inc(s["o_htr"], 1)
                    dve.wait_ge(s["o_down"], o + 1)
                    v.tensor_copy(ye[0][:, :], psum[:, 5:7, :].rearrange("p b n -> p (b n)")).then_inc(s["o_y"], 1)
            dve.wait_ge(s["fin_in"], 16 * 2 * NT)
            for j in range(NT):
                link(v.tensor_scalar(YG[0][:, j, :], YG[0][:, j, :], gw[:, j, 0:1], None, ALU.mult))
                link(v.scalar_tensor_tensor(YG[0][:, j, :], YG[1][:, j, :], gw[:, j, 1:2], YG[0][:, j, :],
                                            ALU.mult, ALU.add))
                link(v.tensor_tensor(YG[0][:, j, :], YG[0][:, j, :], G2[:, min(j, 1), :], ALU.mult))
                last = v.tensor_tensor(XR[:, j, :], XR[:, j, :], YG[0][:, j, :], ALU.add)
            last.then_inc(s["x2"], 1)
            dve.wait_ge(s["nf_in"], 16)
            norm("fin", [XR[:, j, :] for j in range(NT)], NF)


N_VEC = 17
N_FILT = 7
TURN_HI = 6.28125
TURN_LO = 2 * math.pi - 6.28125
PI_DOWN = 3.1415925


def kernel(**inputs):
    import concourse.bacc as bacc
    from concourse.bass_utils import run_bass_kernel_spmd as run

    nc = bacc.Bacc("TRN2", target_bir_lowering=False, num_devices=1)
    big, cols, z, win, masks = shape_constants()
    arrays, A, O = {}, {}, {}
    skip = ("hg_lb",)
    for name, a in list(inputs.items()) + [("const", big), ("z_table", z), ("window", win), ("masks", masks)]:
        if name in skip:
            continue
        a = np.ascontiguousarray(a)
        arrays[f"in_{name}"] = a
        A[name] = nc.dram_tensor(f"in_{name}", a.shape, mybir.dt.from_np(a.dtype), kind="ExternalInput").ap()
    outs = (("y_prompt", (1, CTX, D)), ("y_sample", (1, LAT, D)), ("new_state_rglru", (1, 1, 2, HYC)),
            ("new_state_hgrn", (1, 1, 2, 4, 64, 64)), ("new_state_ret", (1, 1, 2, 4, 64, 64)))
    for name, shape in outs:
        O[name] = nc.dram_tensor(f"out_{name}", shape, F32, kind="ExternalOutput").ap()
    A["h2_rows"] = nc.dram_tensor("h2_rows", (TOK, D), F32, kind="Internal").ap()
    A["y_rows"] = nc.dram_tensor("y_rows", ((E + OVER) * P, D), F32, kind="Internal").ap()
    backbone_step(nc, cols, A, O)
    r = run(nc, [arrays], core_ids=[0])
    return tuple(r.results[0][f"out_{name}"] for name, _ in outs)
```

```python
import math
from contextlib import ExitStack

import numpy as np

import concourse.bass as bass
from concourse import mybir

ALU = mybir.AluOpType
ACT = mybir.ActivationFunctionType
AX = mybir.AxisListType
F32 = mybir.dt.float32
I32 = mybir.dt.int32
U8 = mybir.dt.uint8
F16 = mybir.dt.float16

P = 128
D = 1024
KT = D // P
CTX, LAT = 128, 256
TOK = CTX + LAT
NT = TOK // P
NMOD = 6
CW = 512
ADA_CHUNKS = NMOD * D // CW
E, FE, NG = 16, 512, 4
ROWS = 96
PACK = CW - P
OVER = 2 * TOK // (ROWS + 1)
EPS = 1e-6
GRID_W, DH = 64, 64
HY_EMB, HY_FFN = 33, 64
HYC = 256
SEG_C, SEG_L = 2, 133
PADW = 390
RUN = PADW - 3
LATO = SEG_L - SEG_C
MAGIC = 12582912.0
LEVELS = (64, 32, 16, 8, 4, 2, 1)
NLEV = len(LEVELS) + 1

VROWS = {}
_n = 0
for _name, _rows in (("c", 16), ("norm1", 8), ("norm2", 8), ("hcw", 18), ("hcb", 6), ("rcw", 8), ("rcb", 2),
                     ("rba", 4), ("rbx", 4), ("lam", 4), ("hyd", 4), ("rst", 4)):
    VROWS[_name] = _n
    _n += _rows
NV = _n


def shape_constants():
    cols, parts = {}, []
    at = 0

    def put(name, a):
        nonlocal at
        full = np.zeros((P, a.shape[1]), np.float64)
        full[:a.shape[0]] = a
        cols[name] = (at, a.shape[1])
        parts.append(full)
        at += a.shape[1]

    p = np.arange(P)
    put("ident", np.eye(P))
    put("sel12", np.repeat(np.eye(ADA_CHUNKS), 2, axis=1))
    pick = np.zeros((P, 2))
    pick[0::32, 0] = pick[1::32, 1] = 1.0
    put("pick", pick)
    swap = np.zeros((P, P))
    for i in range(0, P, 2):
        swap[i + 1, i] = -1.0
        swap[i, i + 1] = 1.0
    put("swap", swap)
    put("triu", (p[:, None] < p[None]).astype(float))
    put("ones", np.ones((P, P)))

    def dft(L):
        t, f = np.arange(L)[:, None], np.arange(L)[None]
        re = np.cos(np.pi * f * t / L)
        im = -np.sin(np.pi * f * t / L)
        im[:, 0] = np.cos(np.pi * t[:, 0])
        w = np.full((1, L), 1.0 / L)
        w[0, 0] = 0.5 / L
        return re, im, (re * w).T, (im * w).T
    re, im, ire, iim = dft(CTX)
    put("dft_ctx", np.concatenate([re, im], 1))
    put("idft_ctx", np.concatenate([ire, iim], 1))
    re, im, ire, iim = dft(LAT)
    put("dft_lat", np.concatenate([np.concatenate([re[tt * P:tt * P + P, u * P:u * P + P],
                                                   im[tt * P:tt * P + P, u * P:u * P + P]], 1)
                                   for tt in range(2) for u in range(2)], 1))
    put("idft_lat", np.concatenate([np.concatenate([ire[u * P:u * P + P], iim[u * P:u * P + P]], 1)
                                    for u in range(2)], 1))
    put("alt", np.cos(np.pi * p)[:, None])
    t = np.arange(LAT)
    nf = DH // 4
    inv = 10000.0 ** (-np.arange(nf) / nf)
    ang = np.concatenate([(t // GRID_W)[:, None] * inv, (t % GRID_W)[:, None] * inv], 1)
    half = (p % DH) // 2
    put("cos", np.cos(ang[:, half]).T)
    put("sin", np.sin(ang[:, half]).T)
    s, q = p[:, None], p[None]
    put("dist_f", np.maximum(q - s, 0))
    put("dist_b", np.maximum(s - q, 0))
    put("dist_up", P + q - s)
    put("dist_lo", P + s - q)
    put("mask_f", (q >= s).astype(float))
    put("mask_b", (s >= q).astype(float))
    put("count", np.tile(np.arange(257)[None], (P, 1)))
    put("tokid", np.stack([p + P * j for j in range(NT)], 1))
    put("w4", np.tile(np.array([[4, 3, 2, 1.0]]), (P, 1)))
    put("w16", np.tile(np.arange(16, 0, -1)[None], (P, 1)))
    put("erow", np.tile((np.arange(16) * ROWS)[None], (P, 1)))
    put("selc", np.repeat(pick, P, axis=1))
    reset = np.ones((P, TOK))
    reset[:, ::P] = 0.0
    put("reset", reset)
    big = np.concatenate(parts, 1).astype(np.float32)

    zs, wins = [], []
    deltas = np.abs(np.linspace(np.log(1e-2) / 1.5, np.log(1e-2) / 0.3, HYC))
    for L in (CTX, LAT):
        tl = np.arange(L, dtype=np.float64)
        tn = tl / (L - 1)
        a = (2 * np.pi / L) * tl[:, None] * np.linspace(1e-4, (HY_EMB - 1) // 2 - 1, (HY_EMB - 1) // 2)[None]
        zs.append(np.concatenate([tn[:, None], np.cos(a), np.sin(a)], 1))
        wins.append(np.exp(-tn[:, None] * deltas[None]))
    z = np.concatenate(zs, 0).T
    win = np.concatenate(wins, 0).reshape(NT, P, HYC).transpose(1, 0, 2).reshape(P, NT * HYC)
    masks = np.zeros((P, NLEV, 2, P), np.float32)
    for n, h in enumerate(LEVELS):
        same = (s // (2 * h)) == (q // (2 * h))
        masks[:, n, 0] = same & (s % (2 * h) < h) & (q % (2 * h) >= h)
        masks[:, n, 1] = same & (s % (2 * h) >= h) & (q % (2 * h) < h)
    masks[:, NLEV - 1, :] = np.eye(P)[:, None]
    return big, cols, z.astype(np.float32), win.astype(np.float32), masks.reshape(P, -1)


def backbone_step(nc, cols, A, O):
    PRE = ([("ada", n) for n in range(4)] + [("in", n) for n in (2, 3, 4, 0, 1, 5, 6)] +
           [("ada", n) for n in range(4, 10)] + [("out", 0), ("out", 1), ("ada", 10), ("ada", 11)])
    NS = 3
    assert len(PRE) % NS == 0
    PRE_USES = len(PRE) // NS
    order = {key: i for i, key in enumerate(PRE)}

    ctx = ExitStack()
    with ctx:
        def sem(name):
            return ctx.enter_context(nc.semaphore(name))

        def alloc(stack, name, shape, dt=F32):
            return stack.enter_context(nc.sbuf_tensor(name, shape, dt))

        def sb(name, shape, dt=F32):
            return alloc(ctx, name, shape, dt)

        slot = [sb(f"slot{i}", [P, KT, CW]) for i in range(NS)]
        hT = sb("hT", [P, KT, TOK])
        XS = sb("XS", [P, 8 * PADW])
        NCONST = sum(w for _, w in cols.values())
        FIRST = cols["pick"][0] + cols["pick"][1]
        const = sb("const", [P, NCONST])
        mask = sb("mask", [P, NLEV, 2, P], U8)
        G1 = sb("G1", [P, 2, D])
        VR = sb("VR", [P, P])
        VC = sb("VC", [P, NV])
        SC16 = sb("SC16", [P, 16])
        sptmp = sb("sptmp", [P, 6, 16])
        modrow = sb("modrow", [P, 2, CW])
        bada = sb("bada", [ADA_CHUNKS, CW])
        MC = sb("MC", [P, 4, KT, 2])
        AB = sb("AB", [P, 2, KT, 2])
        siluc = sb("siluc", [P, KT, 32])
        sige = sb("sige", [P, 16])
        stat = sb("stat", [P, 4, 16])
        mhalf = sb("mhalf", [P, 16])
        wr = sb("wr", [P, KT, E])
        rbias = sb("rbias", [P, E])
        hgn = sb("hgn", [P, HYC])
        halfb = sb("halfb", [P, 8])
        tokid16 = sb("tokid16", [P, NT], F16)
        lamc = sb("lamc", [P, 4])

        def C(name):
            a, w = cols[name]
            return const[:, a:a + w]
        ident = C("ident")

        def col(name, i=0):
            r = VROWS[name] + i
            return VC[:, r:r + 1]

        x_in = XS[:, 0:NT * D].rearrange("p (j d) -> p j d", j=NT)
        CU = XS[:, :].rearrange("p (i w) -> p i w", i=8)
        BD = XS[:, 0:1024].rearrange("p (d k t n) -> p d k t n", d=2, k=2, t=2)
        SC = XS[:, 0:3072].rearrange("p (d r b t q) -> p d r b t q", d=2, r=2, b=NT, t=2)

        mix = ExitStack()

        def mb(name, shape, dt=F32):
            return alloc(mix, name, shape, dt)
        U = mb("U", [P, 6, PADW])
        XC = mb("XC", [P, 2, PADW])
        RGG = mb("RGG", [P, 2, TOK])
        HQ = mb("HQ", [P, 2 * TOK])
        HX = mb("HX", [P, 2, 2 * TOK])
        HK = mb("HK", [P, 2, 2 * TOK])
        HTOT = mb("HTOT", [P, 2, 6])
        TMH = mb("TMH", [P, NT, 2 * HYC])
        HF = mb("HF", [P, 3, 2, 2, HYC])
        HNY = mb("HNY", [1, 2, 2, HYC])
        HGS = mb("HGS", [P, 2, 2, 2, P])
        STO = mb("STO", [P, 4, 2, 64])
        RGO = mb("RGO", [P, 4])
        PR = HX[:, :, :].rearrange("p d (t n) -> p (d t) n", t=2)
        TMR = HK[:, :, :].rearrange("p d n -> p (d n)").rearrange("p (j n) -> p j n", j=NT)
        T = mb("T", [P, 7040])

        def t_at(a, n):
            return T[:, a:a + n]
        w1 = U[:, 0, 0:64]
        w2 = U[:, 0, 64:128]
        b12 = U[:, 0, 128:130]
        z_t = U[:, 1, 0:TOK]
        fu = [U[:, 2 + i, 0:TOK] for i in range(3)]
        w3 = TMH[:, :, :].rearrange("p j n -> p (j n)")[:, 0:1024]
        win = HQ[:, :].rearrange("p (j n) -> p j n", j=NT)
        FSQ = [v[:, :, :].rearrange("p d n -> p (d n)").rearrange("p (j n) -> p j n", j=NT) for v in (HX, HK)]
        FH = t_at(0, 3072).rearrange("p (j o d c) -> p j o d c", j=NT, o=2, d=2)
        FS = t_at(3072, 1536).rearrange("p (j n) -> p j n", j=NT)
        FD = t_at(4608, 1536).rearrange("p (j n) -> p j n", j=NT)
        FRS = G1[:, 0, :].rearrange("p (g n) -> p g n", g=2)
        LF = t_at(0, 1536).rearrange("p (d n) -> p d n", d=2)
        W = t_at(1536, 1536).rearrange("p (d n) -> p d n", d=2)
        QL = t_at(3072, 1536).rearrange("p (d n) -> p d n", d=2)
        KL = t_at(4608, 1536).rearrange("p (d n) -> p d n", d=2)
        KTOK = t_at(1536, 1024).rearrange("p (d i t n) -> p d i t n", d=2, i=2, t=2)
        HO = t_at(0, 768).rearrange("p (j n) -> p j n", j=NT)
        HO2 = t_at(768, 768).rearrange("p (j n) -> p j n", j=NT)
        HGATE = t_at(4608, 768).rearrange("p (j n) -> p j n", j=NT)
        RI = t_at(0, 8 * RUN).rearrange("p (d k t n) -> p d k t n", d=2, k=2, t=2)
        RA = t_at(8 * RUN, 4 * RUN).rearrange("p (d t n) -> p d t n", d=2, t=2)
        RB = t_at(12 * RUN, 4 * RUN).rearrange("p (d t n) -> p d t n", d=2, t=2)
        VT = t_at(6192, 768).rearrange("p (j c) -> p j c", j=NT)
        Y = t_at(0, 1536).rearrange("p (u r c) -> p u r c", u=3, r=2)
        M1 = t_at(1536, 1024).rearrange("p (i n) -> p i n", i=2)
        M2 = t_at(2560, 1024).rearrange("p (i n) -> p i n", i=2)
        ZT = t_at(3584, 768).rearrange("p (t n) -> p t n", t=2)
        DEC = t_at(0, 2048).rearrange("p (h k q) -> p h k q", h=4, k=4)
        WL = t_at(2048, 2048).rearrange("p (h n) -> p h n", h=4)
        WC = t_at(4096, 512).rearrange("p (r h n) -> p r h n", r=2, h=2)
        TAIL = t_at(4608, 512).rearrange("p (d t n) -> p d t n", d=2, t=2)
        RKT = t_at(5120, 512).rearrange("p (d t n) -> p d t n", d=2, t=2)
        RS = t_at(5632, 512).rearrange("p (d t n) -> p d t n", d=2, t=2)
        DTMP = t_at(6144, 512).rearrange("p (h q) -> p h q", h=4)
        hf = HF[:, :, :, :, :].rearrange("p u r o c -> p (u r o c)")
        mask_in = hf[:, 0:NLEV * 2 * P]
        EI = hf[:, 0:1024].rearrange("p (d t n) -> p d t n", d=2, t=2)
        QD = hf[:, 1024:2048].rearrange("p (d t n) -> p d t n", d=2, t=2)
        PX = hf[:, 2048:3072].rearrange("p (i n) -> p i n", i=4)
        uf = U[:, :, :].rearrange("p i n -> p (i n)")
        RO = uf[:, 0:768].rearrange("p (j n) -> p j n", j=NT)
        RO2 = uf[:, 768:1536].rearrange("p (j n) -> p j n", j=NT)
        RGATE = uf[:, 1536:2304].rearrange("p (j n) -> p j n", j=NT)
        mix.close()

        moe = ExitStack()

        def eb(name, shape, dt=F32):
            return alloc(moe, name, shape, dt)
        slot += [eb(f"slot{i}", [P, KT, CW]) for i in range(NS, 2 * NS)]
        xe = [eb(f"xe{i}", [P, D]) for i in range(2)]
        xeTa = eb("xeTa", [P, 2, KT, ROWS])
        xeT = [xeTa[:, i] for i in range(2)]
        he = eb("he", [P, 2, FE])
        heT = eb("heT", [P, 3, P])
        ye = [eb(f"ye{i}", [P, D]) for i in range(2)]
        G2 = eb("G2", [P, 2, D])
        gw = eb("gw", [P, NT, 2])
        lst = eb("lst", [P, NT * E], I32)
        rows = eb("rows", [P, NT, 2], I32)
        further_passes = eb("further_passes", [1, 1 + OVER], I32)
        OV = eb("OV", [P, 8, E])
        lsto = eb("lsto", [P, OVER], I32)
        RT = eb("RT", [P, 12, NT, E])
        GR = eb("GR", [P, 3, NT * NG])
        PS = eb("PS", [P, NT * NG, 6])
        SEL = eb("SEL", [P, E, P], F16)
        h2tok = [xe[0], xe[1], ye[0]]
        YG = [slot[3 + k][:, :, :].rearrange("p k n -> p (k n)")[:, 0:NT * D].rearrange("p (j n) -> p j n", j=NT)
              for k in range(2)]
        SO = xeTa[:, 0].rearrange("p k n -> p (k n)")[:, 0:2 * NT * P].rearrange("p (i n) -> p i n", i=2 * NT)
        yp = [y[:, 0:2 * PACK].rearrange("p (h c) -> p h c", h=2) for y in ye]
        NF = he[:, :, :].rearrange("p a n -> p (a n)")
        moe.close()
        XR = x_in

        psum = ctx.enter_context(nc.psum_tensor("psum", [P, 8, 512], F32))
        filled = [sem(f"filled{b}") for b in range(8)]
        emptied = [sem(f"emptied{b}") for b in range(8)]
        loaded = [sem(f"loaded{i}") for i in range(2 * NS)]
        s = {name: sem(name) for name in (
            "first_in", "const_in", "mask_in", "mask_ready", "vec_in", "filt_in", "late_in", "x_in", "res_in", "nf_in",
            "siluc_exp", "siluc", "sp_in", "sp_abs", "sp_ready", "mod1",
            "x_sq", "x_var", "x_rstd", "xn_ready", "x1", "n2_sq", "n2_var", "n2_rstd", "n2_ready", "x2",
            "fin_sq", "fin_var", "fin_rstd", "fin_ready", "fin_out",
            "fu_arg", "fu_sin", "fsq_ready", "fs_ready", "frs_sqrt", "u_ready", "xc_ready", "pads", "z1", "hy_done",
            "hg_abs", "hg_exp", "hq_exp", "hg_tx", "hg_texp", "hg_qk", "kl_zero", "sc_zero", "lev_arg", "lev_exp",
            "lev_ready", "states0", "ho_gexp", "ho_var", "ho_rstd", "ho_ready",
            "gelu_arg", "gelu_t", "bd_ready", "rg_a", "rg_b2", "rg_b", "rgo",
            "ei", "qd", "dec", "rope", "rtail", "rs_ready", "ro_gexp", "ro_var", "ro_rstd", "ro_ready", "state_out",
            "logits_exp", "route", "sel", "sel_used", "passes_known", "h2_out", "y_zero",
            "xe0", "xe1", "xt_filled", "xt_ready", "gate_done", "up_done", "g_exp", "h1", "h2", "h3", "h_ready",
            "ht_filled", "ht_ready", "down_done", "ya", "yb", "y_out0", "y_out1", "fin_in0", "fin_in1", "fin_in2", "fin_w",
            "o_sel", "o_selm", "o_step", "o_lst", "o_xe", "o_xt", "o_xtr", "o_w", "o_up", "o_exp", "o_h1", "o_h2", "o_h3",
            "o_h", "o_ht", "o_htr", "o_down", "o_y", "o_out",
            "act_step", "dve_step", "pool_step")}
        block = ctx.enter_context(nc.Block())

        uses = {}

        def claim(eng, key):
            n = len(uses)
            uses[key] = n
            if n >= 8:
                eng.wait_ge(emptied[n % 8], n // 8)
            return psum[:, n % 8, :]

        def fill(ins, key):
            ins.then_inc(filled[uses[key] % 8], 1)

        def take(eng, key):
            n = uses[key]
            eng.wait_ge(filled[n % 8], n // 8 + 1)
            return psum[:, n % 8, :]

        def give(ins, key):
            ins.then_inc(emptied[uses[key] % 8], 1)

        def taken(eng, key):
            n = uses[key]
            eng.wait_ge(emptied[n % 8], n // 8 + 1)

        def chunk(eng, key):
            i = order[key]
            eng.wait_ge(loaded[i % NS], 16 * (i // NS + 1))
            return slot[i % NS]

        def further(eng):
            eng.wait_ge(s["passes_known"], 1)
            return eng.value_load(further_passes[0:1, 0:1], min_val=0, max_val=OVER)

        def tile(j):
            return slice(j * P, j * P + P)

        def seg(v, j0):
            return v[..., 0:CTX] if j0 == 0 else v[..., CTX:TOK]

        vec = (("c", A["c_ctx"].rearrange("(r n) -> r n", n=P)),
               ("c", A["c"].rearrange("b (r n) -> (b r) n", n=P)),
               ("norm1", A["norm1"].rearrange("b (r n) -> (b r) n", n=P)),
               ("norm2", A["norm2"].rearrange("b (r n) -> (b r) n", n=P)),
               ("hcw", A["hy_conv_w"].rearrange("b k (r n) -> (b k r) n", n=P)),
               ("hcb", A["hy_conv_b"].rearrange("b (r n) -> (b r) n", n=P)),
               ("rcw", A["rg_conv_w"].rearrange("b k (r n) -> (b k r) n", n=P)),
               ("rcb", A["rg_conv_b"].rearrange("b (r n) -> (b r) n", n=P)),
               ("rba", A["rg_ba"].rearrange("b d (r n) -> (b d r) n", n=P)),
               ("rbx", A["rg_bx"].rearrange("b d (r n) -> (b d r) n", n=P)),
               ("lam", A["rg_lambda"].rearrange("b d (r n) -> (b d r) n", n=P)),
               ("hyd", A["hy_d"].rearrange("b d (r n) -> (b d r) n", n=P)),
               ("rst", A["state_rglru"].rearrange("b l d (r n) -> (b l d r) n", n=P)))
        vec_loads = []
        for i, (name, src) in enumerate(vec):
            row = VROWS[name] + (vec[0][1].shape[0] if i == 1 else 0)
            vec_loads.append((VR[row:row + src.shape[0], :], src))
        vec_loads.append((bada[:, :], A["b_ada"].rearrange("b (r n) -> (b r) n", n=CW)))
        vec_loads.append((SC16[:, 4:12], A["ret_decay"].rearrange("b d h -> b (d h)").to_broadcast([P, 8])))
        for half in range(2):
            vec_loads.append((SC16[half * 64:half * 64 + 64, 12:16].rearrange("p (d t) -> p d t", d=2),
                              A["ret_decay"].rearrange("b d (t h) -> h b d t", h=2)[half].to_broadcast([64, 2, 2])))
        assert len(vec_loads) == N_VEC

        @block.tensor
        def _(pe):
            mm = nc.tensor.matmul
            tr = nc.tensor.transpose
            pe.wait_ge(s["first_in"], 16)
            pe.wait_ge(s["vec_in"], 16 * N_VEC)
            o = claim(pe, "vcols")
            fill(tr(o[:, 0:NV], VR[0:NV, :], ident[0:NV, 0:NV]), "vcols")

            def ada(n):
                w = chunk(pe, ("ada", n))
                if n == 0:
                    pe.wait_ge(s["siluc"], 1)
                o = claim(pe, ("ada", n))
                for kt in range(KT):
                    g = kt % 4
                    last = mm(o[32 * g:32 * g + 32, :], siluc[:, kt, :], w[:, kt, :], start=(kt < 4), stop=(kt >= 4),
                              tile_position=(0, 32 * g))
                fill(last, ("ada", n))

            def ada_post(n):
                taken(pe, ("ada", n))
                if n // 2 in (2, 5):
                    for c in range(2):
                        o = claim(pe, ("adag", n, c))
                        mm(o[:, :], C("selc")[:, tile(c)], modrow[:, n % 2, :], start=True, stop=False)
                        fill(mm(o[:, :], C("sel12")[0:ADA_CHUNKS, 2 * n:2 * n + 1].to_broadcast([ADA_CHUNKS, P]),
                                bada[:, :], start=False, stop=True), ("adag", n, c))
                else:
                    o = claim(pe, ("adac", n))
                    for q in range(4):
                        mm(o[:, 2 * q:2 * q + 2], modrow[:, n % 2, tile(q)], C("pick"), start=True, stop=False)
                        last = mm(o[:, 2 * q:2 * q + 2], bada[:, tile(q)], C("sel12")[0:ADA_CHUNKS, 2 * n:2 * n + 2],
                                  start=False, stop=True)
                    fill(last, ("adac", n))

            ada(0)
            pe.wait_ge(s["filt_in"], 16 * N_FILT)
            o = claim(pe, ("fu", 0))
            fill(mm(o[0:HY_FFN, 0:TOK], w1[0:HY_EMB, :], z_t[0:HY_EMB, :], start=True, stop=True), ("fu", 0))
            ada(1)
            ada_post(0)
            pe.wait_ge(s["fu_sin"], 1)
            o = claim(pe, ("fu", 1))
            fill(mm(o[0:HY_FFN, 0:TOK], w2[0:HY_FFN, :], fu[1][0:HY_FFN, :], start=True, stop=True), ("fu", 1))
            ada(2)
            ada_post(1)
            pe.wait_ge(s["fu_sin"], 2)
            for j in range(NT):
                for q in range(2):
                    o = claim(pe, ("fh", j, q))
                    fill(mm(o[:, :], fu[1][0:HY_FFN, tile(j)], w3[0:HY_FFN, q * 512:q * 512 + 512],
                            start=True, stop=True), ("fh", j, q))
            ada(3)
            ada_post(2)
            pe.wait_ge(s["const_in"], 16)
            pe.wait_ge(s["fsq_ready"], 1)
            for g, js in enumerate(((0,), (1, 2))):
                o = claim(pe, ("fss", g))
                for q in range(2):
                    for j in js:
                        for d in range(2):
                            last = mm(o[:, q * HYC:q * HYC + HYC], C("ones"), FSQ[q][:, j, d * HYC:d * HYC + HYC],
                                      start=(j == js[0] and d == 0), stop=(j == js[-1] and d == 1))
                fill(last, ("fss", g))
            ada_post(3)
            pe.wait_ge(s["xn_ready"], 1)
            for kt in range(KT):
                o = claim(pe, ("xT", kt))
                for j in range(NT):
                    last = tr(o[:, tile(j)], x_in[:, j, tile(kt)], ident)
                fill(last, ("xT", kt))
            pe.wait_ge(s["fs_ready"], 1)

            def dft(o, u, part, rhs):
                if u == 0:
                    return mm(o, C("dft_ctx")[:, part * P:part * P + P], rhs(0), start=True, stop=True)
                for tt in range(2):
                    a = (tt * 2 + u - 1) * 2 * P + part * P
                    last = mm(o, C("dft_lat")[:, a:a + P], rhs(1 + tt), start=(tt == 0), stop=(tt == 1))
                return last

            for u in range(3):
                for r in range(2):
                    o = claim(pe, ("fd", u, r))
                    fill(dft(o[:, :], u, r, lambda j: (FS, FD)[r][:, j, :]), ("fd", u, r))
            for g, js in enumerate(((0,), (1, 2))):
                o = claim(pe, ("fn", g))
                for j in js:
                    last = mm(o[0:1, :], C("alt"), FS[:, j, :], start=(j == js[0]), stop=(j == js[-1]))
                fill(last, ("fn", g))

            def proj_T(n, tiles=range(4)):
                w = chunk(pe, ("in", n))
                for i in tiles:
                    o = claim(pe, ("in", n, i))
                    for kt in range(KT):
                        last = mm(o[:, 0:TOK], w[:, kt, tile(i)], hT[:, kt, :], start=(kt == 0), stop=(kt == KT - 1))
                    fill(last, ("in", n, i))

            def proj_rows(n):
                w = chunk(pe, ("in", n))
                for j in range(NT):
                    o = claim(pe, ("in", n, j))
                    for kt in range(KT):
                        last = mm(o[:, :], hT[:, kt, tile(j)], w[:, kt, :], start=(kt == 0), stop=(kt == KT - 1))
                    fill(last, ("in", n, j))

            for kt in range(KT):
                taken(pe, ("xT", kt))
            for n in (2, 3):
                proj_T(n)
            proj_rows(4)
            for n in (0, 1):
                proj_T(n)

            for lev in range(NLEV):
                for d in range(2):
                    if lev < NLEV - 1:
                        pe.wait_ge(s["lev_ready"], 2 * lev + d + 1)
                        ka, qa = KL[:, d, :], QL[:, d, :]
                    else:
                        ka, qa = HK[:, d, :], HQ[:, :]
                    first = [claim(pe, ("lev", lev, d, par)) for par in range(2)]
                    if d == 0:
                        third = [claim(pe, ("lev2", lev, par)) for par in range(2)]
                    for b in (2, 0, 1):
                        for t in range(2):
                            a = t * TOK + b * P
                            for par in range(2):
                                o, c = (third, 2 * d + t) if b == 2 else (first, 2 * b + t)
                                rp = slice(par * 64, par * 64 + 64)
                                last = mm(o[par][:, tile(c)], ka[rp, a:a + P], qa[rp, a:a + P], start=True, stop=True,
                                          tile_position=(64 * par, 0))
                                if b == 1 and t == 1:
                                    fill(last, ("lev", lev, d, par))
                                elif d == 1 and b == 2 and t == 1:
                                    fill(last, ("lev2", lev, par))
            pe.wait_ge(s["hg_qk"], 2)
            for d in range(2):
                o = claim(pe, ("kt", d))
                for i in range(2):
                    b = 0 if i == 0 else (1 if d == 0 else 2)
                    for t in range(2):
                        c = (i * 2 + t) * P
                        last = tr(o[:, c:c + P], KL[:, d, t * TOK + b * P:t * TOK + b * P + P], ident)
                fill(last, ("kt", d))
            for d in range(2):
                taken(pe, ("kt", d))
                o = claim(pe, ("hU", d))
                for i in range(2):
                    b = 0 if i == 0 else (1 if d == 0 else 2)
                    for t in range(2):
                        c = (i * 2 + t) * P
                        last = mm(o[:, c:c + P], KTOK[:, d, i, t, :], TMH[:, b, t * P:t * P + P], start=True, stop=True)
                fill(last, ("hU", d))
            for par in range(2):
                for d in range(2):
                    taken(pe, ("lev", NLEV - 1, d, par))
                taken(pe, ("lev2", NLEV - 1, par))
            for j in range(NT):
                o = claim(pe, ("ho", j))
                first = True
                if j == 1:
                    for d in range(2):
                        taken(pe, ("hU", d))
                if j > 0:
                    for d in range(2):
                        w = (j - 1) if d == 0 else (2 - j)
                        for t in range(2):
                            mm(o[:, t * P:t * P + P], QL[:, d, t * TOK + j * P:t * TOK + j * P + P], HGS[:, w, d, t, :],
                               start=first, stop=False, skip_group_check=True)
                            first = False
                for t in range(2):
                    for par in range(2):
                        h = 2 * t + par
                        for d in range(2):
                            last = mm(o[:, h * 64:h * 64 + 64], SC[:, d, par, j, t, :], TMH[:, j, h * 64:h * 64 + 64],
                                      start=first, stop=(d == 1), skip_group_check=True)
                            first = False
                fill(last, ("ho", j))
            proj_T(5)
            proj_rows(6)

            def turn(name, src, ready, count):
                pe.wait_ge(s[ready], count)
                for t in range(2):
                    o = claim(pe, (name, t))
                    for j in range(NT):
                        last = tr(o[:, tile(j)], src[:, j, tile(t)], ident)
                    fill(last, (name, t))

            turn("hm", HO, "ho_ready", 1)
            pe.wait_ge(s["bd_ready"], 16 * 16)
            pe.wait_ge(s["xc_ready"], 1)
            for d in range(2):
                for k in range(2):
                    for t in range(2):
                        o = claim(pe, ("rg", d, k, t))
                        fill(mm(o[:, 0:RUN], BD[:, d, k, t, :], XC[:, t, SEG_C:SEG_C + RUN], start=True, stop=True),
                             ("rg", d, k, t))

            def spectra(n, meanwhile):
                for u in range(3):
                    o = claim(pe, ("V", n, u))
                    for r in range(2):
                        last = dft(o[:, r * HYC:r * HYC + HYC], u, r, lambda j: VT[:, j, :])
                    fill(last, ("V", n, u))
                meanwhile()
                for u in range(3):
                    taken(pe, ("V", n, u))
                for t in range(2):
                    o = claim(pe, ("y", n, t))
                    for r in range(2):
                        mm(o[:, 0:CTX], Y[:, 0, r, tile(t)], C("idft_ctx")[:, r * CTX:r * CTX + CTX],
                           start=(r == 0), stop=(r == 1))
                    for u in range(2):
                        for r in range(2):
                            a = (u * 2 + r) * LAT
                            last = mm(o[:, CTX:TOK], Y[:, 1 + u, r, tile(t)], C("idft_lat")[:, a:a + LAT],
                                      start=(u == 0 and r == 0), stop=(u == 1 and r == 1))
                    fill(last, ("y", n, t))

            def turn_tokens(n, src):
                for j in range(NT):
                    o = claim(pe, ("vt", n, j))
                    for t in range(2):
                        last = tr(o[:, tile(t)], src(t, j), ident)
                    fill(last, ("vt", n, j))

            ada(4)
            ada(5)
            pe.wait_ge(s["u_ready"], 1)
            turn_tokens(0, lambda t, j: U[:, t, SEG_C:SEG_C + P] if j == 0 else
                        U[:, t, SEG_L + (j - 1) * P:SEG_L + j * P])
            for j in range(NT):
                taken(pe, ("vt", 0, j))
            def modulation_0():
                ada_post(4)
                ada_post(5)
                ada(6)

            def modulation_1():
                ada(7)
                ada_post(6)

            spectra(0, modulation_0)
            pe.wait_ge(s["z1"], 1)
            turn_tokens(1, lambda t, j: ZT[:, t, tile(j)])
            for j in range(NT):
                taken(pe, ("vt", 1, j))
            spectra(1, modulation_1)

            for i in range(4):
                taken(pe, ("in", 5, i))
            for i in range(4):
                o = claim(pe, ("rope", i))
                fill(mm(o[:, 0:LAT], C("swap"), PR[:, i, CTX:TOK], start=True, stop=True), ("rope", i))
            ada(8)
            ada_post(7)
            pe.wait_ge(s["rope"], 1)
            for par in range(2):
                o = claim(pe, ("rsc", par))
                rp = slice(par * 64, par * 64 + 64)
                for t in range(2):
                    last = mm(o[:, tile(t)], PR[rp, 2 + t, 0:CTX], PR[rp, t, 0:CTX], start=True, stop=True)
                fill(last, ("rsc", par))
            for h in range(4):
                rp = slice((h % 2) * 64, (h % 2) * 64 + 64)
                o = claim(pe, ("rsl", h))
                for st in range(2):
                    last = mm(o[:, st * LAT:st * LAT + LAT], PR[rp, 2 + h // 2, CTX + st * P:CTX + st * P + P],
                              PR[rp, h // 2, CTX:TOK], start=True, stop=True)
                fill(last, ("rsl", h))
            ada(9)
            ada_post(8)
            pe.wait_ge(s["rtail"], 1)
            o = claim(pe, "rkt")
            for d in range(2):
                for t in range(2):
                    last = tr(o[:, tile(2 * d + t)], TAIL[:, d, t, :], ident)
            fill(last, "rkt")
            taken(pe, "rkt")
            o = claim(pe, "rU")
            for d in range(2):
                for t in range(2):
                    last = mm(o[:, tile(2 * d + t)], RKT[:, d, t, :], TMR[:, 0, tile(t)], start=True, stop=True)
            fill(last, "rU")
            for par in range(2):
                taken(pe, ("rsc", par))
            for j in range(NT):
                o = claim(pe, ("ro", j))
                first = True
                if j == 1:
                    for h in range(4):
                        taken(pe, ("rsl", h))
                    pe.wait_ge(s["qd"], 1)
                    pe.wait_ge(s["rs_ready"], 16 * 4)
                if j > 0:
                    for d in range(2):
                        for t in range(2):
                            mm(o[:, tile(t)], QD[:, d, t, (j - 1) * P:j * P], RS[:, d, t, :],
                               start=first, stop=False, skip_group_check=True)
                            first = False
                for h in range(4):
                    c = slice(h * 64, h * 64 + 64)
                    if j == 0:
                        last = mm(o[:, c], WC[:, h % 2, h // 2, :], TMR[:, 0, c], start=first, stop=True,
                                  skip_group_check=True)
                        first = False
                    else:
                        for st in range(2):
                            a = st * LAT + (j - 1) * P
                            last = mm(o[:, c], WL[:, h, a:a + P], TMR[:, 1 + st, c], start=False, stop=(st == 1),
                                      skip_group_check=True)
                fill(last, ("ro", j))
            ada_post(9)
            pe.wait_ge(s["rgo"], 1)
            pe.wait_ge(s["hy_done"], 1)
            for t in range(2):
                taken(pe, ("hm", t))
            w = [chunk(pe, ("out", n)) for n in range(2)]
            banks = {}
            for j in range(NT):
                for n in range(2):
                    banks[j, n] = claim(pe, ("out", n, j))
                    for kt in range(KT - 2):
                        mm(banks[j, n][:, :], hT[:, kt, tile(j)], w[n][:, kt, :], start=(kt == 0), stop=False)
            turn("rm", RO, "ro_ready", 1)
            for t in range(2):
                taken(pe, ("rm", t))
            for j in range(NT):
                for n in range(2):
                    for kt in (KT - 2, KT - 1):
                        last = mm(banks[j, n][:, :], hT[:, kt, tile(j)], w[n][:, kt, :], start=False, stop=(kt == KT - 1))
                    fill(last, ("out", n, j))
            ada(10)
            ada(11)
            pe.wait_ge(s["n2_ready"], NT)
            for kt in range(KT):
                o = claim(pe, ("x2T", kt))
                for j in range(NT):
                    last = tr(o[:, tile(j)], h2tok[j][:, tile(kt)], ident)
                fill(last, ("x2T", kt))
            for kt in range(KT):
                taken(pe, ("x2T", kt))
            o = claim(pe, "logits")
            for j in range(NT):
                for kt in range(KT):
                    last = mm(o[:, j * E:j * E + E], hT[:, kt, tile(j)], wr[:, kt, :], start=(kt == 0),
                              stop=(kt == KT - 1))
            fill(last, "logits")
            for j in range(NT):
                for half in range(2):
                    o = claim(pe, ("h2", j, half))
                    for q in range(4):
                        last = tr(o[:, tile(q)], hT[:, half * 4 + q, tile(j)], ident)
                    fill(last, ("h2", j, half))
            ada_post(10)
            ada_post(11)
            pe.wait_ge(s["route"], 1)
            o = claim(pe, "places")
            for j in range(NT):
                for i in range(j + 1):
                    mm(o[:, j * E:j * E + E], C("triu") if i == j else C("ones"), RT[:, 6, i, :],
                       start=(i == 0), stop=(i == j))
            for i in range(NT):
                last = mm(o[:, NT * E:NT * E + E], C("ones"), RT[:, 6, i, :], start=(i == 0), stop=(i == NT - 1))
            fill(last, "places")
            o = claim(pe, "lst")
            for j in range(NT):
                pe.wait_ge(s["sel"], j + 1)
                for e in range(E):
                    last = mm(o[:, e:e + 1], SEL[:, e, :], tokid16[:, j:j + 1], start=(j == 0 and e == 0),
                              stop=(j == NT - 1), skip_group_check=True)
                if j < NT - 1:
                    last.then_inc(s["sel_used"], 1)
            fill(last, "lst")
            n = len(uses)
            for b in range(8):
                pe.wait_ge(emptied[b], (n - b + 7) // 8)

            def packed(bank, x, w, terms):
                for k in range(terms):
                    for g in range(3):
                        mm(psum[32 * g:32 * g + 32, bank, 0:PACK], x(k, g), w(k)[:, 0:PACK], start=(k == 0),
                           stop=(k == terms - 1), tile_position=(0, 32 * g))
                    for g in range(3):
                        last = mm(psum[96:128, bank, tile(g)], x(k, g), w(k)[:, PACK:CW], start=(k == 0 and g == 0),
                                  stop=(k == terms - 1), skip_group_check=True, tile_position=(0, 96))
                return last

            def turn_x(src):
                for kt in range(KT):
                    c = kt % 4 * ROWS
                    last = tr(psum[:, kt // 4, c:c + ROWS], src[0:ROWS, tile(kt)], ident[0:ROWS, 0:ROWS])
                return last

            def turn_h(p):
                for q in range(3):
                    last = tr(psum[:, 4, tile(q)], he[:, p, tile(q)], ident)
                return last

            def up(p, bank, w):
                return packed(bank, lambda k, g: xeT[p][:, k, 32 * g:32 * g + 32], lambda k: w[:, k, :], KT)

            def down(half, w):
                return packed(5 + half, lambda q, g: heT[:, q, 32 * g:32 * g + 32] if q < 3 else heT[:, g, ROWS:P],
                              lambda q: w[:, q, half * CW:half * CW + CW], FE // P)

            def load_x(n, p, it, lead):
                pe.wait_ge(s[f"xe{p}"], 16 * it + 16)
                if not lead:
                    pe.wait_ge(s["xt_ready"], n)
                turn_x(xe[p]).then_inc(s["xt_filled"], 1)

            def experts(it, first, last_pair):
                for p in range(2):
                    n = 2 * it + p
                    base = 0 if p else PRE_USES
                    pe.wait_ge(s["xt_ready"], n + 1)
                    if not (first and p == 0):
                        pe.wait_ge(s["h_ready"], n)
                    for k, (what, bank) in enumerate((("gate_done", 2), ("up_done", 3))):
                        w = slot[NS * p + k]
                        pe.wait_ge(loaded[NS * p + k], 16 * (it + base) + 16)
                        up(p, bank, w).then_inc(s[what], 1)
                    if not (last_pair and p == 1):
                        load_x(n + 1, 1 - p, it + p, False)
                    pe.wait_ge(s["h_ready"], n + 1)
                    if not (first and p == 0):
                        pe.wait_ge(s["ht_ready"], n)
                    turn_h(p).then_inc(s["ht_filled"], 1)
                    w = slot[NS * p + 2][:, :, :].rearrange("p k n -> p (k n)").rearrange("p (k d) -> p k d", d=D)
                    pe.wait_ge(loaded[NS * p + 2], 16 * (it + base) + 16)
                    pe.wait_ge(s["ht_ready"], n + 1)
                    if not (first and p == 0):
                        pe.wait_ge(s["ya"], n)
                        pe.wait_ge(s["yb"], n)
                    down(0, w)
                    down(1, w).then_inc(s["down_done"], 1)

            load_x(0, 0, 0, True)
            experts(0, True, False)
            with pe.Fori(1, E // 2 - 1) as it:
                experts(it, False, False)
            experts(E // 2 - 1, False, True)

            with pe.If(further(pe) > 0):
                for o in range(OVER):
                    pe.wait_ge(s["o_sel"], o + 1)
                    if o > 0:
                        pe.wait_ge(s["o_lst"], o)
                    for i in range(2 * NT):
                        last = mm(psum[:, 7, 0:1], SO[:, i, :], C("tokid")[:, i % NT:i % NT + 1],
                                  start=(i == 0), stop=(i == 2 * NT - 1))
                    last.then_inc(s["o_selm"], 1)
                with pe.Fori(0, OVER) as o:
                    pe.wait_ge(s["o_xe"], 16 * o + 16)
                    turn_x(xe[0]).then_inc(s["o_xt"], 1)
                    pe.wait_ge(s["o_xtr"], o + 1)
                    pe.wait_ge(s["o_w"], 48 * o + 48)
                    up(0, 2, slot[0])
                    up(0, 3, slot[1]).then_inc(s["o_up"], 1)
                    pe.wait_ge(s["o_h"], o + 1)
                    turn_h(0).then_inc(s["o_ht"], 1)
                    pe.wait_ge(s["o_htr"], o + 1)
                    w = slot[2][:, :, :].rearrange("p k n -> p (k n)").rearrange("p (k d) -> p k d", d=D)
                    down(0, w)
                    down(1, w).then_inc(s["o_down"], 1)

        def steps(eng, name):
            count = [0]

            def link(ins):
                count[0] += 1
                ins.then_inc(s[name], 1)
                eng.wait_ge(s[name], count[0])
            return link

        @block.sync
        def _(sp):
            last_of = {"ada": lambda n: ("ada", n), "in": lambda n: ("in", n, 2 if n in (4, 6) else 3),
                       "out": lambda n: ("out", n, NT - 1)}
            src_of = {"ada": A["w_ada"][0], "in": A["w_in"][0], "out": A["w_out"][0]}
            for i, (kind, n) in enumerate(PRE):
                if i >= NS:
                    take(sp, last_of[PRE[i - NS][0]](PRE[i - NS][1]))
                sp.dma_start(slot[i % NS][:, :, :],
                             src_of[kind][:, n * CW:n * CW + CW].rearrange("(k p) n -> p k n", p=P)
                             ).then_inc(loaded[i % NS], 16)
                if i == 0:
                    for dst, src in vec_loads[:N_VEC // 2]:
                        sp.dma_start(dst, src, allow_slow_non_contiguous=True).then_inc(s["vec_in"], 16)
                    sp.dma_start(x_in[:, 0, :], A["x_prompt"][0]).then_inc(s["x_in"], 16)
                    sp.dma_start(x_in[:, 1:3, :], A["x_sample"][0].rearrange("(j p) d -> p j d", p=P)
                                 ).then_inc(s["x_in"], 16)
                    sp.wait_ge(s["filt_in"], 16 * N_FILT)
                if i == 2:
                    sp.dma_start(const[:, FIRST:], A["const"][:, FIRST:]).then_inc(s["const_in"], 16)
                    sp.dma_start(mask_in, A["masks"]).then_inc(s["mask_in"], 16)
                    sp.dma_start(wr[:, :, :], A["w_router"].rearrange("(k p) e -> p k e", p=P)).then_inc(s["late_in"], 16)
                    sp.dma_start(rbias[:, :], A["router_bias"].rearrange("(o e) -> o e", o=1).to_broadcast([P, E])
                                  ).then_inc(s["late_in"], 16)
                    sp.dma_start(hgn[:, :], A["hg_norm"].to_broadcast([P, HYC])).then_inc(s["late_in"], 16)

            def load_expert(e, p, k, it, signal=None):
                w = (A["w_gate"], A["w_up"], A["w_down"])[k]
                dst = slot[NS * p + k]
                src = w[0, e] if isinstance(e, int) else w[0, bass.ds(e, 1)].rearrange("o a b -> (o a) b")
                if k == 2:
                    dst = dst[:, :, :].rearrange("p k n -> p (k n)").rearrange("p (k d) -> p k d", d=D)
                    src = src.rearrange("(k p) d -> p k d", p=P)
                else:
                    dst = dst[:, :, :]
                    src = src.rearrange("(k p) f -> p k f", p=P)
                sp.dma_start(dst, src).then_inc(loaded[NS * p + k] if signal is None else signal, 16)

            for k in range(3):
                key = PRE[len(PRE) - NS + k]
                take(sp, last_of[key[0]](key[1]))
                load_expert(0, 0, k, 0)
            take(sp, ("rm", 1))
            sp.wait_ge(s["state_out"], 16 * 3)
            for k in range(3):
                load_expert(1, 1, k, 0)
            with sp.Fori(1, E // 2) as it:
                for p in range(2):
                    for k, what in enumerate(("gate_done", "up_done", "down_done")):
                        sp.wait_ge(s[what], 2 * it + p - 1)
                        load_expert(2 * it + p, p, k, it)
            with sp.If(further(sp) > 0):
                sp.wait_ge(s["down_done"], E)
                for k in range(3):
                    load_expert(sp.value_load(further_passes[0:1, 1:2], min_val=0, max_val=E - 1), 0, k, 0, s["o_w"])
                with sp.Fori(1, OVER) as o:
                    sp.wait_ge(s["o_down"], o)
                    e = sp.value_load(further_passes[0:1, bass.ds(o + 1, 1)], min_val=0, max_val=E - 1)
                    for k in range(3):
                        load_expert(e, 0, k, 0, s["o_w"])

        @block.gpsimd
        def _(pool):
            link = steps(pool, "pool_step")
            g = nc.gpsimd
            link(g.memset(mhalf[:, :], -0.5))
            g.memset(HGS[:, :, :, :, :], 0.0).then_inc(s["pads"], 1)

            def rstd(kind, dst, src):
                pool.wait_ge(s[kind + "_var"], 1)
                n = src.shape[-1]
                g.tensor_tensor(dst, src, mhalf[:, 0:n], ALU.pow).then_inc(s[kind + "_rstd"], 1)

            rstd("x", stat[:, 1, 0:NT], stat[:, 0, 0:NT])
            pool.wait_ge(s["pads"], 1)
            for half in range(2):
                r = slice(half * 64, half * 64 + 64)
                for d in range(2):
                    pool.dma_start(HGS[r, 0, d, :, half * 64:half * 64 + 64],
                                   A["state_hgrn"][0, 0, d].rearrange("(t h) k v -> h k t v", h=2)[half]
                                   ).then_inc(s["states0"], 16)
            pool.wait_ge(s["mask_in"], 16)
            g.tensor_copy(mask[:, :, :, :].rearrange("p l d q -> p (l d q)"), mask_in).then_inc(s["mask_ready"], 1)
            take(pool, ("xT", KT - 1))
            for a, w in ((0, 2), (130, 3), (389, 1)):
                last = g.memset(CU[:, :, a:a + w], 0.0)
            last.then_inc(s["pads"], 1)
            pool.wait_ge(s["kl_zero"], 1)
            for o in range(OVER):
                pool.dma_start(A["y_rows"][(E + o) * ROWS:(E + o + 1) * ROWS, :],
                               KL[0:ROWS, :, :].rearrange("p d n -> p (d n)")[:, 0:D]).then_inc(s["y_zero"], 16)
            pool.wait_ge(s["u_ready"], 1)
            pool.wait_ge(s["xc_ready"], 1)
            g.memset(XS[:, 0:3072], 0.0).then_inc(s["sc_zero"], 1)
            rstd("ho", stat[:, 3, 0:12], stat[:, 2, 0:12])
            take(pool, ("ho", NT - 1))
            link(g.memset(XS[:, 0:1024], 0.0))
            for k, name in enumerate(("rg_wa", "rg_wx")):
                for q in range(4):
                    r = slice(q * 32, q * 32 + 32)
                    for d in range(2):
                        pool.dma_start(BD[r, d, k, :, q * 32:q * 32 + 32],
                                       A[name][0, d].rearrange("(t q) i j -> q i t j", q=4)[q]).then_inc(s["bd_ready"], 16)
            take(pool, ("rg", 1, 1, 1))
            pool.dma_start(XR[:, 0, :], A["x_prompt"][0]).then_inc(s["res_in"], 16)
            pool.dma_start(XR[:, 1:3, :], A["x_sample"][0].rearrange("(j p) d -> p j d", p=P)).then_inc(s["res_in"], 16)
            pool.wait_ge(s["hy_done"], 1)
            link(g.memset(RS[:, :, :, :], 0.0))
            for half in range(2):
                r = slice(half * 64, half * 64 + 64)
                for d in range(2):
                    pool.dma_start(RS[r, d, :, half * 64:half * 64 + 64],
                                   A["state_ret"][0, 0, d].rearrange("(t h) k v -> h k t v", h=2)[half]
                                   ).then_inc(s["rs_ready"], 16)
            rstd("ro", stat[:, 3, 0:12], stat[:, 2, 0:12])
            rstd("n2", stat[:, 1, 0:NT], stat[:, 0, 0:NT])
            for j in range(NT):
                for half in range(2):
                    taken(pool, ("h2", j, half))
            for j in range(NT):
                pool.dma_start(A["h2_rows"][tile(j), :], h2tok[j][:, :]).then_inc(s["h2_out"], 16)
            taken(pool, "lst")

            pool.wait_ge(s["h2_out"], 16 * NT)
            for n in range(E):
                if n >= 2:
                    pool.wait_ge(s["xt_filled"], n - 1)
                g.indirect_dma_start(out=xe[n % 2][0:ROWS, :], out_offset=None, in_=A["h2_rows"],
                                     in_offset=bass.IndirectOffsetOnAxis(ap=lst[0:ROWS, n:n + 1], axis=0)
                                     ).then_inc(s[f"xe{n % 2}"], 16)
            with pool.If(further(pool) > 0):
                for o in range(OVER):
                    pool.wait_ge(s["o_lst"], o + 1)
                    pool.wait_ge(s["xt_filled"], E) if o == 0 else pool.wait_ge(s["o_xt"], o)
                    g.indirect_dma_start(out=xe[0][0:ROWS, :], out_offset=None, in_=A["h2_rows"],
                                         in_offset=bass.IndirectOffsetOnAxis(ap=lsto[0:ROWS, o:o + 1], axis=0)
                                         ).then_inc(s["o_xe"], 16)
                pool.wait_ge(s["o_out"], 32 * OVER)
            for p in range(2):
                pool.wait_ge(s[f"y_out{p}"], 32 * E // 2)
            for j in range(NT):
                for k in range(2):
                    g.indirect_dma_start(out=YG[k][:, j, :], out_offset=None, in_=A["y_rows"],
                                         in_offset=bass.IndirectOffsetOnAxis(ap=rows[:, j, k:k + 1], axis=0)
                                         ).then_inc(s[f"fin_in{j}"], 16)
            rstd("fin", stat[:, 1, 0:NT], stat[:, 0, 0:NT])

        @block.scalar
        def _(act):
            link = steps(act, "act_step")
            a = nc.scalar.activation
            act.dma_start(const[:, 0:FIRST], A["const"][:, 0:FIRST]).then_inc(s["first_in"], 16)
            for dst, src in vec_loads[N_VEC // 2:]:
                act.dma_start(dst, src, allow_slow_non_contiguous=True).then_inc(s["vec_in"], 16)
            act.dma_start(w1[0:HY_EMB, :], A["hy_w1"][0]).then_inc(s["filt_in"], 16)
            act.dma_start(w2[0:HY_FFN, :], A["hy_w2"][0]).then_inc(s["filt_in"], 16)
            act.dma_start(w3[0:HY_FFN, :], A["hy_w3"][0]).then_inc(s["filt_in"], 16)
            act.dma_start(b12[0:HY_FFN, 0:1], A["hy_b1"].rearrange("b n -> n b"),
                          allow_slow_non_contiguous=True).then_inc(s["filt_in"], 16)
            act.dma_start(b12[0:HY_FFN, 1:2], A["hy_b2"].rearrange("b n -> n b"),
                          allow_slow_non_contiguous=True).then_inc(s["filt_in"], 16)
            act.dma_start(z_t[0:HY_EMB, :], A["z_table"]).then_inc(s["filt_in"], 16)
            act.dma_start(win, A["window"].rearrange("p (j n) -> p j n", j=NT)).then_inc(s["filt_in"], 16)
            taken(act, "vcols")
            a(sige[:, :], VC[:, 0:16], ACT.Exp, scale=-1.0).then_inc(s["siluc_exp"], 1)
            act.wait_ge(s["sp_in"], 1)
            link(a(sptmp[:, 0, :], SC16[:, :], ACT.Abs))
            a(sptmp[:, 1, :], sptmp[:, 0, :], ACT.Exp, scale=-1.0).then_inc(s["sp_abs"], 1)
            act.wait_ge(s["x_in"], 32)
            for j in range(NT):
                last = a(T[:, 3072 + j * D:3072 + j * D + D], x_in[:, j, :], ACT.Square, accum_out=stat[:, 2, j:j + 1])
            last.then_inc(s["x_sq"], 1)

            def modrow_out(n):
                o = take(act, ("ada", n))
                if n >= 2:
                    take(act, ("adag", n - 2, 1) if (n - 2) // 2 in (2, 5) else ("adac", n - 2))
                give(a(modrow[:, n % 2, :], o[:, :], ACT.Copy), ("ada", n))

            def gate_out(n, dst):
                for c in range(2):
                    o = take(act, ("adag", n, c))
                    give(a(dst[:, c, (n % 2) * CW:(n % 2) * CW + CW], o[:, :], ACT.Copy), ("adag", n, c))

            modrow_out(0)
            act.wait_ge(s["fu_arg"], 1)
            a(fu[1][0:HY_FFN, :], fu[0][0:HY_FFN, :], ACT.Sin).then_inc(s["fu_sin"], 1)
            modrow_out(1)
            act.wait_ge(s["fu_arg"], 2)
            a(fu[1][0:HY_FFN, :], fu[0][0:HY_FFN, :], ACT.Sin).then_inc(s["fu_sin"], 1)
            modrow_out(2)
            modrow_out(3)
            for j in range(NT):
                for q in range(2):
                    taken(act, ("fh", j, q))
            for q in range(2):
                v = FH[:, :, q, :, :].rearrange("p j d c -> p j (d c)")
                last = a(FSQ[q], v, ACT.Square)
            last.then_inc(s["fsq_ready"], 1)
            for g in range(2):
                taken(act, ("fss", g))
            a(FRS, FRS, ACT.Sqrt).then_inc(s["frs_sqrt"], 1)
            act.wait_ge(s["mod1"], 1)
            for kt in range(1, KT, 2):
                o = take(act, ("xT", kt))
                for c, r in ((0, slice(0, CTX)), (1, slice(CTX, TOK))):
                    last = a(hT[:, kt, r], o[:, r], ACT.Identity, scale=AB[:, 0, kt, c:c + 1], bias=MC[:, 0, kt, c:c + 1])
                give(last, ("xT", kt))
            for i in range(4):
                o = take(act, ("in", 2, i))
                dst = RGG[:, i, :] if i < 2 else HQ[:, (i - 2) * TOK:(i - 1) * TOK]
                give(a(dst, o[:, 0:TOK], ACT.Copy), ("in", 2, i))
            act.wait_ge(s["fs_ready"], 1)
            for i in range(4):
                o = take(act, ("in", 3, i))
                give(a(LF[:, i // 2, (i % 2) * TOK:(i % 2 + 1) * TOK], o[:, 0:TOK], ACT.Copy), ("in", 3, i))
            for i in range(4):
                taken(act, ("in", 3, i))
            link(a(W, LF, ACT.Abs))
            link(a(W, W, ACT.Exp, scale=-1.0))
            a(W, W, ACT.Ln, bias=1.0).then_inc(s["hg_abs"], 1)
            a(HK[:, :, :], LF, ACT.Exp).then_inc(s["hg_exp"], 1)
            for g in range(2):
                taken(act, ("fn", g))
            for i in (2, 3):
                taken(act, ("in", 2, i))
            a(QL[:, 0, :], HQ[:, :], ACT.Exp, scale=-1.0).then_inc(s["hq_exp"], 1)
            for j in range(NT):
                o = take(act, ("in", 4, j))
                give(a(TMH[:, j, :], o[:, :], ACT.Copy), ("in", 4, j))
            for n in (0, 1):
                for i in range(4):
                    o = take(act, ("in", n, i))
                    a(CU[:, 4 * n + i, SEG_C:SEG_C + CTX], o[:, 0:CTX], ACT.Copy)
                    give(a(CU[:, 4 * n + i, SEG_L:SEG_L + LAT], o[:, CTX:TOK], ACT.Copy), ("in", n, i))
            for lev in range(NLEV):
                if lev < NLEV - 1:
                    for d in range(2):
                        act.wait_ge(s["lev_arg"], 2 * lev + d + 1)
                        a(W[:, d, :], W[:, d, :], ACT.Exp).then_inc(s["lev_exp"], 1)
            act.wait_ge(s["hg_tx"], 1)
            a(W, HX[:, :, :], ACT.Exp)
            a(LF, LF, ACT.Exp)
            a(HTOT[:, :, :], HTOT[:, :, :], ACT.Exp).then_inc(s["hg_texp"], 1)
            take(act, ("kt", 1))
            act.wait_ge(s["hg_qk"], 2)
            a(HGATE, TMH[:, :, HYC:2 * HYC], ACT.Exp, scale=-1.0).then_inc(s["ho_gexp"], 1)
            for j in range(NT):
                o = take(act, ("ho", j))
                give(a(HO[:, j, :], o[:, 0:HYC], ACT.Copy), ("ho", j))
            for i in range(4):
                o = take(act, ("in", 5, i))
                give(a(PR[:, i, :], o[:, 0:TOK], ACT.Copy, scale=1.0 if i < 2 else DH ** -0.5), ("in", 5, i))
            for j in range(NT):
                o = take(act, ("in", 6, j))
                give(a(TMR[:, j, :], o[:, :], ACT.Copy), ("in", 6, j))
            for t in range(2):
                o = take(act, ("hm", t))
                give(a(hT[:, 4 + t, :], o[:, 0:TOK], ACT.Copy), ("hm", t))
            act.wait_ge(s["gelu_arg"], 1)
            for d in range(2):
                for k in range(2):
                    for t in range(2):
                        o = take(act, ("rg", d, k, t))
                        c = 4 * k + 2 * d + t
                        give(a(RI[:, d, k, t, :], o[:, 0:RUN], ACT.Tanh, scale=0.5, bias=halfb[:, c:c + 1]),
                             ("rg", d, k, t))

            def vt_out(n):
                for j in range(NT):
                    o = take(act, ("vt", n, j))
                    give(a(VT[:, j, :], o[:, 0:HYC], ACT.Copy), ("vt", n, j))
            modrow_out(4)
            modrow_out(5)
            vt_out(0)
            for d in range(2):
                for t in range(2):
                    taken(act, ("rg", d, 0, t))
            for d in range(2):
                for t in range(2):
                    c = lamc[:, 2 * d + t:2 * d + t + 1]
                    a(RA[:, d, t, :], RI[:, d, 0, t, :], ACT.Exp, scale=c, bias=c)
                    last = a(RB[:, d, t, :], RI[:, d, 0, t, :], ACT.Tanh, scale=c, bias=c)
            last.then_inc(s["rg_a"], 1)
            a(HQ[:, :], HQ[:, :], ACT.Tanh, scale=math.sqrt(2.0 / math.pi)).then_inc(s["gelu_t"], 1)
            act.wait_ge(s["rg_b2"], 1)
            a(RB, RB, ACT.Sqrt, scale=-1.0).then_inc(s["rg_b"], 1)
            gate_out(4, G1)
            gate_out(5, G1)
            modrow_out(6)
            vt_out(1)
            modrow_out(7)
            act.wait_ge(s["hy_done"], 1)
            cnt = C("count")
            for t in range(2):
                for d in range(2):
                    c = SC16[:, 12 + 2 * d + t:13 + 2 * d + t]
                    a(TAIL[:, d, t, :], cnt[:, 0:P] if d else cnt[:, P - 1::-1], ACT.Exp, scale=c)
                    last = a(EI[:, d, t, :], cnt[:, LAT:0:-1] if d else cnt[:, 1:LAT + 1], ACT.Exp, scale=c)
            last.then_inc(s["ei"], 1)
            for h in range(4):
                f, b = SC16[:, 4 + h:5 + h], SC16[:, 8 + h:9 + h]
                a(DEC[:, h, 0, :], C("dist_f"), ACT.Exp, scale=f)
                a(DTMP[:, h, :], C("dist_b"), ACT.Exp, scale=b)
                a(DEC[:, h, 1, :], C("dist_up"), ACT.Exp, scale=f)
                last = a(DEC[:, h, 2, :], C("dist_lo"), ACT.Exp, scale=b)
            last.then_inc(s["dec"], 1)
            act.wait_ge(s["rtail"], 1)
            a(RGATE, TMR[:, :, HYC:2 * HYC], ACT.Exp, scale=-1.0).then_inc(s["ro_gexp"], 1)
            modrow_out(8)
            modrow_out(9)
            o = take(act, "rkt")
            give(a(RKT.rearrange("p d t n -> p (d t n)"), o[:, :], ACT.Copy), "rkt")
            taken(act, "rU")
            act.wait_ge(s["rgo"], 1)
            for i, name in enumerate(("new_state_hgrn", "new_state_ret")):
                act.dma_start(O[name][0, 0].rearrange("d (t h) k v -> (h k) d t v", h=2), STO[:, 2 * i:2 * i + 2, :, :]
                              ).then_inc(s["state_out"], 16)
            act.dma_start(O["new_state_rglru"][0, 0].rearrange("d (t p) -> p d t", p=P),
                          RGO[:, :].rearrange("p (d t) -> p d t", d=2), allow_slow_non_contiguous=True).then_inc(s["state_out"], 16)
            for j in range(NT):
                o = take(act, ("ro", j))
                give(a(RO[:, j, :], o[:, 0:HYC], ACT.Copy), ("ro", j))
            for t in range(2):
                o = take(act, ("rm", t))
                give(a(hT[:, 6 + t, :], o[:, 0:TOK], ACT.Copy), ("rm", t))
            act.wait_ge(s["state_out"], 48)
            for j in range(NT):
                act.wait_ge(s["x1"], j + 1)
                last = a(h2tok[j][:, :], XR[:, j, :], ACT.Square, accum_out=stat[:, 2, j:j + 1])
            last.then_inc(s["n2_sq"], 1)
            modrow_out(10)
            modrow_out(11)
            for kt in range(1, KT, 2):
                o = take(act, ("x2T", kt))
                for c, r in ((0, slice(0, CTX)), (1, slice(CTX, TOK))):
                    last = a(hT[:, kt, r], o[:, r], ACT.Identity, scale=AB[:, 1, kt, c:c + 1], bias=MC[:, 2, kt, c:c + 1])
                give(last, ("x2T", kt))
            for j in range(NT):
                for half in range(2):
                    o = take(act, ("h2", j, half))
                    give(a(h2tok[j][:, half * 512:half * 512 + 512], o[:, :], ACT.Copy), ("h2", j, half))
                if j == 0:
                    taken(act, "logits")
                    a(RT[:, 0], RT[:, 0], ACT.Exp).then_inc(s["logits_exp"], 1)
            gate_out(10, G2)
            gate_out(11, G2)

            def write_rows(block, p, signal):
                rows = A["y_rows"][block * ROWS:(block + 1) * ROWS, :] if isinstance(block, int) else \
                    A["y_rows"][bass.ds(block * ROWS, ROWS), :]
                act.dma_start(rows.rearrange("r (h c) -> r h c", h=2)[:, :, 0:PACK], yp[p][0:ROWS, :, :]
                              ).then_inc(signal, 16)
                act.dma_start(rows.rearrange("(g r) (h c) -> r h g c", g=3, h=2)[:, :, :, PACK:CW],
                              yp[p][ROWS:P, :, :].rearrange("r h (g c) -> r h g c", g=3)).then_inc(signal, 16)

            def xt_out(n, p, it, lead):
                act.wait_ge(s["xt_filled"], n + 1)
                if not lead:
                    act.wait_ge(s["up_done"], n - 1)
                a(xeTa[:, p].rearrange("p (b k) n -> p b (k n)", b=2), psum[:, 0:2, 0:KT // 2 * ROWS], ACT.Copy
                  ).then_inc(s["xt_ready"], 1)

            def experts(it, first, last_pair):
                for p in range(2):
                    n = 2 * it + p
                    act.wait_ge(s["gate_done"], n + 1)
                    if not first:
                        act.wait_ge(s["ht_filled"], n - 1)
                    a(he[:, p, 0:PACK], psum[:, 2, 0:PACK], ACT.Exp, scale=-1.0).then_inc(s["g_exp"], 1)
                    if not (last_pair and p == 1):
                        xt_out(n + 1, 1 - p, it + p, first and p == 0)
                    act.wait_ge(s["down_done"], n + 1)
                    if not first:
                        act.wait_ge(s[f"y_out{p}"], 32 * it)
                    a(yp[p][:, 0, :], psum[:, 5, 0:PACK], ACT.Copy).then_inc(s["ya"], 1)
                    act.wait_ge(s["ya"], n + 1)
                    act.wait_ge(s["yb"], n + 1)
                    write_rows(n, p, s[f"y_out{p}"])

            xt_out(0, 0, 0, True)
            experts(0, True, False)
            with act.Fori(1, E // 2 - 1) as it:
                experts(it, False, False)
            experts(E // 2 - 1, False, True)
            with act.If(further(act) > 0):
                with act.Fori(0, OVER) as o:
                    act.wait_ge(s["o_xt"], o + 1)
                    a(xeTa[:, 0].rearrange("p (b k) n -> p b (k n)", b=2), psum[:, 0:2, 0:KT // 2 * ROWS], ACT.Copy
                      ).then_inc(s["o_xtr"], 1)
                    act.wait_ge(s["o_up"], o + 1)
                    a(he[:, 0, 0:PACK], psum[:, 2, 0:PACK], ACT.Exp, scale=-1.0).then_inc(s["o_exp"], 1)
                    act.wait_ge(s["o_y"], o + 1)
                    write_rows(o + E, 0, s["o_out"])
                    act.wait_ge(s["o_out"], 32 * o + 32)
            for j in range(NT):
                act.wait_ge(s[f"fin_in{j}"], 32)
                a(YG[0][:, j, :], YG[0][:, j, :], ACT.Copy, scale=gw[:, j, 0:1]).then_inc(s["fin_w"], 1)
            act.dma_start(NF, A["norm_final"].rearrange("(o n) -> o n", o=1).to_broadcast([P, D])
                          ).then_inc(s["nf_in"], 16)
            for j in range(NT):
                act.wait_ge(s["x2"], j + 1)
                last = a(YG[1][:, j, :], XR[:, j, :], ACT.Square, accum_out=stat[:, 2, j:j + 1])
            last.then_inc(s["fin_sq"], 1)
            for j in range(NT):
                dst = O["y_prompt"][0] if j == 0 else O["y_sample"][0, (j - 1) * P:j * P, :]
                act.wait_ge(s["fin_ready"], j + 1)
                act.dma_start(dst, XR[:, j, :]).then_inc(s["fin_out"], 16)
            act.wait_ge(s["fin_out"], 16 * NT)

        @block.vector
        def _(dve):
            link = steps(dve, "dve_step")
            v = nc.vector

            o = take(dve, "vcols")
            give(v.tensor_copy(VC[:, :], o[:, 0:NV]), "vcols")
            taken(dve, "vcols")
            dve.wait_ge(s["vec_in"], 16 * N_VEC)
            v.tensor_copy(SC16[:, 0:4], VC[:, VROWS["lam"]:VROWS["lam"] + 4]).then_inc(s["sp_in"], 1)
            v.tensor_scalar(halfb[:, :], VC[:, VROWS["rba"]:VROWS["rba"] + 8], 0.5, None, ALU.mult)
            dve.wait_ge(s["siluc_exp"], 1)
            link(v.memset(siluc[:, :, :], 0.0))
            link(v.tensor_scalar(sige[:, :], sige[:, :], 1.0, None, ALU.add))
            link(v.reciprocal(sige[:, :], sige[:, :]))
            v.tensor_tensor(siluc[:, :, 0:2].rearrange("p k c -> p c k"),
                            sige[:, :].rearrange("p (c k) -> p c k", c=2),
                            VC[:, 0:16].rearrange("p (c k) -> p c k", c=2), ALU.mult).then_inc(s["siluc"], 1)
            dve.wait_ge(s["x_sq"], 1)
            v.tensor_scalar(stat[:, 0, 0:NT], stat[:, 2, 0:NT], 1.0 / D, EPS, ALU.mult, ALU.add).then_inc(s["x_var"], 1)
            dve.wait_ge(s["sp_abs"], 1)
            w = sptmp[:, 1, :]
            link(v.tensor_scalar(sptmp[:, 2, :], w, 2.0, None, ALU.add))
            link(v.reciprocal(sptmp[:, 2, :], sptmp[:, 2, :]))
            link(v.tensor_tensor(sptmp[:, 2, :], sptmp[:, 2, :], w, ALU.mult))
            link(v.tensor_tensor(sptmp[:, 3, :], sptmp[:, 2, :], sptmp[:, 2, :], ALU.mult))
            link(v.tensor_scalar(sptmp[:, 4, :], sptmp[:, 3, :], 1.0 / 17, 1.0 / 15, ALU.mult, ALU.add))
            for k in range(6, -1, -1):
                link(v.tensor_tensor(sptmp[:, 4, :], sptmp[:, 4, :], sptmp[:, 3, :], ALU.mult))
                link(v.tensor_scalar(sptmp[:, 4, :], sptmp[:, 4, :], 1.0 / (2 * k + 1), None, ALU.add))
            link(v.scalar_tensor_tensor(sptmp[:, 4, :], sptmp[:, 4, :], -2.0, sptmp[:, 2, :], ALU.mult, ALU.mult))
            link(v.scalar_tensor_tensor(SC16[:, :], SC16[:, :], 0.0, sptmp[:, 4, :], ALU.min, ALU.add))
            v.tensor_scalar(lamc[:, :], SC16[:, 0:4], 4.0, None, ALU.mult).then_inc(s["sp_ready"], 1)
            dve.wait_ge(s["x_rstd"], 1)
            for j in range(NT):
                last = v.tensor_scalar(x_in[:, j, :], x_in[:, j, :], stat[:, 1, j:j + 1], None, ALU.mult)
            last.then_inc(s["xn_ready"], 1)

            def sine_arg(n):
                o = take(dve, ("fu", n))
                r, k = fu[0][0:HY_FFN, :], fu[2][0:HY_FFN, :]
                give(v.tensor_scalar(r, o[0:HY_FFN, 0:TOK], b12[0:HY_FFN, n:n + 1], None, ALU.add), ("fu", n))
                taken(dve, ("fu", n))
                link(v.tensor_scalar(k, r, 1.0 / (2 * math.pi), MAGIC, ALU.mult, ALU.add))
                link(v.tensor_scalar(k, k, MAGIC, None, ALU.subtract))
                link(v.scalar_tensor_tensor(r, k, -TURN_HI, r, ALU.mult, ALU.add))
                link(v.scalar_tensor_tensor(r, k, -TURN_LO, r, ALU.mult, ALU.add))
                v.tensor_scalar(r, r, PI_DOWN, -PI_DOWN, ALU.min, ALU.max).then_inc(s["fu_arg"], 1)

            def modcol_out(n):
                o = take(dve, ("adac", n))
                kind = {0: 0, 1: 1, 3: 2, 4: 3}[n // 2]
                give(v.tensor_copy(MC[:, kind, (n % 2) * 4:(n % 2) * 4 + 4, :],
                                   o[:, 0:8].rearrange("p (k c) -> p k c", c=2)), ("adac", n))

            dve.wait_ge(s["filt_in"], 16 * N_FILT)
            sine_arg(0)
            modcol_out(0)
            sine_arg(1)
            modcol_out(1)
            for j in range(NT):
                for q in range(2):
                    o = take(dve, ("fh", j, q))
                    ins = v.tensor_tensor(FH[:, j, q, :, :], o[:, :].rearrange("p (d c) -> p d c", d=2),
                                          win[:, j, :].unsqueeze(1).to_broadcast([P, 2, HYC]), ALU.mult)
                    give(ins, ("fh", j, q))
            modcol_out(2)
            for g in range(2):
                o = take(dve, ("fss", g))
                give(v.tensor_scalar(FRS[:, g, :], o[:, :], EPS, None, ALU.add), ("fss", g))
            modcol_out(3)
            taken(dve, ("adac", 2))
            taken(dve, ("adac", 3))
            v.scalar_tensor_tensor(AB[:, 0], MC[:, 1], 1.0,
                                   VC[:, VROWS["norm1"]:VROWS["norm1"] + KT].unsqueeze(2).to_broadcast([P, KT, 2]),
                                   ALU.add, ALU.mult).then_inc(s["mod1"], 1)
            dve.wait_ge(s["mod1"], 1)

            def modulate(name, which, kts):
                for kt in kts:
                    o = take(dve, (name, kt))
                    for c, r in ((0, slice(0, CTX)), (1, slice(CTX, TOK))):
                        last = v.tensor_scalar(hT[:, kt, r], o[:, r], AB[:, which, kt, c:c + 1],
                                               MC[:, 2 * which, kt, c:c + 1], ALU.mult, ALU.add)
                    give(last, (name, kt))

            dve.wait_ge(s["fsq_ready"], 1)
            for j in (0, 1):
                link(v.memset(FH[0:1, j, :, 1, :], 0.0))
            v.tensor_tensor(FS.rearrange("p j (o c) -> p (j o) c", o=2),
                            FH[:, :, :, 0, :].rearrange("p j o c -> p (j o) c"),
                            FH[:, :, :, 1, :].rearrange("p j o c -> p (j o) c"), ALU.add)
            v.tensor_tensor(FD.rearrange("p j (o c) -> p (j o) c", o=2),
                            FH[:, :, :, 0, :].rearrange("p j o c -> p (j o) c"),
                            FH[:, :, :, 1, :].rearrange("p j o c -> p (j o) c"), ALU.subtract).then_inc(s["fs_ready"], 1)
            modulate("xT", 0, range(0, KT, 2))
            dve.wait_ge(s["frs_sqrt"], 1)
            link(v.reciprocal(FRS, FRS))
            dve.wait_ge(s["mask_ready"], 1)
            for u in range(3):
                for r in range(2):
                    o = take(dve, ("fd", u, r))
                    give(v.tensor_tensor(HF[:, u, r].rearrange("p o c -> p (o c)"), o[:, :], FRS[:, min(u, 1), :],
                                         ALU.mult), ("fd", u, r))
            for g in range(2):
                o = take(dve, ("fn", g))
                give(v.tensor_tensor(HNY[0:1, g].rearrange("p o c -> p (o c)"), o[0:1, :], FRS[0:1, g, :], ALU.mult),
                     ("fn", g))
            taken(dve, ("fn", 1))
            link(v.memset(HF[0:1, 0:2, 1, :, :], 0.0))

            dve.wait_ge(s["hg_abs"], 1)
            dve.wait_ge(s["hg_exp"], 1)
            link(v.scalar_tensor_tensor(LF, LF, 0.0, W, ALU.min, ALU.subtract))
            for d in range(2):
                dst = HX[:, 0, :] if d == 0 else W[:, 1, :]
                for t in range(2):
                    r = slice(t * TOK, t * TOK + TOK)
                    last = v.tensor_tensor_scan(dst[:, r], C("reset"), LF[:, d, r], 0.0, ALU.mult, ALU.add)
            link(last)
            wb = W[:, 1, :].rearrange("p (g n) -> p g n", n=P)
            xb = HX[:, 1, :].rearrange("p (g n) -> p g n", n=P)
            v.tensor_copy(HTOT[:, 0, :], HX[:, 0, :].rearrange("p (g n) -> p g n", n=P)[:, :, P - 1])
            v.tensor_copy(HTOT[:, 1, :], wb[:, :, P - 1])
            v.tensor_copy(xb[:, :, 1:P], wb[:, :, 0:P - 1])
            v.memset(xb[:, :, 0:1], 0.0)
            link(v.tensor_scalar(HK[:, :, :], HK[:, :, :], 1.0, None, ALU.add))
            v.reciprocal(HK[:, :, :], HK[:, :, :])
            dve.wait_ge(s["hq_exp"], 1)
            link(v.tensor_scalar(QL[:, 0, :], QL[:, 0, :], 1.0, None, ALU.add))
            link(v.reciprocal(QL[:, 0, :], QL[:, 0, :]))
            link(v.tensor_tensor(HQ[:, :], HQ[:, :], QL[:, 0, :], ALU.mult))
            v.memset(QL, 0.0)
            v.memset(KL, 0.0).then_inc(s["kl_zero"], 1)
            dve.wait_ge(s["kl_zero"], 1)

            def conv(dst, src, taps, first, w, b, groups):
                n = PADW - (taps - 1)
                for k in range(taps):
                    for t in groups:
                        i_, o_ = src(t)[:, k:k + n], dst(t)[:, first:first + n]
                        if k == 0:
                            last = v.tensor_scalar(o_, i_, w(k, t), b(t), ALU.mult, ALU.add)
                        else:
                            last = v.scalar_tensor_tensor(o_, i_, w(k, t), o_, ALU.mult, ALU.add)
                    if k < taps - 1:
                        link(last)
                return last

            def hyena_conv(groups):
                return conv(lambda t: U[:, t, :], lambda t: CU[:, t, :], 3, 1, lambda k, t: col("hcw", 6 * k + t),
                            lambda t: col("hcb", t), groups)

            dve.wait_ge(s["pads"], 2)
            for i in range(4):
                taken(dve, ("in", 0, i))
            hyena_conv(range(4))

            def halves(a, h):
                b = a.rearrange("p (g n) -> p g n", n=2 * h)
                return b[:, :, 0:h], b[:, :, h:2 * h], b

            def level_args(lev):
                h = LEVELS[lev]
                if lev > 0:
                    dve.wait_ge(s["lev_ready"], 2 * lev)
                for d in range(2):
                    x0, x1, x = halves(HX[:, d, :], h)
                    e0, e1, _ = halves(W[:, d, :], h)
                    ref = x[:, :, h - 1 + d:h + d].to_broadcast([P, 2 * TOK // (2 * h), h])
                    v.tensor_tensor(e0, ref, x0, ALU.subtract)
                    v.tensor_tensor(e1, x1, ref, ALU.subtract).then_inc(s["lev_arg"], 1)

            def level_products(lev, d):
                h = LEVELS[lev]
                e, q, k, ql, kl = (halves(m, h) for m in (W[:, d, :], HQ[:, :], HK[:, d, :], QL[:, d, :], KL[:, d, :]))
                dve.wait_ge(s["lev_exp"], 2 * lev + d + 1)
                if lev > 0:
                    take(dve, ("lev", lev - 1, d, 1))
                v.tensor_tensor(ql[1 - d], q[1 - d], e[1 - d], ALU.mult)
                v.tensor_tensor(kl[d], k[d], e[d], ALU.mult).then_inc(s["lev_ready"], 1)

            level_args(0)
            dve.wait_ge(s["y_zero"], 16 * OVER)
            for d in range(2):
                level_products(0, d)
            for i in range(4):
                taken(dve, ("in", 1, i))
            hyena_conv((4, 5)).then_inc(s["u_ready"], 1)
            conv(lambda t: XC[:, t, :], lambda t: CU[:, 6 + t, :], 4, 2, lambda k, t: col("rcw", 2 * k + t),
                 lambda t: col("rcb", t), range(2)).then_inc(s["xc_ready"], 1)

            scf = XS[:, 0:3072].rearrange("p (e g q) -> p e g q", e=4, g=6)

            def place_first(lev, d):
                for par in range(2):
                    o = take(dve, ("lev", lev, d, par))
                    give(v.copy_predicated(
                        scf[:, 2 * d + par, 0:4, :], mask[:, lev, d, :].unsqueeze(1).to_broadcast([P, 4, P]),
                        o[:, :].rearrange("p (g q) -> p g q", q=P)), ("lev", lev, d, par))

            def place_third(lev):
                for par in range(2):
                    o = take(dve, ("lev2", lev, par))
                    give(v.copy_predicated(
                        scf[:, par::2, 4:6, :], mask[:, lev, :, :].unsqueeze(2).to_broadcast([P, 2, 2, P]),
                        o[:, :].rearrange("p (d t q) -> p d t q", d=2, t=2)), ("lev2", lev, par))

            dve.wait_ge(s["sc_zero"], 1)
            for lev in range(1, NLEV - 1):
                level_args(lev)
                for d in range(2):
                    level_products(lev, d)
                    place_first(lev - 1, d)
                place_third(lev - 1)
            dve.wait_ge(s["lev_ready"], 2 * NLEV - 2)
            last = v.scalar_tensor_tensor(
                LF.rearrange("p d (g n) -> p (d g) n", n=P), HX[:, :, :].rearrange("p d (g n) -> p (d g) n", n=P), -1.0,
                HTOT[:, :, :].rearrange("p d g -> p (d g)").unsqueeze(2).to_broadcast([P, 12, P]), ALU.mult, ALU.add)
            last.then_inc(s["hg_tx"], 1)
            for lev in (NLEV - 2, NLEV - 1):
                for d in range(2):
                    place_first(lev, d)
                place_third(lev)
            dve.wait_ge(s["hg_texp"], 1)
            v.tensor_tensor(QL[:, 0, :], HQ[:, :], W[:, 0, :], ALU.mult)
            v.tensor_tensor(KL[:, 0, :], HK[:, 0, :], LF[:, 0, :], ALU.mult).then_inc(s["hg_qk"], 1)
            v.tensor_tensor(QL[:, 1, :], HQ[:, :], LF[:, 1, :], ALU.mult)
            v.tensor_tensor(KL[:, 1, :], HK[:, 1, :], W[:, 1, :], ALU.mult).then_inc(s["hg_qk"], 1)
            for d in range(2):
                o = take(dve, ("kt", d))
                give(v.tensor_copy(KTOK[:, d].rearrange("p i t n -> p (i t n)"), o[:, :]), ("kt", d))
            dve.wait_ge(s["states0"], 16 * 4)

            def diagonals(o, dst):
                for half in range(2):
                    r = slice(half * 64, half * 64 + 64)
                    yield r, o[r, :, half * 64:half * 64 + 64], dst[r]

            for d in range(2):
                o = take(dve, ("hU", d))
                oo = o[:, :].rearrange("p (i t n) -> p i t n", i=2, t=2)
                for r, src, dst in diagonals(oo[:, 0], STO[:, d]):
                    v.tensor_copy(dst, src)
                b = 1 if d == 0 else 2
                for t in range(2):
                    for half in range(2):
                        r, c = slice(half * 64, half * 64 + 64), slice(half * 64, half * 64 + 64)
                        last = v.scalar_tensor_tensor(HGS[r, 1, d, t, c], HGS[r, 0, d, t, c],
                                                      HTOT[r, d, 3 * t + b:3 * t + b + 1], oo[r, 1, t, c],
                                                      ALU.mult, ALU.add)
                give(last, ("hU", d))

            def head_norm(name, x, x2, gate, g_src, gain):
                n = x.shape[1] * 4
                for j in range(NT):
                    taken(dve, (name, j))
                link(v.tensor_tensor(x2, x, x, ALU.mult))
                link(v.tensor_reduce(stat[:, 0, 0:n], x2.rearrange("p j (h c) -> p (j h) c", c=64), AX.X, ALU.add))
                v.tensor_scalar(stat[:, 2, 0:n], stat[:, 0, 0:n], 1.0 / 64, EPS, ALU.mult, ALU.add
                                ).then_inc(s[name + "_var"], 1)
                dve.wait_ge(s[name + "_gexp"], 1)
                link(v.tensor_scalar(gate, gate, 1.0, None, ALU.add))
                link(v.reciprocal(gate, gate))
                link(v.tensor_tensor(gate, gate, g_src, ALU.mult))
                if gain is not None:
                    link(v.tensor_tensor(gate, gate, gain, ALU.mult))
                dve.wait_ge(s[name + "_rstd"], 1)
                xv = x.rearrange("p j (h c) -> p (j h) c", c=64)
                link(v.tensor_tensor(xv, xv, stat[:, 3, 0:n].unsqueeze(2).to_broadcast([P, n, 64]), ALU.mult))
                v.tensor_tensor(x, x, gate, ALU.mult).then_inc(s[name + "_ready"], 1)

            dve.wait_ge(s["late_in"], 48)
            head_norm("ho", HO, HO2, HGATE, TMH[:, :, HYC:2 * HYC], hgn[:, :].unsqueeze(1).to_broadcast([P, NT, HYC]))

            gx = RGG[:, :, :].rearrange("p t n -> p (t n)")
            link(v.tensor_tensor(HQ[:, :], gx, gx, ALU.mult))
            link(v.tensor_scalar(HQ[:, :], HQ[:, :], 0.044715, 1.0, ALU.mult, ALU.add))
            v.tensor_tensor(HQ[:, :], HQ[:, :], gx, ALU.mult).then_inc(s["gelu_arg"], 1)
            for d in range(2):
                for k in range(2):
                    for t in range(2):
                        taken(dve, ("rg", d, k, t))
            for d in range(2):
                v.scalar_tensor_tensor(RI[:, d, 1], RI[:, d, 1], 1.0, XC[:, :, SEG_C:SEG_C + RUN], ALU.add, ALU.mult)
            dve.wait_ge(s["rg_a"], 1)
            for d in range(2):
                last = v.tensor_tensor(RI[:, d, 0], RA[:, d], RA[:, d], ALU.mult)
            link(last)
            for d in range(2):
                last = v.scalar_tensor_tensor(RB[:, d], RI[:, d, 0], 1.0, RB[:, d], ALU.add, ALU.mult)
            last.then_inc(s["rg_b2"], 1)
            dve.wait_ge(s["gelu_t"], 1)
            link(v.scalar_tensor_tensor(gx, HQ[:, :], 1.0, gx, ALU.add, ALU.mult))
            dve.wait_ge(s["rg_b"], 1)
            for d in range(2):
                last = v.scalar_tensor_tensor(RB[:, d], RI[:, d, 1], 0.5, RB[:, d], ALU.mult, ALU.mult)
            link(last)
            for t in range(2):
                for d in range(2):
                    out = RI[:, d, 0, t, :]
                    st = col("rst", 2 * d + t)
                    fw = slice(None, None, 1 if d == 0 else -1)
                    v.tensor_tensor_scan(out[:, 0:CTX][:, fw], RA[:, d, t, 0:CTX][:, fw], RB[:, d, t, 0:CTX][:, fw],
                                         0.0, ALU.mult, ALU.add)
                    last = v.tensor_tensor_scan(out[:, LATO:RUN][:, fw], RA[:, d, t, LATO:RUN][:, fw],
                                                RB[:, d, t, LATO:RUN][:, fw], st, ALU.mult, ALU.add)
            link(last)
            v.tensor_copy(RGO[:, 0:2], RI[:, 0, 0, :, CTX - 1])
            link(v.tensor_copy(RGO[:, 2:4], RI[:, 1, 0, :, 0]))
            link(v.tensor_tensor(RI[:, 0, 0], RI[:, 0, 0], RI[:, 1, 0], ALU.add))
            take(dve, ("in", 6, NT - 1))
            for a0, a1, b0 in ((0, CTX, 0), (CTX, TOK, LATO)):
                last = v.scalar_tensor_tensor(hT[:, 2:4, a0:a1], RI[:, 0, 0, :, b0:b0 + a1 - a0], 0.5,
                                              RGG[:, :, a0:a1], ALU.mult, ALU.mult)
            last.then_inc(s["rgo"], 1)

            for n in range(2):
                for u in range(3):
                    o = take(dve, ("V", n, u))
                    m1, m2 = M1[:, u % 2], M2[:, u % 2]
                    if n == 1 and u == 0:
                        dve.wait_ge(filled[uses[("y", 0, 1)] % 8], uses[("y", 0, 1)] // 8 + 1)
                    re, im = HF[:, u, 0, n, :], HF[:, u, 1, n, :]
                    v.tensor_tensor(m1.rearrange("p (r c) -> p r c", r=2), o[:, :].rearrange("p (r c) -> p r c", r=2),
                                    re.unsqueeze(1).to_broadcast([P, 2, HYC]), ALU.mult)
                    last = v.tensor_tensor(m2.rearrange("p (r c) -> p r c", r=2),
                                           o[:, :].rearrange("p (r c) -> p r c", r=2),
                                           im.unsqueeze(1).to_broadcast([P, 2, HYC]), ALU.mult)
                    link(last)
                    if u < 2:
                        ny = HNY[0:1, u, n, :]
                        link(v.tensor_tensor(m1[0:1, HYC:], o[0:1, HYC:], ny, ALU.mult))
                    v.tensor_tensor(Y[:, u, 0, :], m1[:, 0:HYC], m2[:, HYC:], ALU.subtract)
                    give(v.tensor_tensor(Y[:, u, 1, :], m1[:, HYC:], m2[:, 0:HYC], ALU.add), ("V", n, u))
                if n == 1:
                    modcol_out(6)
                for t in range(2):
                    o = take(dve, ("y", n, t))
                    for a0, a1, b0 in ((0, CTX, SEG_C), (CTX, TOK, SEG_L)):
                        z0 = U[:, t, b0:b0 + a1 - a0] if n == 0 else ZT[:, t, a0:a1]
                        last = v.scalar_tensor_tensor(M1.rearrange("p i n -> p (i n)")[:, t * TOK + a0:t * TOK + a1], z0,
                                                      col("hyd", 2 * n + t), o[:, a0:a1], ALU.mult, ALU.add)
                    give(last, ("y", n, t))
                    taken(dve, ("y", n, t))
                dst = ZT if n == 0 else hT[:, 0:2, :]
                for a0, a1, b0 in ((0, CTX, SEG_C), (CTX, TOK, SEG_L)):
                    last = v.tensor_tensor(dst[:, :, a0:a1], M1.rearrange("p i n -> p (i n)")[:, 0:2 * TOK].rearrange(
                        "p (t n) -> p t n", t=2)[:, :, a0:a1], U[:, 2 + 2 * n:4 + 2 * n, b0:b0 + a1 - a0], ALU.mult)
                last.then_inc(s["z1" if n == 0 else "hy_done"], 1)

            dve.wait_ge(s["hy_done"], 1)
            for i in range(4):
                o = take(dve, ("rope", i))
                give(v.tensor_tensor(PX[:, i, :], o[:, 0:LAT], C("sin"), ALU.mult), ("rope", i))
            for i in range(4):
                taken(dve, ("rope", i))
            lat = PR[:, :, CTX:TOK]
            link(v.tensor_tensor(lat, lat, C("cos").unsqueeze(1).to_broadcast([P, 4, LAT]), ALU.mult))
            v.tensor_tensor(lat, lat, PX, ALU.add).then_inc(s["rope"], 1)
            dve.wait_ge(s["rope"], 1)
            dve.wait_ge(s["ei"], 1)
            for d in range(2):
                last = v.tensor_tensor(TAIL[:, d], TAIL[:, d], PR[:, 2:4, 0:CTX], ALU.mult)
            last.then_inc(s["rtail"], 1)
            for d in range(2):
                last = v.tensor_tensor(QD[:, d], EI[:, d], PR[:, 0:2, CTX:TOK], ALU.mult)
            last.then_inc(s["qd"], 1)
            dve.wait_ge(s["dec"], 1)
            last = v.tensor_tensor(DEC[:, :, 0, :], DEC[:, :, 0, :], C("mask_f").unsqueeze(1).to_broadcast([P, 4, P]),
                                   ALU.mult)
            link(v.tensor_tensor(DTMP, DTMP, C("mask_b").unsqueeze(1).to_broadcast([P, 4, P]), ALU.mult))
            link(v.tensor_tensor(DEC[:, :, 0, :], DEC[:, :, 0, :], DTMP, ALU.add))
            link(v.tensor_copy(DEC[:, :, 3, :], DEC[:, :, 0, :]))
            modcol_out(7)
            for par in range(2):
                o = take(dve, ("rsc", par))
                give(v.tensor_tensor(WC[:, par], o[:, 0:2 * P].rearrange("p (h q) -> p h q", h=2),
                                     DEC[:, par:4:2, 0, :], ALU.mult), ("rsc", par))
            for h in range(4):
                o = take(dve, ("rsl", h))
                give(v.tensor_tensor(WL[:, h, :], o[:, :], DEC[:, h].rearrange("p k q -> p (k q)"), ALU.mult),
                     ("rsl", h))
            modcol_out(8)
            o = take(dve, "rU")
            oo = o[:, :].rearrange("p (d t n) -> p d t n", d=2, t=2)
            for d in range(2):
                for r, src, dst in diagonals(oo[:, d], STO[:, 2 + d]):
                    last = v.tensor_copy(dst, src)
            give(last, "rU")
            head_norm("ro", RO, RO2, RGATE, TMR[:, :, HYC:2 * HYC], None)

            modcol_out(9)

            dve.wait_ge(s["res_in"], 32)
            dve.wait_ge(s["state_out"], 48)
            for j in range(NT):
                for n in range(2):
                    o = take(dve, ("out", n, j))
                    c = slice(n * CW, n * CW + CW)
                    g1 = G1[:, min(j, 1), c]
                    give(v.tensor_tensor(h2tok[j][:, c], o[:, :], g1, ALU.mult), ("out", n, j))
                    taken(dve, ("out", n, j))
                    last = v.tensor_tensor(XR[:, j, c], XR[:, j, c], h2tok[j][:, c], ALU.add)
                last.then_inc(s["x1"], 1)

            def norm(name, outs, gain):
                dve.wait_ge(s[name + "_sq"], 1)
                v.tensor_scalar(stat[:, 0, 0:NT], stat[:, 2, 0:NT], 1.0 / D, EPS, ALU.mult, ALU.add
                                ).then_inc(s[name + "_var"], 1)
                dve.wait_ge(s[name + "_rstd"], 1)
                for j in range(NT):
                    if gain is None:
                        last = v.tensor_scalar(outs[j], XR[:, j, :], stat[:, 1, j:j + 1], None, ALU.mult)
                    else:
                        last = v.scalar_tensor_tensor(outs[j], XR[:, j, :], stat[:, 1, j:j + 1], gain, ALU.mult, ALU.mult)
                    last.then_inc(s[name + "_ready"], 1)

            link(v.scalar_tensor_tensor(AB[:, 1], MC[:, 3], 1.0,
                                        VC[:, VROWS["norm2"]:VROWS["norm2"] + KT].unsqueeze(2).to_broadcast([P, KT, 2]),
                                        ALU.add, ALU.mult))
            norm("n2", [h2tok[j][:, :] for j in range(NT)], None)
            modulate("x2T", 1, range(0, KT, 2))

            R = [RT[:, i] for i in range(12)]
            o = take(dve, "logits")
            mx = stat[:, 0, 0:NT]
            lg = o[:, 0:NT * E].rearrange("p (j e) -> p j e", j=NT)

            def over(a, n):
                return a.unsqueeze(2).to_broadcast([P, a.shape[1], n])
            link(v.tensor_reduce(mx, lg, AX.X, ALU.max))
            give(v.tensor_tensor(R[0], lg, over(mx, E), ALU.subtract), "logits")
            dve.wait_ge(s["logits_exp"], 1)
            link(v.tensor_reduce(mx, R[0], AX.X, ALU.add))
            link(v.reciprocal(mx, mx))
            link(v.tensor_tensor(R[0], R[0], over(mx, E), ALU.mult))
            link(v.tensor_tensor(R[1], R[0], rbias[:, :].unsqueeze(1).to_broadcast([P, NT, E]), ALU.add))
            sg = R[1].rearrange("p j (g i) -> p (j g) i", g=NG)
            for a0, b0, c0, w_ in ((0, 1, 0, 3), (0, 2, 3, 2), (0, 3, 5, 1)):
                last = v.tensor_tensor(PS[:, :, c0:c0 + w_], sg[:, :, a0:a0 + w_], sg[:, :, b0:b0 + w_], ALU.add)
            link(last)
            gs, gk, gm = GR[:, 0, :], GR[:, 1, :], stat[:, 1, 0:NT]
            link(v.tensor_reduce(gs, PS[:, :, :], AX.X, ALU.max))
            g3 = gs.rearrange("p (j g) -> p j g", j=NT)
            k3 = gk.rearrange("p (j g) -> p j g", j=NT)

            def first_highest(out, key, x, m, order_row, n):
                link(v.tensor_reduce(m, x, AX.X, ALU.max))
                link(v.tensor_tensor(key, x, over(m, n), ALU.is_equal))
                link(v.tensor_tensor(key, key, order_row.unsqueeze(1).to_broadcast([P, NT, n]), ALU.mult))
                link(v.tensor_reduce(m, key, AX.X, ALU.max))
                link(v.tensor_tensor(out, key, over(m, n), ALU.is_equal))

            first_highest(GR[:, 2, :].rearrange("p (j g) -> p j g", j=NT), k3, g3, gm, C("w4"), NG)
            oh = GR[:, 2, :]
            link(v.tensor_scalar(gs, oh, 1e30, -1e30, ALU.mult, ALU.add))
            m16 = R[2].rearrange("p j (g i) -> p (j g) i", g=NG)
            link(v.tensor_tensor(m16, sg, over(oh, 4), ALU.mult))
            link(v.tensor_tensor(m16, m16, over(gs, 4), ALU.add))
            first_highest(R[3], R[5], R[2], gm, C("w16"), E)
            link(v.scalar_tensor_tensor(R[2], R[3], -3e30, R[2], ALU.mult, ALU.add))
            first_highest(R[4], R[5], R[2], gm, C("w16"), E)
            v.tensor_tensor(R[6], R[3], R[4], ALU.add).then_inc(s["route"], 1)
            v.tensor_tensor(R[8], R[0], R[3], ALU.mult)
            link(v.tensor_tensor(R[9], R[0], R[4], ALU.mult))
            v.tensor_reduce(gw[:, :, 0], R[8], AX.X, ALU.add)
            link(v.tensor_reduce(gw[:, :, 1], R[9], AX.X, ALU.add))
            link(v.tensor_reduce(gm, gw[:, :, :], AX.X, ALU.add))
            link(v.reciprocal(gm, gm))
            link(v.tensor_tensor(gw[:, :, :], gw[:, :, :], over(gm, 2), ALU.mult))
            o = take(dve, "places")
            link(v.tensor_copy(R[7], o[:, 0:NT * E].rearrange("p (j e) -> p j e", j=NT)))
            cnt, more, upto, base, shift = (OV[:, i, :] for i in range(5))
            give(v.tensor_copy(cnt, o[:, NT * E:NT * E + E]), "places")
            taken(dve, "places")
            link(v.scalar_tensor_tensor(R[10], R[7], 1.0, R[6], ALU.add, ALU.mult))
            link(v.tensor_scalar(R[10], R[10], -1.0, None, ALU.add))
            v.tensor_copy(tokid16[:, :], C("tokid"))
            dve.wait_ge(s["n2_sq"], 1)
            for j in range(NT):
                if j > 0:
                    dve.wait_ge(s["sel_used"], j)
                v.tensor_tensor(SEL[:, :, :], C("count")[:, 0:P].unsqueeze(1).to_broadcast([P, E, P]),
                                R[10][:, j, :].unsqueeze(2).to_broadcast([P, E, P]), ALU.is_equal).then_inc(s["sel"], 1)
            o = take(dve, "lst")
            give(v.tensor_copy(lst[:, 0:E], o[:, 0:E]), "lst")
            link(v.tensor_scalar(more, cnt, float(ROWS), None, ALU.is_gt))
            for m in range(2, (TOK - 1) // ROWS + 1):
                link(v.scalar_tensor_tensor(more, cnt, float(m * ROWS), more, ALU.is_gt, ALU.add))
            link(v.tensor_tensor_scan(upto, C("ones")[:, 0:E], more, 0.0, ALU.mult, ALU.add))
            link(v.tensor_tensor(base, upto, more, ALU.subtract))
            link(v.tensor_scalar(shift, base, float(ROWS), (E - 1.0) * ROWS, ALU.mult, ALU.add))
            link(v.tensor_tensor(shift, shift, C("erow"), ALU.subtract))
            link(v.tensor_scalar(R[8], R[7], float(ROWS), None, ALU.is_ge))
            link(v.tensor_tensor(R[8], R[8], shift.unsqueeze(1).to_broadcast([P, NT, E]), ALU.mult))
            link(v.tensor_tensor(R[8], R[8], R[7], ALU.add))
            link(v.tensor_tensor(R[8], R[8], C("erow").unsqueeze(1).to_broadcast([P, NT, E]), ALU.add))
            for k in range(2):
                link(v.tensor_tensor(R[9], R[8], R[3 + k], ALU.mult))
                link(v.tensor_reduce(GR[:, 0, k * NT:k * NT + NT], R[9], AX.X, ALU.add))
                link(v.tensor_copy(rows[:, :, k], GR[:, 0, k * NT:k * NT + NT]))
            for o in range(OVER):
                link(v.tensor_scalar(OV[:, 5, :], upto, float(o), None, ALU.is_gt))
                link(v.tensor_scalar(OV[:, 6, :], base, float(o), None, ALU.is_le))
                link(v.tensor_tensor(OV[:, 5, :], OV[:, 5, :], OV[:, 6, :], ALU.mult))
                link(v.tensor_tensor(OV[:, 5, :], OV[:, 5, :], C("count")[:, 0:E], ALU.mult))
                link(v.tensor_reduce(OV[:, 7, o:o + 1], OV[:, 5, :], AX.X, ALU.add))
            v.tensor_copy(further_passes[0:1, 1:1 + OVER], OV[0:1, 7, 0:OVER])
            v.tensor_copy(further_passes[0:1, 0:1], upto[0:1, E - 1:E]).then_inc(s["passes_known"], 1)

            def experts(it, first):
                for p in range(2):
                    n = 2 * it + p
                    dve.wait_ge(s["g_exp"], n + 1)
                    v.tensor_scalar(he[:, p, 0:PACK], he[:, p, 0:PACK], 1.0, None, ALU.add).then_inc(s["h1"], 1)
                    dve.wait_ge(s["h1"], n + 1)
                    v.reciprocal(he[:, p, 0:PACK], he[:, p, 0:PACK]).then_inc(s["h2"], 1)
                    dve.wait_ge(s["h2"], n + 1)
                    v.tensor_tensor(he[:, p, 0:PACK], he[:, p, 0:PACK], psum[:, 2, 0:PACK], ALU.mult).then_inc(s["h3"], 1)
                    dve.wait_ge(s["h3"], n + 1)
                    dve.wait_ge(s["up_done"], n + 1)
                    v.tensor_tensor(he[:, p, 0:PACK], he[:, p, 0:PACK], psum[:, 3, 0:PACK], ALU.mult).then_inc(s["h_ready"], 1)
                    dve.wait_ge(s["ht_filled"], n + 1)
                    if not (first and p == 0):
                        dve.wait_ge(s["down_done"], n)
                    v.tensor_copy(heT[:, :, :].rearrange("p q n -> p (q n)"), psum[:, 4, 0:PACK]).then_inc(s["ht_ready"], 1)
                    dve.wait_ge(s["down_done"], n + 1)
                    if not first:
                        dve.wait_ge(s[f"y_out{p}"], 32 * it)
                    v.tensor_copy(yp[p][:, 1, :], psum[:, 6, 0:PACK]).then_inc(s["yb"], 1)

            experts(0, True)
            with dve.Fori(1, E // 2) as it:
                experts(it, False)
            with dve.If(further(dve) > 0):
                link_further = steps(dve, "o_step")
                dve.wait_ge(s["up_done"], E)
                for o in range(OVER):
                    if o > 0:
                        dve.wait_ge(s["o_selm"], o)
                    for i in range(2 * NT):
                        link_further(v.tensor_scalar(OV[:, 7, i:i + 1], GR[:, 0, i:i + 1], -1.0 * (E + o) * ROWS, None, ALU.add))
                        last = v.tensor_scalar(SO[:, i, :], C("count")[:, 0:P], OV[:, 7, i:i + 1], None, ALU.is_equal)
                    last.then_inc(s["o_sel"], 1)
                    dve.wait_ge(s["o_selm"], o + 1)
                    v.tensor_copy(lsto[:, o:o + 1], psum[:, 7, 0:1]).then_inc(s["o_lst"], 1)
                dve.wait_ge(s["y_out0"], 32 * E // 2)
                with dve.Fori(0, OVER) as o:
                    dve.wait_ge(s["o_exp"], o + 1)
                    v.tensor_scalar(he[:, 0, 0:PACK], he[:, 0, 0:PACK], 1.0, None, ALU.add).then_inc(s["o_h1"], 1)
                    dve.wait_ge(s["o_h1"], o + 1)
                    v.reciprocal(he[:, 0, 0:PACK], he[:, 0, 0:PACK]).then_inc(s["o_h2"], 1)
                    dve.wait_ge(s["o_h2"], o + 1)
                    v.tensor_tensor(he[:, 0, 0:PACK], he[:, 0, 0:PACK], psum[:, 2, 0:PACK], ALU.mult).then_inc(s["o_h3"], 1)
                    dve.wait_ge(s["o_h3"], o + 1)
                    v.tensor_tensor(he[:, 0, 0:PACK], he[:, 0, 0:PACK], psum[:, 3, 0:PACK], ALU.mult).then_inc(s["o_h"], 1)
                    dve.wait_ge(s["o_ht"], o + 1)
                    v.tensor_copy(heT[:, :, :].rearrange("p q n -> p (q n)"), psum[:, 4, 0:PACK]).then_inc(s["o_htr"], 1)
                    dve.wait_ge(s["o_down"], o + 1)
                    v.tensor_copy(yp[0], psum[:, 5:7, 0:PACK]).then_inc(s["o_y"], 1)
            for j in range(NT):
                dve.wait_ge(s["fin_w"], j + 1)
                link(v.scalar_tensor_tensor(YG[0][:, j, :], YG[1][:, j, :], gw[:, j, 1:2], YG[0][:, j, :],
                                            ALU.mult, ALU.add))
                link(v.tensor_tensor(YG[0][:, j, :], YG[0][:, j, :], G2[:, min(j, 1), :], ALU.mult))
                v.tensor_tensor(XR[:, j, :], XR[:, j, :], YG[0][:, j, :], ALU.add).then_inc(s["x2"], 1)
            dve.wait_ge(s["nf_in"], 16)
            norm("fin", [XR[:, j, :] for j in range(NT)], NF)


N_VEC = 17
N_FILT = 7
TURN_HI = 6.28125
TURN_LO = 2 * math.pi - 6.28125
PI_DOWN = 3.1415925


def kernel(**inputs):
    import concourse.bacc as bacc
    from concourse.bass_utils import run_bass_kernel_spmd as run

    nc = bacc.Bacc("TRN2", target_bir_lowering=False, num_devices=1)
    big, cols, z, win, masks = shape_constants()
    arrays, A, O = {}, {}, {}
    skip = ("hg_lb",)
    for name, a in list(inputs.items()) + [("const", big), ("z_table", z), ("window", win), ("masks", masks)]:
        if name in skip:
            continue
        a = np.ascontiguousarray(a)
        arrays[f"in_{name}"] = a
        A[name] = nc.dram_tensor(f"in_{name}", a.shape, mybir.dt.from_np(a.dtype), kind="ExternalInput").ap()
    outs = (("y_prompt", (1, CTX, D)), ("y_sample", (1, LAT, D)), ("new_state_rglru", (1, 1, 2, HYC)),
            ("new_state_hgrn", (1, 1, 2, 4, 64, 64)), ("new_state_ret", (1, 1, 2, 4, 64, 64)))
    for name, shape in outs:
        O[name] = nc.dram_tensor(f"out_{name}", shape, F32, kind="ExternalOutput").ap()
    A["h2_rows"] = nc.dram_tensor("h2_rows", (TOK, D), F32, kind="Internal").ap()
    A["y_rows"] = nc.dram_tensor("y_rows", ((E + OVER) * ROWS, D), F32, kind="Internal").ap()
    backbone_step(nc, cols, A, O)
    r = run(nc, [arrays], core_ids=[0])
    return tuple(r.results[0][f"out_{name}"] for name, _ in outs)
```
